# Optimizing a Trainium2 kernel written in Bass

```python
import math
import jax
import jax.numpy as jnp
from jax import lax
import numpy as np

D_MODEL = 1024
BATCH = 1
SEQ = 1024
DEPTH = 1

N_MEM = 256
EPS = 1e-6
NEG_INF = -1e30
Q_BLOCK = 128

MLA_HEADS = 8
MLA_NOPE = 64
MLA_ROPE = 32
MLA_V = 64
MLA_Q_RANK = 256
MLA_KV_RANK = 128
ROPE_THETA = 10000.0

NSA_HEADS = 8
NSA_KV_GROUPS = 2
NSA_HD = 64
CMP_LEN = 32
CMP_STRIDE = 16
CMP_HIDDEN = 128
SLC_LEN = 64
SLC_TOPK = 16
WIN = 512
FORCE_SCORE = 1e9

REL_BUCKETS = 32
REL_MAX_EXACT = 16
REL_MAX_DIST = 512

MEM_HEADS = 4
MEM_HD = 64

N_EXPERTS = 32
TOP_K = 4
D_FF = 1024
SWIGLU_LIMIT = 7.0
SWIGLU_ALPHA = 1.702
MOE_BLOCK = 128

D_MIX = MLA_HEADS * MLA_V + NSA_HEADS * NSA_HD
IN_SPLIT_SIZES = (MLA_Q_RANK, MLA_KV_RANK, MLA_ROPE, NSA_HEADS * NSA_HD) + (NSA_KV_GROUPS * NSA_HD,) * 6 + (3 * NSA_HEADS,)
IN_COLS = sum(IN_SPLIT_SIZES)

kernel_name = "hymba_mla_nsa_t5bias_memxattn_gptoss_moe"

def rms_norm(x, g):
    xf = x.astype(jnp.float32)
    y = xf * lax.rsqrt(jnp.mean(xf * xf, axis=-1, keepdims=True) + EPS)
    return (y * g.astype(jnp.float32)).astype(x.dtype)

def masked_softmax(logits, mask):
    logits = jnp.where(mask, logits.astype(jnp.float32), NEG_INF)
    m = jnp.max(logits, axis=-1, keepdims=True)
    e = jnp.exp(logits - m) * mask
    return e / jnp.maximum(jnp.sum(e, axis=-1, keepdims=True), 1e-30)

def rope(x, pos):
    half = x.shape[-1] // 2
    inv = ROPE_THETA ** (-jnp.arange(half, dtype=jnp.float32) / half)
    ang = pos.astype(jnp.float32)[:, None] * inv
    cos, sin = jnp.cos(ang)[:, None, :], jnp.sin(ang)[:, None, :]
    x1 = x[..., :half].astype(jnp.float32)
    x2 = x[..., half:].astype(jnp.float32)
    return jnp.concatenate([x1 * cos - x2 * sin, x2 * cos + x1 * sin], axis=-1).astype(x.dtype)

def rel_bucket(dist):
    n = jnp.maximum(dist, 0)
    nf = jnp.maximum(n, 1).astype(jnp.float32)
    large = REL_MAX_EXACT + (jnp.log(nf / REL_MAX_EXACT) / math.log(REL_MAX_DIST / REL_MAX_EXACT)
                             * (REL_BUCKETS - REL_MAX_EXACT)).astype(jnp.int32)
    large = jnp.minimum(large, REL_BUCKETS - 1)
    return jnp.where(n < REL_MAX_EXACT, n, large)

def causal_block_attention(q, k, v, scale):
    B, S, H, _ = q.shape
    nb = S // Q_BLOCK
    qb = q.reshape(B, nb, Q_BLOCK, H, q.shape[-1]).swapaxes(0, 1)
    kpos = jnp.arange(S)

    def one_block(args):
        qi, i = args
        qpos = i * Q_BLOCK + jnp.arange(Q_BLOCK)
        s = jnp.einsum('bqhd,bkhd->bhqk', qi, k).astype(jnp.float32) * scale
        p = masked_softmax(s, kpos[None, :] <= qpos[:, None])
        return jnp.einsum('bhqk,bkhd->bqhd', p.astype(v.dtype), v)

    out = lax.map(one_block, (qb, jnp.arange(nb)))
    return out.swapaxes(0, 1).reshape(B, S, H, v.shape[-1])

def mla_mixer(cq, ckv, krope, g_cq, w_uq, g_ckv, w_ukv, g_q, g_k):
    B, S, _ = cq.shape
    H = MLA_HEADS
    q = (rms_norm(cq, g_cq) @ w_uq).reshape(B, S, H, MLA_NOPE + MLA_ROPE)
    kv = (rms_norm(ckv, g_ckv) @ w_ukv).reshape(B, S, H, MLA_NOPE + MLA_V)
    k_nope, v = kv[..., :MLA_NOPE], kv[..., MLA_NOPE:]
    k = jnp.concatenate([k_nope, jnp.broadcast_to(krope[:, :, None, :], (B, S, H, MLA_ROPE))], axis=-1)
    q = rms_norm(q, g_q)
    k = rms_norm(k, g_k)
    pos = jnp.arange(S)
    q = jnp.concatenate([q[..., :MLA_NOPE], rope(q[..., MLA_NOPE:], pos)], axis=-1)
    k = jnp.concatenate([k[..., :MLA_NOPE], rope(k[..., MLA_NOPE:], pos)], axis=-1)
    o = causal_block_attention(q, k, v, (MLA_NOPE + MLA_ROPE) ** -0.5)
    return o.reshape(B, S, H * MLA_V)

def compress_blocks(t, cmp_idx, pos_emb, w1, w2):
    blk = t[:, cmp_idx] + pos_emb[None, None, :, None, :]
    hid = jax.nn.gelu(jnp.einsum('bnlgd,ldf->bngf', blk, w1))
    return jnp.einsum('bngf,fd->bngd', hid, w2)

def nsa_mixer(q, kc, vc, ks, vs, kw, vw, gate_logits, cmp_k_pos, cmp_k_w1, cmp_k_w2,
              cmp_v_pos, cmp_v_w1, cmp_v_w2, g_q, g_k, rel_table):
    B, S = q.shape[:2]
    G, HPG, D = NSA_KV_GROUPS, NSA_HEADS // NSA_KV_GROUPS, NSA_HD
    n_cmp = (S - CMP_LEN) // CMP_STRIDE + 1
    n_slc = S // SLC_LEN
    n_sel = min(SLC_TOPK, n_slc)
    nb = S // Q_BLOCK
    scale = D ** -0.5

    q = rms_norm(q.reshape(B, S, G, HPG, D), g_q)
    kc, vc, ks, vs, kw, vw = (t.reshape(B, S, G, D) for t in (kc, vc, ks, vs, kw, vw))

    cmp_idx = jnp.arange(n_cmp)[:, None] * CMP_STRIDE + jnp.arange(CMP_LEN)[None, :]
    k_cmp = rms_norm(compress_blocks(kc, cmp_idx, cmp_k_pos, cmp_k_w1, cmp_k_w2), g_k)
    v_cmp = compress_blocks(vc, cmp_idx, cmp_v_pos, cmp_v_w1, cmp_v_w2)
    cmp_start, cmp_end = cmp_idx[:, 0], cmp_idx[:, -1]
    slc_start = jnp.arange(n_slc) * SLC_LEN
    overlap = ((cmp_start[:, None] < slc_start[None, :] + SLC_LEN)
               & (cmp_end[:, None] >= slc_start[None, :])).astype(jnp.float32)

    k_blk = rms_norm(ks, g_k).transpose(0, 2, 1, 3).reshape(B, G, n_slc, SLC_LEN, D)
    v_blk = vs.transpose(0, 2, 1, 3).reshape(B, G, n_slc, SLC_LEN, D)

    pad = ((0, 0), (WIN, 0), (0, 0), (0, 0))
    k_pad = jnp.pad(rms_norm(kw, g_k), pad)
    v_pad = jnp.pad(vw, pad)

    tbl_gh = rel_table.reshape(REL_BUCKETS, G, HPG)
    tbl_g = tbl_gh.transpose(1, 0, 2)
    b_idx = jnp.arange(B)[:, None, None, None]
    g_idx = jnp.arange(G)[None, :, None, None]

    def bias_gh(dist):
        return jnp.moveaxis(tbl_gh[rel_bucket(dist)], (-2, -1), (0, 1)).astype(jnp.float32)

    qb = q.reshape(B, nb, Q_BLOCK, G, HPG, D).swapaxes(0, 1)
    gb = jax.nn.sigmoid(gate_logits.astype(jnp.float32)).reshape(B, nb, Q_BLOCK, G, HPG, 3).swapaxes(0, 1)

    def one_block(args):
        qi, gi, i = args
        q0 = i * Q_BLOCK
        qpos = q0 + jnp.arange(Q_BLOCK)

        s = jnp.einsum('bqghd,bngd->bghqn', qi, k_cmp).astype(jnp.float32) * scale
        s = s + bias_gh(qpos[:, None] - cmp_end[None, :])
        p_cmp = masked_softmax(s, cmp_end[None, :] <= qpos[:, None])
        o_cmp = jnp.einsum('bghqn,bngd->bqghd', p_cmp.astype(v_cmp.dtype), v_cmp)

        imp = jnp.einsum('bghqn,nj->bgqj', p_cmp, overlap)
        j = jnp.arange(n_slc)[None, :]
        cur = (qpos // SLC_LEN)[:, None]
        forced = (j == 0) | (j == cur) | (j == cur - 1)
        imp = jnp.where(forced, FORCE_SCORE, imp)
        imp = jnp.where(slc_start[None, :] <= qpos[:, None], imp, NEG_INF)
        _, sel = lax.top_k(imp, n_sel)
        k_sel = k_blk[b_idx, g_idx, sel].reshape(B, G, Q_BLOCK, n_sel * SLC_LEN, D)
        v_sel = v_blk[b_idx, g_idx, sel].reshape(B, G, Q_BLOCK, n_sel * SLC_LEN, D)
        tok = (sel[..., None] * SLC_LEN + jnp.arange(SLC_LEN)).reshape(B, G, Q_BLOCK, n_sel * SLC_LEN)
        bucket = rel_bucket(qpos[None, None, :, None] - tok)
        bias_sel = jnp.moveaxis(tbl_g[g_idx, bucket], -1, 2).astype(jnp.float32)
        s = jnp.einsum('bqghd,bgqnd->bghqn', qi, k_sel).astype(jnp.float32) * scale + bias_sel
        p = masked_softmax(s, (tok <= qpos[None, None, :, None])[:, :, None])
        o_slc = jnp.einsum('bghqn,bgqnd->bqghd', p.astype(v_sel.dtype), v_sel)

        kwin = lax.dynamic_slice_in_dim(k_pad, q0, WIN + Q_BLOCK, axis=1)
        vwin = lax.dynamic_slice_in_dim(v_pad, q0, WIN + Q_BLOCK, axis=1)
        kpos = q0 - WIN + jnp.arange(WIN + Q_BLOCK)
        dist = qpos[:, None] - kpos[None, :]
        s = jnp.einsum('bqghd,bkgd->bghqk', qi, kwin).astype(jnp.float32) * scale + bias_gh(dist)
        p = masked_softmax(s, (dist >= 0) & (dist < WIN) & (kpos[None, :] >= 0))
        o_win = jnp.einsum('bghqk,bkgd->bqghd', p.astype(vwin.dtype), vwin)

        out = gi[..., 0:1] * o_cmp + gi[..., 1:2] * o_slc + gi[..., 2:3] * o_win
        return out.astype(q.dtype).reshape(B, Q_BLOCK, G * HPG * D)

    out = lax.map(one_block, (qb, gb, jnp.arange(nb)))
    return out.swapaxes(0, 1).reshape(B, S, NSA_HEADS * D)

def memory_cross_attention(h, mem_n, w_mq, w_mkv, g_mq, g_mk, w_mo):
    B, S, _ = h.shape
    M = mem_n.shape[1]
    q = rms_norm((h @ w_mq).reshape(B, S, MEM_HEADS, MEM_HD), g_mq)
    kv = (mem_n @ w_mkv).reshape(B, M, 2, MEM_HEADS, MEM_HD)
    k = rms_norm(kv[:, :, 0], g_mk)
    v = kv[:, :, 1]
    s = jnp.einsum('bqhd,bkhd->bhqk', q, k).astype(jnp.float32) * MEM_HD ** -0.5
    p = jax.nn.softmax(s, axis=-1)
    o = jnp.einsum('bhqk,bkhd->bqhd', p.astype(v.dtype), v).reshape(B, S, MEM_HEADS * MEM_HD)
    return o @ w_mo

def moe_ffn(h, router_w, router_b, w_gate_up, b_gate_up, w_down, b_down):
    B, S, D = h.shape
    N = B * S
    NK = N * TOP_K
    t = h.reshape(N, D)
    logits = (t @ router_w + router_b).astype(jnp.float32)
    top_logit, top_idx = lax.top_k(logits, TOP_K)
    gates = jax.nn.softmax(top_logit, axis=-1)
    flat_e = top_idx.reshape(NK)
    flat_tok = jnp.arange(NK, dtype=jnp.int32) // TOP_K
    order = jnp.argsort(flat_e)
    se, stok, sgate = flat_e[order], flat_tok[order], gates.reshape(NK)[order]
    counts = jnp.bincount(flat_e, length=N_EXPERTS)
    start = jnp.cumsum(counts) - counts
    padded = (counts + MOE_BLOCK - 1) // MOE_BLOCK * MOE_BLOCK
    pad_end = jnp.cumsum(padded)
    pad_start = pad_end - padded
    dest = pad_start[se] + jnp.arange(NK) - start[se]
    P = ((NK + MOE_BLOCK - 1) // MOE_BLOCK + N_EXPERTS) * MOE_BLOCK
    buf_tok = jnp.zeros((P,), jnp.int32).at[dest].set(stok)
    buf_gate = jnp.zeros((P,), jnp.float32).at[dest].set(sgate)
    n_blk = P // MOE_BLOCK
    blk_e = jnp.minimum(jnp.searchsorted(pad_end, jnp.arange(n_blk) * MOE_BLOCK, side='right'), N_EXPERTS - 1)

    def expert_block(args):
        tok, e = args
        gu = t[tok] @ w_gate_up[e] + b_gate_up[e]
        gate = jnp.minimum(gu[:, 0::2], SWIGLU_LIMIT)
        up = jnp.clip(gu[:, 1::2], -SWIGLU_LIMIT, SWIGLU_LIMIT)
        act = (up + 1.0) * gate * jax.nn.sigmoid(SWIGLU_ALPHA * gate)
        return act @ w_down[e] + b_down[e]

    ys = lax.map(expert_block, (buf_tok.reshape(n_blk, MOE_BLOCK), blk_e)).reshape(P, D)
    out = jax.ops.segment_sum(ys * buf_gate[:, None].astype(ys.dtype), buf_tok, num_segments=N)
    return out.reshape(B, S, D)

def setup_inputs(seed: int = 0) -> dict:
    key = jax.random.key(seed)
    keys = iter(jax.random.split(key, 64))

    def nrm(shape, scale):
        return jax.random.normal(next(keys), shape, jnp.float32) * scale

    def gain(*shape):
        return 1.0 + nrm(shape, 0.05)

    L = DEPTH
    return {
        "x": nrm((BATCH, SEQ, D_MODEL), 1.0),
        "mem": nrm((BATCH, N_MEM, D_MODEL), 1.0),
        "g_attn_norm": gain(L, D_MODEL),
        "w_in": nrm((L, D_MODEL, IN_COLS), D_MODEL ** -0.5),
        "g_cq": gain(L, MLA_Q_RANK),
        "w_uq": nrm((L, MLA_Q_RANK, MLA_HEADS * (MLA_NOPE + MLA_ROPE)), MLA_Q_RANK ** -0.5),
        "g_ckv": gain(L, MLA_KV_RANK),
        "w_ukv": nrm((L, MLA_KV_RANK, MLA_HEADS * (MLA_NOPE + MLA_V)), MLA_KV_RANK ** -0.5),
        "g_q_mla": gain(L, MLA_NOPE + MLA_ROPE),
        "g_k_mla": gain(L, MLA_NOPE + MLA_ROPE),
        "cmp_k_pos": nrm((L, CMP_LEN, NSA_HD), 0.1),
        "cmp_k_w1": nrm((L, CMP_LEN, NSA_HD, CMP_HIDDEN), (CMP_LEN * NSA_HD) ** -0.5),
        "cmp_k_w2": nrm((L, CMP_HIDDEN, NSA_HD), CMP_HIDDEN ** -0.5),
        "cmp_v_pos": nrm((L, CMP_LEN, NSA_HD), 0.1),
        "cmp_v_w1": nrm((L, CMP_LEN, NSA_HD, CMP_HIDDEN), (CMP_LEN * NSA_HD) ** -0.5),
        "cmp_v_w2": nrm((L, CMP_HIDDEN, NSA_HD), CMP_HIDDEN ** -0.5),
        "g_q_nsa": gain(L, NSA_HD),
        "g_k_nsa": gain(L, NSA_HD),
        "rel_table": nrm((REL_BUCKETS, NSA_HEADS), 0.5),
        "g_out_mla": gain(L, MLA_HEADS * MLA_V),
        "g_out_nsa": gain(L, NSA_HEADS * NSA_HD),
        "w_out": nrm((L, D_MIX, D_MODEL), D_MIX ** -0.5),
        "g_mem_norm": gain(L, D_MODEL),
        "g_mem_src": gain(L, D_MODEL),
        "w_mq": nrm((L, D_MODEL, MEM_HEADS * MEM_HD), D_MODEL ** -0.5),
        "w_mkv": nrm((L, D_MODEL, 2 * MEM_HEADS * MEM_HD), D_MODEL ** -0.5),
        "g_mq": gain(L, MEM_HD),
        "g_mk": gain(L, MEM_HD),
        "w_mo": nrm((L, MEM_HEADS * MEM_HD, D_MODEL), (MEM_HEADS * MEM_HD) ** -0.5),
        "g_moe_norm": gain(L, D_MODEL),
        "router_w": nrm((L, D_MODEL, N_EXPERTS), D_MODEL ** -0.5),
        "router_b": nrm((L, N_EXPERTS), 0.01),
        "w_gate_up": nrm((L, N_EXPERTS, D_MODEL, 2 * D_FF), D_MODEL ** -0.5),
        "b_gate_up": nrm((L, N_EXPERTS, 2 * D_FF), 0.01),
        "w_down": nrm((L, N_EXPERTS, D_FF, D_MODEL), D_FF ** -0.5),
        "b_down": nrm((L, N_EXPERTS, D_MODEL), 0.01),
    }

def reference(x, mem, g_attn_norm, w_in, g_cq, w_uq, g_ckv, w_ukv, g_q_mla, g_k_mla,
              cmp_k_pos, cmp_k_w1, cmp_k_w2, cmp_v_pos, cmp_v_w1, cmp_v_w2, g_q_nsa, g_k_nsa,
              rel_table, g_out_mla, g_out_nsa, w_out, g_mem_norm, g_mem_src, w_mq, w_mkv,
              g_mq, g_mk, w_mo, g_moe_norm, router_w, router_b, w_gate_up, b_gate_up,
              w_down, b_down):
    split_points = np.cumsum(IN_SPLIT_SIZES)[:-1].tolist()
    for l in range(DEPTH):
        h = rms_norm(x, g_attn_norm[l])
        parts = jnp.split(h @ w_in[l], split_points, axis=-1)
        cq, ckv, krope, q_nsa = parts[0], parts[1], parts[2], parts[3]
        kc, vc, ks, vs, kw, vw = parts[4], parts[5], parts[6], parts[7], parts[8], parts[9]
        gate_logits = parts[10]
        y_mla = mla_mixer(cq, ckv, krope, g_cq[l], w_uq[l], g_ckv[l], w_ukv[l], g_q_mla[l], g_k_mla[l])
        y_nsa = nsa_mixer(q_nsa, kc, vc, ks, vs, kw, vw, gate_logits, cmp_k_pos[l], cmp_k_w1[l],
                          cmp_k_w2[l], cmp_v_pos[l], cmp_v_w1[l], cmp_v_w2[l], g_q_nsa[l], g_k_nsa[l],
                          rel_table)
        mix = jnp.concatenate([rms_norm(y_mla, g_out_mla[l]), rms_norm(y_nsa, g_out_nsa[l])], axis=-1)
        x = x + mix @ w_out[l]
        x = x + memory_cross_attention(rms_norm(x, g_mem_norm[l]), rms_norm(mem, g_mem_src[l]),
                                       w_mq[l], w_mkv[l], g_mq[l], g_mk[l], w_mo[l])
        x = x + moe_ffn(rms_norm(x, g_moe_norm[l]), router_w[l], router_b[l], w_gate_up[l],
                        b_gate_up[l], w_down[l], b_down[l])
    return x


_drawn_inputs = setup_inputs


def setup_inputs(seed=0):
    import zlib

    import numpy as np

    out = dict(_drawn_inputs(seed))
    spreads = {}
    factors = {'g_mem_norm': 3.966,
     'g_mem_src': 2.917,
     'g_mq': 3.526,
     'g_mk': 4.005,
     'router_b': 9.352,
     'b_gate_up': 27.228,
     'b_down': 31.789}
    for name, (base, spread) in spreads.items():
        noise = np.random.default_rng([zlib.crc32(name.encode()), seed]).standard_normal(out[name].shape)
        drawn = base * np.exp(spread * noise) if base else spread * noise
        out[name] = jnp.asarray(drawn.astype(out[name].dtype))
    for name, factor in factors.items():
        out[name] = (out[name] * factor).astype(out[name].dtype)
    return out
```

```python
from contextlib import ExitStack

import numpy as np
import concourse.bass as bass
from concourse import mybir

F32 = mybir.dt.float32
U32 = mybir.dt.uint32
I32 = mybir.dt.int32
ALU = mybir.AluOpType
ACT = mybir.ActivationFunctionType
AX = mybir.AxisListType

P = 128
D = 1024
S = 1024
NT = S // P
KD = D // P
EPS = 1e-6
NEG = -1e30

HM, NOPE, ROPE, VD = 8, 64, 32, 64
QK = NOPE + ROPE
QR, KVR = 256, 128
HN, G, HD = 8, 2, 64
HPG = HN // G
CMP_LEN, CMP_STRIDE, CMP_HID = 32, 16, 128
NCMP = (S - CMP_LEN) // CMP_STRIDE + 1
WIN = 512
BUCKETS, MAX_EXACT, MAX_DIST = 32, 16, 512
N_MEM, MH, MHD = 256, 4, 64
NE, TOPK, FF = 32, 4, 1024
LIMIT, ALPHA = 7.0, 1.702
IN_COLS = 1720
PCH = 430
C_CQ, C_CKV, C_KR, C_Q = 0, 256, 384, 416
C_KC, C_VC, C_KS, C_VS, C_KW, C_VW, C_GT = 928, 1056, 1184, 1312, 1440, 1568, 1696
REV = S + P
PASS = 256
NPASS = NE + (S * TOPK - NE) // PASS
NOBODY = 1 << 20
CAP = S


CREDIT = 8


def give_credit(eng, sems):
    for s in sems:
        eng.sem_inc(s, CREDIT)


class Chain:

    def __init__(self, eng, sem, turn=0, per=0):
        self.eng, self.sem, self.base, self.per, self.n = eng, sem, turn * per, per, 0

    def __call__(self, ins):
        ins.then_inc(self.sem, 1)
        self.n += 1
        self.eng.wait_ge(self.sem, CREDIT + self.base + self.n)

    def end(self):
        assert self.n == self.per, (self.n, self.per)


def bcast(ap, shape):
    return ap.to_broadcast(shape)


def hold(eng, sem):
    eng.sem_inc(sem)


class Env:
    pass


def add_tools(nc, e, ctx):
    e.sb = lambda n, s, d=F32: ctx.enter_context(nc.sbuf_tensor(n, s, d))
    e.sems = []

    def sem(name):
        e.sems.append(ctx.enter_context(nc.semaphore(name)))
        return e.sems[-1]

    e.dma_sem = lambda name: ctx.enter_context(nc.semaphore(name))

    e.sem = sem
    e.ps = ctx.enter_context(nc.psum_tensor("ps" + str(nc.next_id()), [P, 8, 512], F32))
    return e.sb, e.sem, e.ps


def stage_setup(nc, e):
    with ExitStack() as ctx:
        sb, sem, ps = add_tools(nc, e, ctx)
        onehot = sb("onehot", [BUCKETS, REV])
        negrow = sb("negrow", [HN + 1, REV])
        negwin = sb("negwin", [HN + 1, REV])
        table = sb("table", [BUCKETS, HN + 1])
        rev = sb("rev", [HN + 1, 2, REV])
        flip = sb("flip", [P, P])
        skew = sb("skew", [P, 2, S])
        strip = sb("strip", [P, 2, S])
        bgu = sb("bgu", [NE, 2 * FF])
        ident = sb("ident_s", [P, P])
        s_in, s_tab, s_rows, s_rowsum = sem("u_in"), sem("u_table"), sem("u_rows"), sem("u_row_done")
        s_out, s_skew, s_flip, s_strip, s_stored = sem("u_rev_stored"), sem("u_skew"), sem("u_flip"), sem("u_strip"), sem("u_stored")
        with nc.Block() as block:
            @block.gpsimd
            def _(pool):
                give_credit(pool, e.sems)

            @block.sync
            def _(sp):
                sp.dma_start(onehot[:, :], e.c_onehot).then_inc(s_in, 16)
                sp.dma_start(negrow[:, :], e.c_negrow).then_inc(s_in, 16)
                sp.dma_start(negwin[:, :], e.c_negwin).then_inc(s_in, 16)
                sp.dma_start(flip[:, :], e.c_flip).then_inc(s_in, 16)
                sp.dma_start(ident[:, :], e.c_ident).then_inc(s_in, 16)
                sp.dma_start(bgu[:, :], e.b_gate_up[0]).then_inc(s_in, 16)
                sp.wait_ge(s_tab, CREDIT + 1)
                sp.dma_start(table[:, 0:HN], e.rel_table).then_inc(s_in, 16)
                sp.wait_ge(s_rowsum, CREDIT + 2)
                sp.dma_start(e.d_rev.rearrange("k h n -> h k n"), rev[:, :, :]).then_inc(s_out, 16)
                sp.wait_ge(s_out, CREDIT + 16)
                with sp.Fori(0, HN + 1) as h:
                    sp.wait_ge(s_flip, CREDIT + h)
                    for k in range(2):
                        sp.dma_start(skew[:, k, :], e.skew_view(k, h)).then_inc(s_skew, 16)
                    sp.wait_ge(s_strip, CREDIT + h + 1)
                    sp.dma_start(e.d_strip[bass.ds(h, 1)].rearrange("o p n -> (o p) n"), strip[:, 0, :]).then_inc(s_stored, 16)
                    sp.dma_start(e.d_wstrip[bass.ds(h, 1)].rearrange("o p n -> (o p) n"), strip[:, 1, 384:S]).then_inc(s_stored, 16)
                sp.wait_ge(s_stored, CREDIT + 32 * (HN + 1))

            @block.vector
            def _(dve):
                dve.memset(table[:, :], 0.0).then_inc(s_tab, 1)
                dve.wait_ge(s_in, CREDIT + 16 * 7)
                for k, neg in enumerate((negrow, negwin)):
                    dve.wait_ge(s_rows, CREDIT + k + 1)
                    dve.tensor_tensor(rev[:, k, :].rearrange("h (c n) -> h c n", c=3), ps[0:HN + 1, 0:3, 0:REV // 3],
                                      neg[:, :].rearrange("h (c n) -> h c n", c=3), ALU.add).then_inc(s_rowsum, 1)
                dve.wait_ge(s_rows, CREDIT + 3)
                dve.tensor_copy(e.bgT[:, :, :].rearrange("p (b j) n -> p b j n", b=4),
                                ps[:, 4:8, 0:4 * NE].rearrange("p b (j n) -> p b j n", n=NE)).then_inc(s_rowsum, 1)
                with dve.Fori(0, HN + 1) as h:
                    dve.wait_ge(s_flip, CREDIT + h + 1)
                    dve.wait_ge(s_stored, CREDIT + 32 * h)
                    dve.tensor_copy(strip[:, :, :].rearrange("p k (c n) -> p (k c) n", c=2), ps[:, 0:4, :]).then_inc(s_strip, 1)

            @block.tensor
            def _(pe):
                pe.wait_ge(s_in, CREDIT + 16 * 7)
                for k in range(2):
                    if k:
                        pe.wait_ge(s_rowsum, CREDIT + 1)
                    for c in range(3):
                        mm = pe.matmul(ps[0:HN + 1, c, 0:REV // 3], table[:, :], onehot[:, c * (REV // 3):(c + 1) * (REV // 3)],
                                       start=True, stop=True)
                    mm.then_inc(s_rows, 1)
                for half in range(2):
                    for j in range(8):
                        n = half * 8 + j
                        mm = pe.transpose(ps[:, 4 + n // 4, (n % 4) * NE:(n % 4 + 1) * NE],
                                          bgu[:, 2 * P * j + half:2 * P * (j + 1):2], ident[0:NE, 0:NE])
                mm.then_inc(s_rows, 1)
                pe.wait_ge(s_rowsum, CREDIT + 3)
                with pe.Fori(0, HN + 1) as h:
                    pe.wait_ge(s_strip, CREDIT + h)
                    pe.wait_ge(s_skew, CREDIT + 32 * (h + 1))
                    for k in range(2):
                        for c in range(2):
                            mm = pe.matmul(ps[:, 2 * k + c, :], flip[:, :], skew[:, k, c * 512:(c + 1) * 512], start=True, stop=True)
                    mm.then_inc(s_flip, 1)


def stage_project(nc, e):
    with ExitStack() as ctx:
        sb, sem, ps = add_tools(nc, e, ctx)
        w_in = sb("w_in", [P, KD, IN_COLS])
        w_uq = sb("w_uq", [P, 2, HM * QK])
        w_ukv = sb("w_ukv", [P, HM * (NOPE + VD)])
        ident = sb("ident_a", [P, P])
        g_x = sb("g_x", [P, KD])
        g_c = sb("g_c", [P, 3])
        g_qk = sb("g_qk", [P, 2 * HM, QK])
        g_qn = sb("g_qn", [P, HD])
        g_kn = sb("g_kn", [P, HD])
        inv_d = sb("inv_d", [P, 14])
        post = sb("post", [P, 14])
        post2 = sb("post2", [P, 16])
        eps = sb("eps_a", [P, 1])
        x = sb("x_a", [P, D])
        trig = sb("trig", [P, ROPE])
        sq = sb("sq_a", [P, IN_COLS])
        st = sb("st_a", [P, 4])
        xn = sb("xn_a", [P, D])
        hT = sb("hT_a", [P, KD, P])
        pr = sb("pr", [P, IN_COLS])
        st1 = sb("st1", [P, 14])
        cn = sb("cn", [P, 384])
        cT = sb("cT", [P, 3, P])
        qk = sb("qk", [P, 2 * HM, QK])
        sqk = sb("sqk", [P, 2 * HM, QK])
        st2 = sb("st2", [P, 16])
        ra = sb("ra", [P, 4, 2 * HM, 16])
        v_m = sb("v_m", [P, HM, VD])
        nq = sb("nq", [P, 768])
        gt = sb("gt", [P, 24])
        qkT = sb("qkT", [QK, 2 * HM, P])
        nT = sb("nT", [P, 8, P])
        s_w, s_x, s_ssq, s_std, s_xn, s_xT, s_hT = (sem("a_" + n) for n in ("weights", "x", "ssq", "std", "xn", "xT", "hT"))
        s_pr, s_prA, s_prD, s_st1, s_std1, s_cn, s_cT, s_cTd = (sem("a_" + n) for n in ("proj", "projA", "projD", "st1", "std1", "cn", "cT", "cTd"))
        s_up, s_upA, s_upD, s_st2, s_std2, s_nq, s_qk, s_gt = (sem("a_" + n) for n in ("up", "upA", "upD", "st2", "std2", "nq", "qk", "gates"))
        s_oT, s_oTA, s_oTD, s_st, s_dch, s_ach = (sem("a_" + n) for n in ("outT", "outTA", "outTD", "stored", "dve_chain", "act_chain"))
        s_qkg, s_ra, s_ro, s_eps = sem("a_qkg"), sem("a_ra"), sem("a_ro"), sem("a_eps")
        DVE_A = 17
        with nc.Block() as block:
            @block.gpsimd
            def _(pool):
                give_credit(pool, e.sems)

            @block.sync
            def _(sp):
                n = 0
                for dst, src in ((ident[:, :], e.c_ident), (w_in[:, :, :], e.w_in[0].rearrange("(k p) n -> p k n", p=P)),
                                 (w_uq[:, :, :], e.w_uq[0].rearrange("(k p) n -> p k n", p=P)), (w_ukv[:, :], e.w_ukv[0]),
                                 (inv_d[:, :], e.c_inv_d.partition_broadcast(P)), (post[:, :], e.c_post.partition_broadcast(P)),
                                 (post2[:, :], e.c_post2.partition_broadcast(P)),
                                 (g_qn[:, :], e.g_q_nsa[0].partition_broadcast(P)), (g_kn[:, :], e.g_k_nsa[0].partition_broadcast(P))):
                    sp.dma_start(dst, src).then_inc(s_w, 16)
                    n += 1
                for i in range(2 * HM):
                    sp.dma_start(g_qk[:, i, :], (e.g_q_mla if i < HM else e.g_k_mla)[0].partition_broadcast(P)).then_inc(s_w, 16)
                    n += 1
                with nc.allow_non_contiguous_dma("gain columns, once"):
                    for dst, src in ((g_x[:, :], e.g_attn_norm[0].rearrange("(k p) -> p k", p=P)),
                                     (g_c[:, 0:2], e.g_cq[0].rearrange("(k p) -> p k", p=P)),
                                     (g_c[:, 2:3], e.g_ckv[0].rearrange("(k p) -> p k", p=P))):
                        sp.dma_start(dst, src).then_inc(s_w, 16)
                        n += 1
                assert n == 28
                with sp.Fori(0, NT) as t:
                    rows = bass.ds(t * P, P)
                    sp.wait_ge(s_xn, CREDIT + t)
                    sp.wait_ge(s_qk, CREDIT + t)
                    sp.dma_start(x[:, :], e.x[0, rows, :]).then_inc(s_x, 16)
                    sp.dma_start(trig[:, :], e.c_trig[rows, :]).then_inc(s_x, 16)
                    sp.wait_ge(s_upD, CREDIT + t + 1)
                    sp.dma_start(e.d_vm[:, rows, :].rearrange("h p d -> p h d"), v_m[:, :, :]).then_inc(s_st, 16)
                    sp.wait_ge(s_gt, CREDIT + t + 1)
                    with nc.allow_non_contiguous_dma("12-byte gates"):
                        sp.dma_start(e.d_gt[:, rows, :].rearrange("h p d -> p h d"), gt[:, :].rearrange("p (h d) -> p h d", d=3)).then_inc(s_st, 16)
                    for i, c in enumerate((C_VS, C_VW)):
                        sp.dma_start(e.d_vn[i][:, rows, :].rearrange("g p d -> p g d"),
                                     pr[:, c:c + 128].rearrange("p (g d) -> p g d", d=HD)).then_inc(s_st, 16)
                    sp.wait_ge(s_oTA, CREDIT + t + 1)
                    sp.wait_ge(s_oTD, CREDIT + t + 1)
                    hold(sp, e.sp_passed)
                    sp.dma_start(e.d_qm[:, :, rows].rearrange("h d p -> d h p"), qkT[:, 0:HM, :]).then_inc(s_st, 16)
                    sp.dma_start(e.d_km[:, :, rows].rearrange("h d p -> d h p"), qkT[:, HM:, :]).then_inc(s_st, 16)
                    for par in range(2):
                        sp.dma_start(e.d_qn[par][:, :, rows].rearrange("j d p -> d j p"), nT[HD * par:HD * (par + 1), 0:4, :]).then_inc(s_st, 16)
                    sp.dma_start(e.d_kn[:, :, rows].rearrange("w d p -> d w p"), nT[:, 4:6, :]).then_inc(s_st, 16)
                    sp.dma_start(e.d_cn[:, :, rows].rearrange("w d p -> d w p"), nT[:, 6:8, :]).then_inc(s_st, 16)
                    sp.wait_ge(s_st, CREDIT + 160 * t + 160)
                    hold(sp, e.sp_passed)

            @block.scalar
            def _(act):
                act.wait_ge(s_w, CREDIT + 16 * 28)
                act.wait_ge(s_eps, CREDIT + 1)
                with act.Fori(0, NT) as t:
                    ch = Chain(act, s_ach, t, 1)
                    act.wait_ge(s_x, CREDIT + 32 * t + 32)
                    act.wait_ge(s_std1, CREDIT + t)
                    act.activation(xn[:, :], x[:, :], ACT.Square, accum_out=st[:, 0:1]).then_inc(s_ssq, 1)
                    act.wait_ge(s_ssq, CREDIT + t + 1)
                    act.activation(st[:, 1:2], st[:, 0:1], ACT.Sqrt, bias=eps[:, 0:1], scale=1.0 / D).then_inc(s_std, 1)
                    act.wait_ge(s_pr, CREDIT + t + 1)
                    act.wait_ge(s_st, CREDIT + 160 * t)
                    act.activation(pr[:, 0:2 * PCH].rearrange("p (c n) -> p c n", c=2), ps[:, 0:2, 0:PCH], ACT.Copy).then_inc(s_prA, 1)
                    act.wait_ge(s_st1, CREDIT + t + 1)
                    act.activation(st1[:, :], st1[:, :], ACT.Sqrt, bias=eps[:, 0:1]).then_inc(s_std1, 1)
                    act.wait_ge(s_up, CREDIT + t + 1)
                    act.activation(qk[:, 0:HM, :].rearrange("p (c n) d -> p c (n d)", c=2), ps[:, 0:2, 0:4 * QK], ACT.Copy).then_inc(s_upA, 1)
                    act.wait_ge(s_prD, CREDIT + t + 1)
                    ch(act.activation(gt[:, :], pr[:, C_GT:C_GT + 24], ACT.Sigmoid))
                    act.wait_ge(s_st2, CREDIT + t + 1)
                    act.activation(st2[:, :], st2[:, :], ACT.Sqrt, bias=eps[:, 0:1], scale=1.0 / QK).then_inc(s_std2, 1)
                    act.wait_ge(s_oT, CREDIT + 2 * t + 1)
                    act.activation(nT[:, :, :].rearrange("p (c n) d -> p c (n d)", c=2), ps[:, 0:2, :], ACT.Copy).then_inc(s_gt, 1)
                    act.wait_ge(s_oT, CREDIT + 2 * t + 2)
                    act.activation(qkT[:, 0:HM, :].rearrange("p (c n) d -> p c (n d)", c=2), ps[0:QK, 4:6, :], ACT.Copy).then_inc(s_oTA, 1)
                    ch.end()

            @block.vector
            def _(dve):
                dve.memset(eps[:, :], EPS).then_inc(s_eps, 1)
                dve.wait_ge(s_w, CREDIT + 16 * 28)
                with dve.Fori(0, NT) as t:
                    ch = Chain(dve, s_dch, t, DVE_A)
                    dve.wait_ge(s_std, CREDIT + t + 1)
                    ch(dve.reciprocal(st[:, 2:3], st[:, 1:2]))
                    dve.tensor_scalar(xn[:, :], x[:, :], st[:, 2:3], None, ALU.mult).then_inc(s_xn, 1)
                    dve.wait_ge(s_xT, CREDIT + t + 1)
                    dve.wait_ge(s_pr, CREDIT + t)
                    dve.tensor_tensor(hT[:, :, :].rearrange("p (c n) d -> p c n d", c=2), ps[:, 4:6, :].rearrange("p c (n d) -> p c n d", d=P),
                                      bcast(g_x[:, :].rearrange("p (c n) -> p c n", c=2).unsqueeze(3), [P, 2, 4, P]), ALU.mult).then_inc(s_hT, 1)
                    dve.wait_ge(s_pr, CREDIT + t + 1)
                    dve.wait_ge(s_st, CREDIT + 160 * t)
                    dve.tensor_copy(pr[:, 2 * PCH:].rearrange("p (c n) -> p c n", c=2), ps[:, 2:4, 0:PCH]).then_inc(s_prD, 1)
                    dve.wait_ge(s_prD, CREDIT + t + 1)
                    dve.wait_ge(s_prA, CREDIT + t + 1)
                    ch(dve.tensor_tensor(sq[:, :], pr[:, :], pr[:, :], ALU.mult))
                    ch(dve.tensor_reduce(st1[:, 0:1], sq[:, C_CQ:C_CQ + QR], AX.X, ALU.add))
                    ch(dve.tensor_reduce(st1[:, 1:2], sq[:, C_CKV:C_CKV + KVR], AX.X, ALU.add))
                    ch(dve.tensor_reduce(st1[:, 2:10], sq[:, C_Q:C_Q + 512].rearrange("p (h d) -> p h d", d=HD), AX.X, ALU.add))
                    ch(dve.tensor_reduce(st1[:, 10:12], sq[:, C_KS:C_KS + 128].rearrange("p (h d) -> p h d", d=HD), AX.X, ALU.add))
                    ch(dve.tensor_reduce(st1[:, 12:14], sq[:, C_KW:C_KW + 128].rearrange("p (h d) -> p h d", d=HD), AX.X, ALU.add))
                    dve.tensor_tensor(st1[:, :], st1[:, :], inv_d[:, :], ALU.mult).then_inc(s_st1, 1)
                    dve.wait_ge(s_std1, CREDIT + t + 1)
                    ch(dve.reciprocal(st1[:, :], st1[:, :]))
                    ch(dve.tensor_tensor(st1[:, :], st1[:, :], post[:, :], ALU.mult))
                    ch(dve.tensor_scalar(cn[:, 0:QR], pr[:, C_CQ:C_CQ + QR], st1[:, 0:1], None, ALU.mult))
                    dve.tensor_scalar(cn[:, QR:], pr[:, C_CKV:C_CKV + KVR], st1[:, 1:2], None, ALU.mult).then_inc(s_cn, 1)
                    dve.wait_ge(s_cT, CREDIT + t + 1)
                    dve.tensor_tensor(cT[:, :, :], ps[:, 6, 0:384].rearrange("p (n d) -> p n d", d=P),
                                      bcast(g_c[:, :].unsqueeze(2), [P, 3, P]), ALU.mult).then_inc(s_cTd, 1)
                    for dst, src, r, n in ((0, C_Q, 2, 8), (512, C_KS, 10, 2), (640, C_KW, 12, 2)):
                        d3 = nq[:, dst:dst + n * HD].rearrange("p (h d) -> p h d", d=HD)
                        dve.tensor_tensor(d3, pr[:, src:src + n * HD].rearrange("p (h d) -> p h d", d=HD),
                                          bcast(st1[:, r:r + n].unsqueeze(2), [P, n, HD]), ALU.mult).then_inc(s_nq, 1)
                    dve.wait_ge(s_nq, CREDIT + 4 * t + 3)
                    ch(dve.tensor_tensor(nq[:, 0:512].rearrange("p (h d) -> p h d", d=HD), nq[:, 0:512].rearrange("p (h d) -> p h d", d=HD),
                                         bcast(g_qn[:, :].unsqueeze(1), [P, 8, HD]), ALU.mult))
                    dve.tensor_tensor(nq[:, 512:].rearrange("p (h d) -> p h d", d=HD), nq[:, 512:].rearrange("p (h d) -> p h d", d=HD),
                                      bcast(g_kn[:, :].unsqueeze(1), [P, 4, HD]), ALU.mult).then_inc(s_nq, 1)
                    dve.wait_ge(s_up, CREDIT + t + 1)
                    kv = ps[:, 2:4, :].rearrange("p c (n d) -> p c n d", d=NOPE + VD)
                    ch(dve.tensor_copy(qk[:, HM:, 0:NOPE].rearrange("p (c n) d -> p c n d", c=2), kv[:, :, :, 0:NOPE]))
                    dve.tensor_copy(v_m[:, :, :].rearrange("p (c n) d -> p c n d", c=2), kv[:, :, :, NOPE:]).then_inc(s_upD, 1)
                    ch(dve.tensor_copy(qk[:, HM:, NOPE:], bcast(pr[:, C_KR:C_KR + ROPE].unsqueeze(1), [P, HM, ROPE])))
                    dve.wait_ge(s_upA, CREDIT + t + 1)
                    ch(dve.tensor_tensor(sqk[:, :, :], qk[:, :, :], qk[:, :, :], ALU.mult))
                    dve.tensor_reduce(st2[:, :], sqk[:, :, :], AX.X, ALU.add).then_inc(s_st2, 1)
                    dve.wait_ge(s_std2, CREDIT + t + 1)
                    ch(dve.reciprocal(st2[:, :], st2[:, :]))
                    ch(dve.tensor_tensor(st2[:, :], st2[:, :], post2[:, :], ALU.mult))
                    ch(dve.tensor_tensor(qk[:, :, :], qk[:, :, :], bcast(st2[:, :].unsqueeze(2), [P, 16, QK]), ALU.mult))
                    dve.tensor_tensor(qk[:, :, :], qk[:, :, :], g_qk[:, :, :], ALU.mult).then_inc(s_qkg, 1)
                    dve.wait_ge(s_qkg, CREDIT + t + 1)
                    x1, x2 = qk[:, :, NOPE:NOPE + 16], qk[:, :, NOPE + 16:]
                    cos, sin = (bcast(trig[:, a:a + 16].unsqueeze(1), [P, 16, 16]) for a in (0, 16))
                    for n, (a, b) in enumerate(((x1, cos), (x2, sin), (x2, cos), (x1, sin))):
                        dve.tensor_tensor(ra[:, n, :, :], a, b, ALU.mult).then_inc(s_ra, 1)
                    dve.wait_ge(s_ra, CREDIT + 4 * t + 4)
                    dve.tensor_tensor(x1, ra[:, 0, :, :], ra[:, 1, :, :], ALU.subtract).then_inc(s_ro, 1)
                    dve.tensor_tensor(x2, ra[:, 2, :, :], ra[:, 3, :, :], ALU.add).then_inc(s_qk, 1)
                    dve.wait_ge(s_oT, CREDIT + 2 * t + 2)
                    dve.tensor_copy(qkT[:, HM:, :].rearrange("p (c n) d -> p c (n d)", c=2), ps[0:QK, 6:8, :]).then_inc(s_oTD, 1)
                    dve.wait_ge(s_oTD, CREDIT + t + 1)
                    ch.end()

            @block.tensor
            def _(pe):
                pe.wait_ge(s_w, CREDIT + 16 * 28)
                with pe.Fori(0, NT) as t:
                    pe.wait_ge(s_xn, CREDIT + t + 1)
                    pe.wait_ge(s_oTA, CREDIT + t)
                    for k in range(KD):
                        mm = pe.transpose(ps[:, 4 + k // 4, (k % 4) * P:(k % 4 + 1) * P], xn[:, k * P:(k + 1) * P], ident[:, :])
                    mm.then_inc(s_xT, 1)
                    pe.wait_ge(s_hT, CREDIT + t + 1)
                    pe.wait_ge(s_gt, CREDIT + t)
                    for c in range(4):
                        for k in range(KD):
                            mm = pe.matmul(ps[:, c, 0:PCH], hT[:, k, :], w_in[:, k, c * PCH:(c + 1) * PCH], start=(k == 0), stop=(k == KD - 1))
                    mm.then_inc(s_pr, 1)
                    pe.wait_ge(s_cn, CREDIT + t + 1)
                    pe.wait_ge(s_oTD, CREDIT + t)
                    for k in range(3):
                        mm = pe.transpose(ps[:, 6, k * P:(k + 1) * P], cn[:, k * P:(k + 1) * P], ident[:, :])
                    mm.then_inc(s_cT, 1)
                    pe.wait_ge(s_cTd, CREDIT + t + 1)
                    pe.wait_ge(s_prA, CREDIT + t + 1)
                    pe.wait_ge(s_prD, CREDIT + t + 1)
                    for c in range(2):
                        for k in range(2):
                            pe.matmul(ps[:, c, 0:4 * QK], cT[:, k, :], w_uq[:, k, c * 4 * QK:(c + 1) * 4 * QK], start=(k == 0), stop=(k == 1))
                    for c in range(2):
                        mm = pe.matmul(ps[:, 2 + c, :], cT[:, 2, :], w_ukv[:, c * 512:(c + 1) * 512], start=True, stop=True)
                    mm.then_inc(s_up, 1)
                    pe.wait_ge(s_nq, CREDIT + 4 * t + 4)
                    pe.wait_ge(s_upA, CREDIT + t + 1)
                    for j in range(8):
                        src = nq[:, j * P:(j + 1) * P] if j < 6 else pr[:, C_KC + (j - 6) * P:C_KC + (j - 5) * P]
                        mm = pe.transpose(ps[:, j // 4, (j % 4) * P:(j % 4 + 1) * P], src, ident[:, :])
                    mm.then_inc(s_oT, 1)
                    pe.wait_ge(s_qk, CREDIT + t + 1)
                    for j in range(2 * HM):
                        mm = pe.transpose(ps[0:QK, 4 + j // 4, (j % 4) * P:(j % 4 + 1) * P], qk[:, j, :], ident[:, :])
                    mm.then_inc(s_oT, 1)


def stage_compress(nc, e):
    with ExitStack() as ctx:
        sb, sem, ps = add_tools(nc, e, ctx)
        ident = sb("ident_c", [P, P])
        kcT = sb("kcT_all", [HD, 2, G, S])
        w1 = sb("w1", [HD, 2, CMP_LEN, CMP_HID])
        w2 = sb("w2", [CMP_HID, 2, HD])
        pos = sb("pos", [CMP_LEN, 2, HD])
        posT = sb("posT", [HD, 2, CMP_LEN])
        pb = sb("pb", [CMP_HID, 2])
        gk = sb("gk", [P, HD])
        eps = sb("eps_c", [P, 1])
        u = sb("u", [CMP_HID, 2, G * NCMP])
        hid = sb("hid", [CMP_HID, 2, G * NCMP])
        cc = sb("cc", [NCMP, 2 * G, HD])
        sq = sb("sq_c", [NCMP, G, HD])
        st = sb("st_c", [NCMP, G])
        kT = sb("kT_c", [HD, G, NCMP])
        s_in, s_ps, s_dv, s_act, s_out = (sem("c_" + n) for n in ("in", "pe", "dve", "act", "stored"))
        with nc.Block() as block:
            @block.gpsimd
            def _(pool):
                give_credit(pool, e.sems)

            @block.sync
            def _(sp):
                sp.dma_start(ident[:, :], e.c_ident).then_inc(s_in, 16)
                sp.dma_start(gk[:, :], e.g_k_nsa[0].partition_broadcast(P)).then_inc(s_in, 16)
                for i in range(2):
                    for g in range(G):
                        sp.dma_start(kcT[:, i, g, :], e.d_cn[i, g * HD:(g + 1) * HD, :]).then_inc(s_in, 16)
                for i, (a, b, c) in enumerate(((e.cmp_k_w1, e.cmp_k_w2, e.cmp_k_pos), (e.cmp_v_w1, e.cmp_v_w2, e.cmp_v_pos))):
                    sp.dma_start(w1[:, i, :, :], a[0].rearrange("l d f -> d l f")).then_inc(s_in, 16)
                    sp.dma_start(w2[:, i, :], b[0]).then_inc(s_in, 16)
                    sp.dma_start(pos[:, i, :], c[0]).then_inc(s_in, 16)
                sp.wait_ge(s_dv, CREDIT + 11)
                sp.dma_start(e.d_ck.rearrange("g d n -> d g n"), kT[:, :, :]).then_inc(s_out, 16)
                sp.dma_start(e.d_cv.rearrange("g n d -> n g d"), cc[:, G:, :]).then_inc(s_out, 16)
                sp.wait_ge(s_out, CREDIT + 32)

            @block.tensor
            def _(pe):
                pe.wait_ge(s_in, CREDIT + 16 * 12)
                for i in range(2):
                    mm = pe.transpose(ps[0:HD, 0, i * CMP_LEN:(i + 1) * CMP_LEN], pos[:, i, :], ident[0:CMP_LEN, 0:CMP_LEN])
                mm.then_inc(s_ps, 1)
                pe.wait_ge(s_dv, CREDIT + 2)
                for i in range(2):
                    for l in range(CMP_LEN):
                        mv = kcT[:, i, :, l:l + CMP_STRIDE * (NCMP - 1) + 1:CMP_STRIDE]
                        pe.matmul(ps[:, 1 + i, 0:G * NCMP].rearrange("p (g n) -> p g n", g=G), w1[:, i, l, :], mv, start=(l == 0), stop=(l == CMP_LEN - 1))
                    for l in range(CMP_LEN):
                        mm = pe.matmul(ps[:, 3 + i, 0:1], w1[:, i, l, :], posT[:, i, l:l + 1], start=(l == 0), stop=(l == CMP_LEN - 1))
                mm.then_inc(s_ps, 1)
                pe.wait_ge(s_act, CREDIT + 2)
                for i in range(2):
                    for g in range(G):
                        mm = pe.matmul(ps[0:NCMP, 5, (i * G + g) * HD:(i * G + g + 1) * HD], hid[:, i, g * NCMP:(g + 1) * NCMP], w2[:, i, :], start=True, stop=True)
                mm.then_inc(s_ps, 1)
                pe.wait_ge(s_dv, CREDIT + 10)
                for g in range(G):
                    mm = pe.transpose(ps[0:HD, 6, g * P:g * P + NCMP], cc[:, g, :], ident[0:NCMP, 0:NCMP])
                mm.then_inc(s_ps, 1)

            @block.scalar
            def _(act):
                for i in range(2):
                    act.wait_ge(s_dv, CREDIT + 4 + 2 * i)
                    act.activation(hid[:, i, :], u[:, i, :], ACT.Gelu_apprx_tanh).then_inc(s_act, 1)
                act.wait_ge(s_dv, CREDIT + 9)
                act.activation(st[:, :], st[:, :], ACT.Sqrt, bias=eps[0:NCMP, 0:1], scale=1.0 / HD).then_inc(s_act, 1)

            @block.vector
            def _(dve):
                n = [0]

                def step(ins):
                    ins.then_inc(s_dv, 1)
                    n[0] += 1
                    dve.wait_ge(s_dv, CREDIT + n[0])
                step(dve.memset(eps[:, :], EPS))
                dve.wait_ge(s_ps, CREDIT + 1)
                step(dve.tensor_copy(posT[:, :, :], ps[0:HD, 0, 0:2 * CMP_LEN].rearrange("p (i l) -> p i l", i=2)))
                dve.wait_ge(s_ps, CREDIT + 2)
                for i in range(2):
                    step(dve.tensor_copy(pb[:, i:i + 1], ps[:, 3 + i, 0:1]))
                    step(dve.tensor_scalar(u[:, i, :], ps[:, 1 + i, 0:G * NCMP], pb[:, i:i + 1], None, ALU.add))
                dve.wait_ge(s_ps, CREDIT + 3)
                dve.wait_ge(s_in, CREDIT + 16 * 12)
                step(dve.tensor_copy(cc[:, :, :], ps[0:NCMP, 5, 0:2 * G * HD].rearrange("p (i d) -> p i d", d=HD)))
                step(dve.tensor_tensor(sq[:, :, :], cc[:, 0:G, :], cc[:, 0:G, :], ALU.mult))
                step(dve.tensor_reduce(st[:, :], sq[:, :, :], AX.X, ALU.add))
                dve.wait_ge(s_act, CREDIT + 3)
                dve.reciprocal(st[:, :], st[:, :]).then_inc(s_act, 1)
                dve.wait_ge(s_act, CREDIT + 4)
                dve.tensor_tensor(cc[:, 0:G, :], cc[:, 0:G, :], bcast(st[:, :].unsqueeze(2), [NCMP, G, HD]), ALU.mult).then_inc(s_act, 1)
                dve.wait_ge(s_act, CREDIT + 5)
                step(dve.tensor_tensor(cc[:, 0:G, :], cc[:, 0:G, :], bcast(gk[0:NCMP, :].unsqueeze(1), [NCMP, G, HD]), ALU.mult))
                dve.wait_ge(s_ps, CREDIT + 4)
                step(dve.tensor_copy(kT[:, :, :], ps[0:HD, 6, 0:G * P].rearrange("p (g n) -> p g n", g=G)[:, :, 0:NCMP]))


def stage_attend(nc, e):
    STEPS = [(b, q) for b in "mcws" for q in range(NT)]
    NS = len(STEPS)

    def tiles(b, q):
        return [0] if b == "c" else list(range(max(0, q - WIN // P), q + 1)) if b == "w" else list(range(q + 1))

    def width(b, q):
        return min(NCMP, (P * (q + 1) - CMP_LEN) // CMP_STRIDE + 1) if b == "c" else P * len(tiles(b, q))

    groups = [(len(tiles(*s)) + 3) // 4 for s in STEPS]
    NG = sum(groups)
    N2 = sum(g == 2 for g in groups)
    gdone = [sum(groups[:i + 1]) for i in range(NS)]
    g2done = [sum(g == 2 for g in groups[:i + 1]) for i in range(NS)]
    with ExitStack() as ctx:
        sb, sem, ps = add_tools(nc, e, ctx)
        ident = sb("ident_t", [P, P])
        qm, km = sb("qm", [QK, S]), sb("km", [QK, S])
        vm = sb("vm", [P, NT, VD])
        qn = sb("qn", [HD, S])
        kn = sb("kn", [HD, 2, S])
        vn = sb("vn", [P, 2, NT, HD])
        ck, cv = sb("ck", [HD, NCMP]), sb("cv", [NCMP, HD])
        mstrip, strip, wstrip = sb("mstrip", [P, S]), sb("strip_t", [P, S]), sb("wstrip", [P, WIN + P])
        gates = sb("gates", [P, NT, 3])
        cvalid = sb("cvalid", [P, 1])
        sc = sb("sc", [P, 4, S])
        pT = sb("pT", [P, 2, S])
        mx, nm, rs, co = (sb(n, [P, 4]) for n in ("mx", "nm", "rs", "co"))
        ym, yn = sb("ym", [P, NT, VD]), sb("yn", [P, NT, HD])
        s_c, s_lm, s_ln, s_fm, s_g = (sem("t_" + n) for n in ("const", "load_mla", "load_nsa", "mla_used", "gate"))
        s_s, s_m, s_p, s_pT, s_cA, s_cD, s_o, s_y = (sem("t_" + n) for n in
            ("scores", "max", "probs", "probsT", "copiedA", "copiedD", "out", "y"))
        s_ym, s_yn, s_dch, s_hd = (sem("t_" + n) for n in ("ym_stored", "yn_stored", "dve_chain", "sc_set"))
        NLN = 9
        DCH = 3 * NS - NT + 1
        dy = e.d_y.rearrange("(t p) n -> p t n", p=P)
        with nc.Block() as block:
            @block.gpsimd
            def _(pool):
                give_credit(pool, e.sems)

            @block.sync
            def _(sp):
                sp.dma_start(ident[:, :], e.c_ident).then_inc(s_c, 16)
                sp.dma_start(mstrip[:, :], e.d_strip[HN]).then_inc(s_c, 16)
                sp.dma_start(cvalid[:, :], e.c_cvalid).then_inc(s_c, 16)
                with sp.Fori(0, HM) as h:
                    one = bass.ds(h, 1)
                    sp.wait_ge(s_o, CREDIT + NS * h + 0)
                    sp.wait_ge(s_y, CREDIT + NS * h)
                    g = bass.ds(h // HPG, 1)
                    gd = bass.ds((h // HPG) * HD, HD)
                    sp.dma_start(qm[:, :], e.d_qm[one].rearrange("o d n -> (o d) n")).then_inc(s_lm, 16)
                    sp.dma_start(km[:, :], e.d_km[one].rearrange("o d n -> (o d) n")).then_inc(s_lm, 16)
                    sp.dma_start(vm[:, :, :], e.d_vm[one].rearrange("o (t p) d -> p (o t) d", p=P)).then_inc(s_lm, 16)
                    sp.dma_start(ck[:, :], e.d_ck[g].rearrange("o d n -> (o d) n")).then_inc(s_ln, 16)
                    sp.dma_start(cv[:, :], e.d_cv[g].rearrange("o n d -> (o n) d")).then_inc(s_ln, 16)
                    sp.dma_start(qn[:, :], e.d_qn_flat[one].rearrange("o d n -> (o d) n")).then_inc(s_ln, 16)
                    sp.dma_start(kn[:, :, :], e.d_kn[:, gd, :].rearrange("w d n -> d w n")).then_inc(s_ln, 16)
                    for i in range(2):
                        sp.dma_start(vn[:, i, :, :], e.d_vn[i][g].rearrange("o (t p) d -> p (o t) d", p=P)).then_inc(s_ln, 16)
                    sp.dma_start(strip[:, :], e.d_strip[one].rearrange("o p n -> (o p) n")).then_inc(s_ln, 16)
                    sp.dma_start(wstrip[:, :], e.d_wstrip[one].rearrange("o p n -> (o p) n")).then_inc(s_ln, 16)
                    with nc.allow_non_contiguous_dma("12-byte gates"):
                        sp.dma_start(gates[:, :, :], e.d_gt[one].rearrange("o (t p) b -> p (o t) b", p=P)).then_inc(s_ln, 16)
                    sp.wait_ge(s_y, CREDIT + NS * h + NT)
                    sp.dma_start(dy[:, :, bass.ds(h * VD, VD)], ym[:, :, :]).then_inc(s_ym, 16)
                    sp.wait_ge(s_y, CREDIT + NS * h + NS)
                    sp.dma_start(dy[:, :, bass.ds(h * HD + HM * VD, HD)], yn[:, :, :]).then_inc(s_yn, 16)
                sp.wait_ge(s_ym, CREDIT + 16 * HM)
                sp.wait_ge(s_yn, CREDIT + 16 * HM)

            @block.tensor
            def _(pe):
                pe.wait_ge(s_c, CREDIT + 48)
                with pe.Fori(0, HM) as h:
                    def scores(i):
                        b, q = STEPS[i]
                        if i == 0:
                            pe.wait_ge(s_lm, CREDIT + 48 * h + 48)
                        if i == NT:
                            pe.wait_ge(s_ln, CREDIT + 16 * NLN * h + 16 * NLN)
                        pe.wait_ge(s_m, CREDIT + NS * h + max(i - 1, 0))
                        hold(pe, e.pe_passed)
                        w, lo = width(b, q), tiles(b, q)[0] * P
                        Q = qm if b == "m" else qn
                        K = {"m": km, "c": ck, "w": kn[:, 1, :], "s": kn[:, 0, :]}[b][:, lo:lo + w]
                        for c in range(0, w, 512):
                            mm = pe.matmul(ps[:, 2 * (i % 2) + c // 512, 0:min(512, w - c)], Q[:, q * P:(q + 1) * P], K[:, c:min(c + 512, w)],
                                           start=True, stop=True)
                        mm.then_inc(s_s, 1)

                    def turn(i):
                        pe.wait_ge(s_p, CREDIT + NS * h + i + 1)
                        hold(pe, e.pe_passed)
                        n = len(tiles(*STEPS[i]))
                        for j in range(groups[i]):
                            if j == 0:
                                pe.wait_ge(s_cA, CREDIT + NS * h + i)
                            else:
                                pe.wait_ge(s_cD, CREDIT + N2 * h + g2done[i] - 1)
                            hold(pe, e.pe_passed)
                            for k in range(4 * j, min(n, 4 * j + 4)):
                                mm = pe.transpose(ps[:, 4 + j, (k % 4) * P:(k % 4 + 1) * P], sc[:, i % 4, k * P:(k + 1) * P], ident[:, :])
                            mm.then_inc(s_pT, 1)

                    def values(i):
                        b, q = STEPS[i]
                        pe.wait_ge(s_cA, CREDIT + NS * h + i + 1)
                        if groups[i] == 2:
                            pe.wait_ge(s_cD, CREDIT + N2 * h + g2done[i])
                        pe.wait_ge(s_y, CREDIT + NS * h + max(i - 1, 0))
                        hold(pe, e.pe_passed)
                        ts = tiles(b, q)
                        for n, k in enumerate(ts):
                            if b == "c":
                                w = width(b, q)
                                mm = pe.matmul(ps[:, 6 + i % 2, 0:HD], pT[0:w, i % 2, 0:P], cv[0:w, :], start=True, stop=True)
                            else:
                                V = vm[:, k, :] if b == "m" else vn[:, "sw".index(b), k, :]
                                mm = pe.matmul(ps[:, 6 + i % 2, 0:HD], pT[:, i % 2, n * P:(n + 1) * P], V, start=(n == 0), stop=(n == len(ts) - 1))
                        mm.then_inc(s_o, 1)

                    scores(0)
                    scores(1)
                    for i in range(NS):
                        turn(i)
                        if i:
                            values(i - 1)
                        if i + 2 < NS:
                            scores(i + 2)
                    values(NS - 1)

            @block.scalar
            def _(act):
                act.wait_ge(s_c, CREDIT + 48)
                with act.Fori(0, HM) as h:
                    def copy(i):
                        act.wait_ge(s_pT, CREDIT + NG * h + gdone[i] - groups[i] + 1)
                        act.wait_ge(s_o, CREDIT + NS * h + max(i - 1, 0))
                        w = P * min(4, len(tiles(*STEPS[i])))
                        act.activation(pT[:, i % 2, 0:w], ps[:, 4, 0:w], ACT.Copy).then_inc(s_cA, 1)

                    def exps(i):
                        act.wait_ge(s_m, CREDIT + NS * h + i + 1)
                        w = width(*STEPS[i])
                        act.activation(sc[:, i % 4, 0:w], sc[:, i % 4, 0:w], ACT.Exp, bias=nm[:, i % 4:i % 4 + 1],
                                       accum_out=rs[:, i % 4:i % 4 + 1]).then_inc(s_p, 1)

                    exps(0)
                    for i in range(NS):
                        if i + 1 < NS:
                            exps(i + 1)
                        copy(i)

            @block.vector
            def _(dve):
                dve.memset(sc[:, :, :], 0.0).then_inc(s_hd, 1)
                dve.wait_ge(s_hd, CREDIT + 1)
                dve.wait_ge(s_c, CREDIT + 48)
                with dve.Fori(0, HM) as h:
                    ch = Chain(dve, s_dch, h, DCH)

                    def peak(i):
                        b, q = STEPS[i]
                        w = width(b, q)
                        if b == "c":
                            bias = strip[:, S + CMP_LEN - 1 - P * (q + 1):S + CMP_LEN - 1 - P * (q + 1) + CMP_STRIDE * (w - 1) + 1:CMP_STRIDE]
                        elif b == "w":
                            bias = wstrip[:, WIN + P - w:]
                        else:
                            bias = (mstrip if b == "m" else strip)[:, S - w:]
                        if i == NT:
                            dve.wait_ge(s_ln, CREDIT + 16 * NLN * h + 16 * NLN)
                            ch(dve.tensor_tensor(gates[:, 0, 0:1], gates[:, 0, 0:1], cvalid[:, :], ALU.mult))
                        dve.wait_ge(s_s, CREDIT + NS * h + i + 1)
                        dve.wait_ge(s_pT, CREDIT + NG * h + (gdone[i - 4] if i >= 4 else 0))
                        hold(dve, e.dve_passed)
                        src = ps[:, 2 * (i % 2):2 * (i % 2) + 2, :].rearrange("p c n -> p (c n)")[:, 0:w]
                        ch(dve.tensor_tensor_reduce(sc[:, i % 4, 0:w], src, bias, 1.0, -3.0e38, ALU.add, ALU.max, mx[:, i % 4:i % 4 + 1]))
                        dve.tensor_scalar(nm[:, i % 4:i % 4 + 1], mx[:, i % 4:i % 4 + 1], -1.0, None, ALU.mult).then_inc(s_m, 1)

                    def copy(i):
                        if groups[i] == 2:
                            n = len(tiles(*STEPS[i])) - 4
                            dve.wait_ge(s_pT, CREDIT + NG * h + gdone[i])
                            dve.wait_ge(s_o, CREDIT + NS * h + max(i - 1, 0))
                            dve.tensor_copy(pT[:, i % 2, 512:512 + n * P], ps[:, 5, 0:n * P]).then_inc(s_cD, 1)

                    def finish(i):
                        b, q = STEPS[i]
                        k = i % 4
                        if i == 0:
                            dve.wait_ge(s_ym, CREDIT + 16 * h)
                        if i == NT:
                            dve.wait_ge(s_yn, CREDIT + 16 * h)
                        dve.wait_ge(s_o, CREDIT + NS * h + i + 1)
                        ch(dve.reciprocal(co[:, k:k + 1], rs[:, k:k + 1]))
                        O = ps[:, 6 + i % 2, 0:HD]
                        if b == "m":
                            dve.tensor_scalar(ym[:, q, :], O, co[:, k:k + 1], None, ALU.mult).then_inc(s_y, 1)
                        else:
                            ch(dve.tensor_tensor(co[:, k:k + 1], co[:, k:k + 1], gates[:, q, "csw".index(b):"csw".index(b) + 1], ALU.mult))
                            if b == "c":
                                dve.tensor_scalar(yn[:, q, :], O, co[:, k:k + 1], None, ALU.mult).then_inc(s_y, 1)
                            else:
                                dve.scalar_tensor_tensor(yn[:, q, :], O, co[:, k:k + 1], yn[:, q, :], ALU.mult, ALU.add).then_inc(s_y, 1)

                    peak(0)
                    for i in range(NS):
                        if i + 1 < NS:
                            peak(i + 1)
                        copy(i)
                        if i:
                            finish(i - 1)
                    finish(NS - 1)
                    ch.end()


def stage_memory(nc, e):
    with ExitStack() as ctx:
        sb, sem, ps = add_tools(nc, e, ctx)
        MT = N_MEM // P
        ident = sb("ident_m", [P, P])
        w = sb("w_mkv", [P, KD, 2 * MH * MHD])
        gx, gk = sb("gx_m", [P, KD]), sb("gk_m", [P, MHD])
        eps = sb("eps_m", [P, 1])
        m, mn, sq = sb("m", [P, MT, D]), sb("mn", [P, D]), sb("sq_m", [P, D])
        st, sk = sb("st_m", [P, 2]), sb("sk_m", [P, MH])
        mT = sb("mT", [P, KD, P])
        kk = sb("kk", [P, MH, MHD])
        none = sb("none", [P, 2 * NE * CAP // P], U32)
        s_in, s_pe, s_act, s_dv, s_z, s_k = (sem("m_" + n) for n in ("in", "pe", "act", "dve", "rows_unused", "key"))
        with nc.Block() as block:
            @block.sync
            def _(sp):
                for dst, src in ((ident[:, :], e.c_ident), (w[:, :, :], e.w_mkv[0].rearrange("(k p) n -> p k n", p=P)),
                                 (m[:, :, :], e.mem[0].rearrange("(t p) d -> p t d", p=P)), (gk[:, :], e.g_mk[0].partition_broadcast(P))):
                    sp.dma_start(dst, src).then_inc(s_in, 16)
                with nc.allow_non_contiguous_dma("gain columns, once"):
                    sp.dma_start(gx[:, :], e.g_mem_src[0].rearrange("(k p) -> p k", p=P)).then_inc(s_in, 16)
                sp.wait_ge(s_z, CREDIT + 1)
                sp.dma_start(e.d_tok.rearrange("(p n) o -> p (n o)", p=P), none[:, :]).then_inc(s_z, 16)
                sp.wait_ge(s_z, CREDIT + 17)

            @block.gpsimd
            def _(pool):
                give_credit(pool, e.sems)
                pool.memset(none[:, :], NOBODY).then_inc(s_z, 1)

            @block.scalar
            def _(act):
                act.wait_ge(s_in, CREDIT + 80)
                for i in range(MT):
                    act.wait_ge(s_dv, CREDIT + 7 * i + 1)
                    act.activation(sq[:, :], m[:, i, :], ACT.Square, accum_out=st[:, 0:1]).then_inc(s_act, 1)
                    act.wait_ge(s_act, CREDIT + 3 * i + 1)
                    act.activation(st[:, 1:2], st[:, 0:1], ACT.Sqrt, bias=eps[:, 0:1], scale=1.0 / D).then_inc(s_act, 1)
                    act.wait_ge(s_dv, CREDIT + 7 * i + 5)
                    act.activation(sk[:, :], sk[:, :], ACT.Sqrt, bias=eps[:, 0:1], scale=1.0 / MHD).then_inc(s_act, 1)

            @block.vector
            def _(dve):
                n = [0]

                def step(ins):
                    ins.then_inc(s_dv, 1)
                    n[0] += 1
                    dve.wait_ge(s_dv, CREDIT + n[0])

                step(dve.memset(eps[:, :], EPS))
                dve.wait_ge(s_in, CREDIT + 80)
                for i in range(MT):
                    dve.wait_ge(s_act, CREDIT + 3 * i + 2)
                    dve.reciprocal(st[:, 1:2], st[:, 1:2]).then_inc(s_k, 1)
                    dve.wait_ge(s_k, CREDIT + 4 * i + 1)
                    step(dve.tensor_scalar(mn[:, :], m[:, i, :], st[:, 1:2], None, ALU.mult))
                    dve.wait_ge(s_pe, CREDIT + 3 * i + 1)
                    step(dve.tensor_tensor(mT[:, :, :].rearrange("p (c n) d -> p c n d", c=2), ps[:, 0:2, :].rearrange("p c (n d) -> p c n d", d=P),
                                           bcast(gx[:, :].rearrange("p (c n) -> p c n", c=2).unsqueeze(3), [P, 2, 4, P]), ALU.mult))
                    dve.wait_ge(s_pe, CREDIT + 3 * i + 2)
                    dve.tensor_copy(kk[:, :, :], ps[:, 2, 0:256].rearrange("p (h d) -> p h d", d=MHD)).then_inc(s_k, 1)
                    dve.wait_ge(s_k, CREDIT + 4 * i + 2)
                    step(dve.tensor_tensor(sq[:, 0:256].rearrange("p (h d) -> p h d", d=MHD), kk[:, :, :], kk[:, :, :], ALU.mult))
                    step(dve.tensor_reduce(sk[:, :], sq[:, 0:256].rearrange("p (h d) -> p h d", d=MHD), AX.X, ALU.add))
                    dve.wait_ge(s_act, CREDIT + 3 * i + 3)
                    dve.reciprocal(sk[:, :], sk[:, :]).then_inc(s_k, 1)
                    dve.wait_ge(s_k, CREDIT + 4 * i + 3)
                    dve.tensor_tensor(kk[:, :, :], kk[:, :, :], bcast(sk[:, :].unsqueeze(2), [P, MH, MHD]), ALU.mult).then_inc(s_k, 1)
                    dve.wait_ge(s_k, CREDIT + 4 * i + 4)
                    step(dve.tensor_tensor(kk[:, :, :], kk[:, :, :], bcast(gk[:, :].unsqueeze(1), [P, MH, MHD]), ALU.mult))
                    step(dve.tensor_copy(e.vmem[:, i, :, :], ps[:, 2, 256:512].rearrange("p (h d) -> p h d", d=MHD)))
                    dve.wait_ge(s_pe, CREDIT + 3 * i + 3)
                    step(dve.tensor_copy(e.kTm[:, :, i * P:(i + 1) * P], ps[:, 3, 0:256].rearrange("p (j n) -> p j n", n=P)))

            @block.tensor
            def _(pe):
                pe.wait_ge(s_in, CREDIT + 80)
                for i in range(MT):
                    pe.wait_ge(s_dv, CREDIT + 7 * i + 2)
                    for k in range(KD):
                        mm = pe.transpose(ps[:, k // 4, (k % 4) * P:(k % 4 + 1) * P], mn[:, k * P:(k + 1) * P], ident[:, :])
                    mm.then_inc(s_pe, 1)
                    pe.wait_ge(s_dv, CREDIT + 7 * i + 3)
                    for k in range(KD):
                        mm = pe.matmul(ps[:, 2, :], mT[:, k, :], w[:, k, :], start=(k == 0), stop=(k == KD - 1))
                    mm.then_inc(s_pe, 1)
                    pe.wait_ge(s_dv, CREDIT + 7 * i + 6)
                    for j in range(2):
                        mm = pe.transpose(ps[:, 3, j * P:(j + 1) * P], kk[:, 2 * j:2 * j + 2, :].rearrange("p h d -> p (h d)"), ident[:, :])
                    mm.then_inc(s_pe, 1)


def stage_mix(nc, e):
    with ExitStack() as ctx:
        sb, sem, ps = add_tools(nc, e, ctx)
        ident, before, ones = sb("ident_x", [P, P]), sb("before", [P, P]), sb("ones", [P, P])
        w_out, w_mq = sb("w_out", [P, KD, D]), sb("w_mq", [P, KD, MH * MHD])
        w_mo, rw = sb("w_mo", [P, 2, D]), sb("rw", [P, KD, NE])
        bdown = sb("bdown", [NE, D])
        g_o, g_m, g_e = sb("g_o", [P, KD]), sb("g_m", [P, KD]), sb("g_e", [P, D])
        g_q, rb, iota, ebase = sb("g_q", [P, MHD]), sb("rb", [P, NE]), sb("iota", [P, NE]), sb("ebase", [P, NE])
        eps = sb("eps_x", [P, 1])
        tok = sb("tok", [P, TOPK, 2], U32)
        x, y = sb("x_x", [P, D]), sb("y_x", [P, D])
        sq, h, hT = sb("sq_x", [P, D]), sb("h_x", [P, D]), sb("hT_x", [P, KD, P])
        x1, x2, x3 = sb("x1", [P, D]), sb("x2", [P, D]), sb("x3", [P, D])
        st = sb("st_x", [P, 4])
        q, sq4 = sb("q_x", [P, MH, MHD]), sb("sq4", [P, MH])
        qT = sb("qT_x", [P, 2, P])
        pr, pT = sb("pr_x", [P, MH, N_MEM]), sb("pT_x", [P, 2 * MH, P])
        mx, rs = sb("mx_x", [P, MH]), sb("rs_x", [P, MH])
        o, oT = sb("o_x", [P, MH, MHD]), sb("oT_x", [P, 2, P])
        lg, m8, i8, i8f = sb("lg", [P, NE]), sb("m8", [P, 8]), sb("i8", [P, 8], U32), sb("i8f", [P, 8])
        g4, gs, hot, tmp = sb("g4", [P, TOPK]), sb("gs", [P, 2]), sb("hot", [P, TOPK, NE]), sb("tmp", [P, TOPK, NE])
        mask, gm, gmT, where = sb("mask", [P, NE]), sb("gm", [P, NE]), sb("gmT", [NE, P]), sb("where", [P, NE])
        slf, slot = sb("slf", [P, TOPK]), sb("slot", [P, TOPK], U32)
        s_w, s_in, s_tok, s_dv, s_ak, s_sd, s_st = (sem("x_" + n) for n in ("weights", "in", "tok", "dve", "act", "scatter_done", "stored"))
        s_sc = e.dma_sem("x_scattered")
        names = ("ssy yn yT yTd o1 x1 ss1 h2 h2T h2Td q qn qT qTd s mx p pT pTc O on oT oTd mo x2 ss2 h3 h3T h3Td lg gx g4 "
                 "msk rk gmT slot bd x3").split()
        m = {n: sem("x_m_" + n) for n in names + ["s0", "qd"]}

        N_W = 18
        DV, AK = 24, 4
        with nc.Block() as block:
            @block.sync
            def _(sp):
                n = 0
                for dst, src in ((ident[:, :], e.c_ident), (before[:, :], e.c_before), (ones[:, :], e.c_ones),
                                 (w_out[:, :, :], e.w_out[0].rearrange("(k p) n -> p k n", p=P)),
                                 (w_mq[:, :, :], e.w_mq[0].rearrange("(k p) n -> p k n", p=P)),
                                 (w_mo[:, :, :], e.w_mo[0].rearrange("(k p) n -> p k n", p=P)),
                                 (rw[:, :, :], e.router_w[0].rearrange("(k p) n -> p k n", p=P)), (bdown[:, :], e.b_down[0]),
                                 (g_e[:, :], e.g_moe_norm[0].partition_broadcast(P)), (g_q[:, :], e.g_mq[0].partition_broadcast(P)),
                                 (rb[:, :], e.router_b[0].partition_broadcast(P)), (iota[:, :], e.c_iota.partition_broadcast(P)),
                                 (ebase[:, :], e.c_ebase.partition_broadcast(P))):
                    sp.dma_start(dst, src).then_inc(s_w, 16)
                    n += 1
                with nc.allow_non_contiguous_dma("gain columns, once"):
                    for dst, src in ((g_o[:, 0:4], e.g_out_mla[0].rearrange("(k p) -> p k", p=P)),
                                     (g_o[:, 4:8], e.g_out_nsa[0].rearrange("(k p) -> p k", p=P)),
                                     (g_m[:, :], e.g_mem_norm[0].rearrange("(k p) -> p k", p=P))):
                        sp.dma_start(dst, src).then_inc(s_w, 16)
                        n += 1
                assert n == N_W - 2
                with sp.Fori(0, NT) as t:
                    rows = bass.ds(t * P, P)
                    sp.wait_ge(m["x1"], CREDIT + t)
                    sp.dma_start(y[:, :], e.d_y[rows, :]).then_inc(s_in, 16)
                    sp.dma_start(x[:, :], e.x[0, rows, :]).then_inc(s_in, 16)
                    sp.wait_ge(s_sd, CREDIT + t)
                    hold(sp, e.sp_passed)
                    sp.dma_start(tok[:, :, :], e.c_tok[rows, :, :]).then_inc(s_tok, 16)
                    sp.wait_ge(m["h3"], CREDIT + t + 1)
                    sp.dma_start(e.d_h3[rows, :], h[:, :]).then_inc(s_st, 16)
                    sp.wait_ge(m["slot"], CREDIT + t + 1)
                    hold(sp, e.sp_passed)
                    sp.dma_start(e.d_gate[rows, :], g4[:, :]).then_inc(s_st, 16)
                    sp.wait_ge(m["x3"], CREDIT + t + 1)
                    sp.dma_start(e.d_x3[rows, :], x3[:, :]).then_inc(s_st, 16)
                sp.wait_ge(s_st, CREDIT + 48 * NT)

            @block.gpsimd
            def _(pool):
                give_credit(pool, e.sems)
                pool.memset(e.cnt[:, :], 0.0).then_inc(s_w, 16)
                pool.memset(eps[:, :], EPS).then_inc(s_w, 16)
                with pool.Fori(0, NT) as t:
                    pool.wait_ge(m["slot"], CREDIT + t + 1)
                    hold(pool, e.pool_passed)
                    pool.wait_ge(s_tok, CREDIT + 16 * t + 16)
                    hold(pool, e.pool_passed)
                    for k in range(TOPK):
                        pool.indirect_dma_start(out=e.d_tok, out_offset=bass.IndirectOffsetOnAxis(ap=slot[:, k:k + 1], axis=0),
                                                in_=tok[:, k, :], in_offset=None).then_inc(s_sc, 16)
                    pool.wait_ge(s_sc, 64 * t + 64)
                    pool.sem_inc(s_sd)

            @block.scalar
            def _(act):
                act.wait_ge(s_w, CREDIT + 16 * N_W)
                with act.Fori(0, NT) as t:
                    ch = Chain(act, s_ak, t, AK)
                    act.wait_ge(s_in, CREDIT + 32 * t + 32)
                    ch(act.activation(sq[:, 0:512], y[:, 0:512], ACT.Square, accum_out=st[:, 0:1]))
                    ch(act.activation(sq[:, 512:], y[:, 512:], ACT.Square, accum_out=st[:, 1:2]))
                    act.activation(st[:, 0:2], st[:, 0:2], ACT.Sqrt, bias=eps[:, 0:1], scale=1.0 / 512).then_inc(m["ssy"], 1)
                    act.wait_ge(m["x1"], CREDIT + t + 1)
                    ch(act.activation(sq[:, :], x1[:, :], ACT.Square, accum_out=st[:, 2:3]))
                    act.activation(st[:, 2:3], st[:, 2:3], ACT.Sqrt, bias=eps[:, 0:1], scale=1.0 / D).then_inc(m["ss1"], 1)
                    act.wait_ge(m["q"], CREDIT + t + 1)
                    act.activation(sq4[:, :], sq4[:, :], ACT.Sqrt, bias=eps[:, 0:1], scale=1.0 / MHD).then_inc(m["qn"], 1)
                    act.wait_ge(m["mx"], CREDIT + t + 1)
                    for j in range(MH):
                        act.activation(pr[:, j, :], ps[:, 4 + j % 2, (j // 2) * N_MEM:(j // 2 + 1) * N_MEM], ACT.Exp, bias=mx[:, j:j + 1],
                                       accum_out=rs[:, j:j + 1]).then_inc(m["p"], 1)
                    act.wait_ge(m["x2"], CREDIT + t + 1)
                    ch(act.activation(sq[:, :], x2[:, :], ACT.Square, accum_out=st[:, 3:4]))
                    act.activation(st[:, 3:4], st[:, 3:4], ACT.Sqrt, bias=eps[:, 0:1], scale=1.0 / D).then_inc(m["ss2"], 1)
                    act.wait_ge(m["gx"], CREDIT + t + 1)
                    act.activation(g4[:, :], m8[:, 0:TOPK], ACT.Exp, bias=gs[:, 0:1], accum_out=gs[:, 1:2]).then_inc(m["g4"], 1)
                    ch.end()

            @block.vector
            def _(dve):
                dve.wait_ge(s_w, CREDIT + 16 * N_W)
                with dve.Fori(0, NT) as t:
                    ch = Chain(dve, s_dv, t, DV)

                    def wait(name, k=1):
                        dve.wait_ge(m[name], CREDIT + k * t + k)

                    def turned(dst, src, gain):
                        d4 = dst.rearrange("p (c n) d -> p c n d", c=2)
                        s4 = src.rearrange("p c (n d) -> p c n d", d=P)
                        if gain is None:
                            return dve.tensor_copy(d4, s4)
                        return dve.tensor_tensor(d4, s4, bcast(gain.rearrange("p (c n) -> p c n", c=2).unsqueeze(3), [P, 2, 4, P]), ALU.mult)

                    wait("ssy")
                    ch(dve.reciprocal(st[:, 0:2], st[:, 0:2]))
                    dve.wait_ge(s_st, CREDIT + 48 * t)
                    dve.tensor_tensor(h[:, :].rearrange("p (c n) -> p c n", c=2), y[:, :].rearrange("p (c n) -> p c n", c=2),
                                      bcast(st[:, 0:2].unsqueeze(2), [P, 2, 512]), ALU.mult).then_inc(m["yn"], 1)
                    wait("yT")
                    turned(hT[:, :, :], ps[:, 0:2, :], g_o[:, :]).then_inc(m["yTd"], 1)
                    wait("o1")
                    dve.tensor_tensor(x1[:, :].rearrange("p (c n) -> p c n", c=2), ps[:, 2:4, :], x[:, :].rearrange("p (c n) -> p c n", c=2), ALU.add).then_inc(m["x1"], 1)
                    wait("ss1")
                    ch(dve.reciprocal(st[:, 2:3], st[:, 2:3]))
                    dve.tensor_scalar(h[:, :], x1[:, :], st[:, 2:3], None, ALU.mult).then_inc(m["h2"], 1)
                    wait("h2T")
                    turned(hT[:, :, :], ps[:, 0:2, :], g_m[:, :]).then_inc(m["h2Td"], 1)
                    wait("s0")
                    q2 = q[:, :, :]
                    ch(dve.tensor_copy(q2, ps[:, 2, 0:256].rearrange("p (h d) -> p h d", d=MHD)))
                    s2 = h[:, 0:256].rearrange("p (h d) -> p h d", d=MHD)
                    ch(dve.tensor_tensor(s2, q2, q2, ALU.mult))
                    dve.tensor_reduce(sq4[:, :], s2, AX.X, ALU.add).then_inc(m["q"], 1)
                    wait("qn")
                    ch(dve.reciprocal(sq4[:, :], sq4[:, :]))
                    ch(dve.tensor_scalar(sq4[:, :], sq4[:, :], MHD ** -0.5, None, ALU.mult))
                    ch(dve.tensor_tensor(q2, q2, bcast(sq4[:, :].unsqueeze(2), [P, MH, MHD]), ALU.mult))
                    dve.tensor_tensor(q2, q2, bcast(g_q[:, :].unsqueeze(1), [P, MH, MHD]), ALU.mult).then_inc(m["qd"], 1)
                    wait("qT")
                    dve.tensor_copy(qT[:, :, :], ps[:, 3, 0:256].rearrange("p (j n) -> p j n", n=P)).then_inc(m["qTd"], 1)
                    wait("s")
                    ch(dve.tensor_reduce(mx[:, :].rearrange("p (j c) -> p c j", c=2), ps[:, 4:6, :].rearrange("p c (j n) -> p c j n", n=N_MEM), AX.X, ALU.max))
                    dve.tensor_scalar(mx[:, :], mx[:, :], -1.0, None, ALU.mult).then_inc(m["mx"], 1)
                    wait("pT")
                    turned(pT[:, :, :], ps[:, 6:8, :], None).then_inc(m["pTc"], 1)
                    ch(dve.reciprocal(rs[:, :], rs[:, :]))
                    wait("O")
                    dve.tensor_tensor(o[:, :, :], ps[:, 0, 0:256].rearrange("p (h d) -> p h d", d=MHD), bcast(rs[:, :].unsqueeze(2), [P, MH, MHD]), ALU.mult).then_inc(m["on"], 1)
                    wait("oT")
                    dve.tensor_copy(oT[:, :, :], ps[:, 1, 0:256].rearrange("p (j n) -> p j n", n=P)).then_inc(m["oTd"], 1)
                    wait("mo")
                    dve.tensor_tensor(x2[:, :].rearrange("p (c n) -> p c n", c=2), ps[:, 2:4, :], x1[:, :].rearrange("p (c n) -> p c n", c=2), ALU.add).then_inc(m["x2"], 1)
                    wait("ss2")
                    ch(dve.reciprocal(st[:, 3:4], st[:, 3:4]))
                    dve.scalar_tensor_tensor(h[:, :], x2[:, :], st[:, 3:4], g_e[:, :], ALU.mult, ALU.mult).then_inc(m["h3"], 1)
                    wait("h3T")
                    turned(hT[:, :, :], ps[:, 0:2, :], None).then_inc(m["h3Td"], 1)
                    wait("lg")
                    ch(dve.tensor_tensor(lg[:, :], ps[:, 2, 0:NE], rb[:, :], ALU.add))
                    hold(dve, e.dve_passed)
                    ch(dve.max(m8[:, :], lg[:, :]))
                    hold(dve, e.dve_passed)
                    ch(dve.max_index(i8[:, :], m8[:, :], lg[:, :]))
                    dve.tensor_scalar(gs[:, 0:1], m8[:, 0:1], -1.0, None, ALU.mult).then_inc(m["gx"], 1)
                    ch(dve.tensor_copy(i8f[:, :], i8[:, :]))
                    ch(dve.tensor_tensor(hot[:, :, :], bcast(iota[:, :].unsqueeze(1), [P, TOPK, NE]), bcast(i8f[:, 0:TOPK].unsqueeze(2), [P, TOPK, NE]), ALU.is_equal))
                    ch(dve.tensor_reduce(mask[:, :], hot[:, :, :].rearrange("p k e -> p e k"), AX.X, ALU.add))
                    wait("g4")
                    ch(dve.reciprocal(gs[:, 1:2], gs[:, 1:2]))
                    ch(dve.tensor_scalar(g4[:, :], g4[:, :], gs[:, 1:2], None, ALU.mult))
                    ch(dve.tensor_tensor(tmp[:, :, :], hot[:, :, :], bcast(g4[:, :].unsqueeze(2), [P, TOPK, NE]), ALU.mult))
                    dve.tensor_reduce(gm[:, :], tmp[:, :, :].rearrange("p k e -> p e k"), AX.X, ALU.add).then_inc(m["msk"], 1)
                    wait("rk")
                    ch(dve.tensor_tensor(where[:, :], ps[:, 3, 0:NE], e.cnt[:, :], ALU.add))
                    ch(dve.tensor_tensor(where[:, :], where[:, :], ebase[:, :], ALU.add))
                    dve.tensor_copy(gmT[:, :], ps[0:NE, 4, 0:P]).then_inc(m["gmT"], 1)
                    ch(dve.tensor_tensor(tmp[:, :, :], hot[:, :, :], bcast(where[:, :].unsqueeze(1), [P, TOPK, NE]), ALU.mult))
                    ch(dve.tensor_reduce(slf[:, :], tmp[:, :, :], AX.X, ALU.add))
                    dve.wait_ge(s_sd, CREDIT + t)
                    dve.tensor_copy(slot[:, :], slf[:, :]).then_inc(m["slot"], 1)
                    ch(dve.tensor_tensor(e.cnt[:, :], e.cnt[:, :], ps[:, 3, NE:2 * NE], ALU.add))
                    wait("bd")
                    dve.tensor_tensor(x3[:, :].rearrange("p (c n) -> p c n", c=2), ps[:, 0:2, :], x2[:, :].rearrange("p (c n) -> p c n", c=2), ALU.add).then_inc(m["x3"], 1)
                    ch.end()

            @block.tensor
            def _(pe):
                pe.wait_ge(s_w, CREDIT + 16 * N_W)
                with pe.Fori(0, NT) as t:
                    def wait(name, k=1):
                        pe.wait_ge(m[name], CREDIT + k * t + k)

                    def turn(src, bank):
                        for k in range(KD):
                            mm = pe.transpose(ps[:, bank + k // 4, (k % 4) * P:(k % 4 + 1) * P], src[:, k * P:(k + 1) * P], ident[:, :])
                        return mm

                    def project(w, cols, bank, n=KD, src=hT):
                        for c in range(0, cols, 512):
                            for k in range(n):
                                mm = pe.matmul(ps[:, bank + c // 512, 0:min(512, cols - c)], src[:, k, :], w[:, k, c:min(cols, c + 512)], start=(k == 0), stop=(k == n - 1))
                        return mm

                    wait("yn")
                    pe.wait_ge(m["x3"], CREDIT + t)
                    turn(h, 0).then_inc(m["yT"], 1)
                    wait("yTd")
                    project(w_out, D, 2).then_inc(m["o1"], 1)
                    wait("h2")
                    turn(h, 0).then_inc(m["h2T"], 1)
                    wait("h2Td")
                    wait("x1")
                    project(w_mq, MH * MHD, 2).then_inc(m["s0"], 1)
                    wait("qd")
                    for j in range(2):
                        mm = pe.transpose(ps[:, 3, j * P:(j + 1) * P], q[:, 2 * j:2 * j + 2, :].rearrange("p h d -> p (h d)"), ident[:, :])
                    mm.then_inc(m["qT"], 1)
                    wait("qTd")
                    hold(pe, e.pe_passed)
                    for j in range(MH):
                        r = slice(MHD * (j % 2), MHD * (j % 2 + 1))
                        mm = pe.matmul(ps[:, 4 + j % 2, (j // 2) * N_MEM:(j // 2 + 1) * N_MEM], qT[r, j // 2, :], e.kTm[r, j // 2, :], start=True, stop=True)
                    mm.then_inc(m["s"], 1)
                    wait("p", MH)
                    for j in range(2 * MH):
                        mm = pe.transpose(ps[:, 6 + j // 4, (j % 4) * P:(j % 4 + 1) * P], pr[:, j // 2, (j % 2) * P:(j % 2 + 1) * P], ident[:, :])
                    mm.then_inc(m["pT"], 1)
                    wait("pTc")
                    for j in range(2 * MH):
                        mm = pe.matmul(ps[:, 0, (j // 2) * MHD:(j // 2 + 1) * MHD], pT[:, j, :], e.vmem[:, j % 2, j // 2, :], start=(j % 2 == 0), stop=(j % 2 == 1))
                    mm.then_inc(m["O"], 1)
                    wait("on")
                    for j in range(2):
                        mm = pe.transpose(ps[:, 1, j * P:(j + 1) * P], o[:, 2 * j:2 * j + 2, :].rearrange("p h d -> p (h d)"), ident[:, :])
                    mm.then_inc(m["oT"], 1)
                    wait("oTd")
                    project(w_mo, D, 2, n=2, src=oT).then_inc(m["mo"], 1)
                    wait("h3")
                    turn(h, 0).then_inc(m["h3T"], 1)
                    wait("h3Td")
                    project(rw, NE, 2).then_inc(m["lg"], 1)
                    wait("msk")
                    pe.matmul(ps[:, 3, 0:NE], before[:, :], mask[:, :], start=True, stop=True)
                    pe.matmul(ps[:, 3, NE:2 * NE], ones[:, :], mask[:, :], start=True, stop=True)
                    pe.transpose(ps[0:NE, 4, 0:P], gm[:, :], ident[:, :]).then_inc(m["rk"], 1)
                    wait("gmT")
                    for c in range(2):
                        mm = pe.matmul(ps[:, c, :], gmT[:, :], bdown[:, c * 512:(c + 1) * 512], start=True, stop=True)
                    mm.then_inc(m["bd"], 1)


def stage_plan(nc, e):
    with ExitStack() as ctx:
        sb, sem, ps = add_tools(nc, e, ctx)
        iota, pidx, ones = sb("iota_p", [P, NE]), sb("pidx", [P, 1]), sb("ones_p", [P, NE])
        a, npas, ends, done, eq = (sb(n, [P, NE]) for n in ("a", "npas", "ends", "donep", "eq"))
        r = sb("r", [P, 8])
        plan = sb("plan_f", [P, 4], I32)
        s_in, s_dv, s_out = sem("p_in"), sem("p_dve"), sem("p_out")
        with nc.Block() as block:
            @block.gpsimd
            def _(pool):
                give_credit(pool, e.sems)

            @block.sync
            def _(sp):
                sp.dma_start(iota[:, :], e.c_iota.partition_broadcast(P)).then_inc(s_in, 16)
                sp.dma_start(pidx[:, :], e.c_pidx).then_inc(s_in, 16)
                sp.wait_ge(s_dv, CREDIT + 25)
                sp.dma_start(e.d_plan.rearrange("(p n) -> p n", n=4), plan[:, :]).then_inc(s_out, 16)
                sp.wait_ge(s_out, CREDIT + 16)
                sp.dma_start(e.plan[:, :], e.d_plan.rearrange("(o n) -> o n", o=1)).then_inc(s_out, 16)
                sp.wait_ge(s_out, CREDIT + 32)

            @block.vector
            def _(dve):
                n = [0]

                def step(ins):
                    ins.then_inc(s_dv, 1)
                    n[0] += 1
                    dve.wait_ge(s_dv, CREDIT + n[0])

                cnt = e.cnt
                dve.wait_ge(s_in, CREDIT + 32)
                step(dve.memset(ones[:, :], 1.0))
                step(dve.memset(r[:, :], 0.0))
                step(dve.tensor_scalar(npas[:, :], cnt[:, :], 0.0, None, ALU.is_gt))
                for k in range(1, CAP // PASS):
                    step(dve.tensor_scalar(a[:, :], cnt[:, :], float(k * PASS), None, ALU.is_gt))
                    step(dve.tensor_tensor(npas[:, :], npas[:, :], a[:, :], ALU.add))
                step(dve.tensor_tensor_scan(ends[:, :], ones[:, :], npas[:, :], 0.0, ALU.mult, ALU.add))
                step(dve.tensor_scalar(done[:, :], ends[:, :], pidx[:, 0:1], None, ALU.is_le))
                step(dve.tensor_reduce(r[:, 0:1], done[:, :], AX.X, ALU.add))
                step(dve.tensor_tensor(a[:, :], done[:, :], npas[:, :], ALU.mult))
                step(dve.tensor_reduce(r[:, 1:2], a[:, :], AX.X, ALU.add))
                step(dve.tensor_tensor(r[:, 2:3], pidx[:, :], r[:, 1:2], ALU.subtract))
                step(dve.tensor_scalar(r[:, 2:3], r[:, 2:3], float(PASS), None, ALU.mult))
                step(dve.tensor_scalar(eq[:, :], iota[:, :], r[:, 0:1], None, ALU.is_equal))
                step(dve.tensor_tensor(a[:, :], eq[:, :], cnt[:, :], ALU.mult))
                step(dve.tensor_reduce(r[:, 3:4], a[:, :], AX.X, ALU.add))
                step(dve.tensor_tensor(r[:, 6:7], r[:, 3:4], r[:, 2:3], ALU.subtract))
                step(dve.tensor_scalar(r[:, 6:7], r[:, 6:7], 0.0, None, ALU.max))
                step(dve.tensor_scalar(r[:, 4:5], r[:, 0:1], float(NE - 1), None, ALU.min))
                step(dve.scalar_tensor_tensor(r[:, 5:6], r[:, 4:5], float(CAP), r[:, 2:3], ALU.mult, ALU.add))
                step(dve.tensor_scalar(r[:, 5:6], r[:, 5:6], float(NE * CAP - PASS), None, ALU.min))
                step(dve.tensor_copy(plan[:, :], r[:, 4:8]))


def stage_experts(nc, e):
    with ExitStack() as ctx:
        sb, sem, ps = add_tools(nc, e, ctx)
        NCH = 4
        JD = FF // P
        ident = sb("ident_e", [P, P])
        wg = sb("wg", [P, NCH, KD, 512])
        wd = sb("wd", [P, NCH, 2, D])
        src, dst = sb("src", [P, 2, 2], U32), sb("dst", [P, 2, 2], U32)
        xg, xT = sb("xg", [P, 2, D]), sb("xT_e", [P, KD, PASS])
        bias = sb("bias", [P, 16])
        gg, ss, uu = (sb(n, [P, 2, PASS]) for n in ("gg", "ss", "uu"))
        aT = sb("aT", [P, JD, PASS])
        ys = sb("ys_e", [P, 2, D])
        s_id, s_src, s_dst, s_xT, s_xTc, s_xset = (sem("e_" + n) for n in
            ("ident", "source_rows", "target_rows", "rowsT", "rowsT_copied", "rows_set"))
        s_x, s_st = e.dma_sem("e_rows"), e.dma_sem("e_stored")
        s_wg = [sem(f"e_wg{c}") for c in range(NCH)]
        s_wd = [sem(f"e_wd{c}") for c in range(NCH)]
        s_gu, s_g, s_sig, s_a, s_down, s_y, s_sd, s_dch = (sem("e_" + n) for n in
            ("gate_up", "gate", "sigmoid", "act", "down", "y", "scatter_done", "dve_chain"))

        def rows_left(eng, i):
            return eng.value_load(e.plan[0:1, bass.ds(4 * i + 2, 1)], min_val=0, max_val=CAP)

        def expert(eng, i):
            return eng.value_load(e.plan[0:1, bass.ds(4 * i, 1)], min_val=0, max_val=NE - 1)

        def first_slot(eng, i):
            return eng.value_load(e.plan[0:1, bass.ds(4 * i + 1, 1)], min_val=0, max_val=NE * CAP - PASS)

        def by_size(eng, n, body):
            with eng.If(n > P):
                with eng.If(n > P + P // 2):
                    body(2 * P, 2)
                with eng.Else():
                    body(P + P // 2, 2)
            with eng.Else():
                body(P, 1)

        with nc.Block() as block:
            @block.sync
            def _(sp):
                sp.dma_start(ident[:, :], e.c_ident).then_inc(s_id, 16)
                with sp.Fori(0, NPASS) as i:
                    n = rows_left(sp, i)
                    ex = expert(sp, i)
                    with sp.If(n > 0):
                        one = bass.ds(ex, 1)
                        for c in range(NCH):
                            sp.wait_ge(s_gu, CREDIT + JD * i + 2 * (c + 1) - JD)
                            hold(sp, e.sp_passed)
                            sp.dma_start(wg[:, c, :, :], e.w_gate_up[0][one, :, c * 512:(c + 1) * 512].rearrange("o (k p) n -> p (o k) n", p=P)).then_inc(s_wg[c], 16)
                        for c in range(NCH):
                            sp.wait_ge(s_down, CREDIT + NCH * i + c + 1 - NCH)
                            hold(sp, e.sp_passed)
                            sp.dma_start(wd[:, c, :, :], e.w_down[0][one, c * 256:(c + 1) * 256, :].rearrange("o (k p) n -> p (o k) n", p=P)).then_inc(s_wd[c], 16)

            @block.gpsimd
            def _(pool):
                give_credit(pool, e.sems)

                def gather(i):
                    pool.wait_ge(s_src, CREDIT + 16 * i + 16)
                    hold(pool, e.pool_passed)
                    pool.wait_ge(s_xT, CREDIT + 4 * i)
                    hold(pool, e.pool_passed)
                    for b in range(2):
                        pool.indirect_dma_start(out=xg[:, b, :], out_offset=None, in_=e.d_h3, bounds_check=S - 1, oob_is_err=False,
                                                in_offset=bass.IndirectOffsetOnAxis(ap=src[:, b, 0:1], axis=0)).then_inc(s_x, 16)

                pool.memset(xg[:, :, :], 0.0).then_inc(s_xset, 1)
                pool.wait_ge(s_xset, CREDIT + 2)
                gather(0)
                with pool.Fori(0, NPASS) as i:
                    n = rows_left(pool, i)
                    with pool.If(n > 0):
                        gather(i + 1)
                        pool.wait_ge(s_dst, CREDIT + 16 * i + 16)
                        hold(pool, e.pool_passed)

                        def scatter(nb):
                            for b in range(nb):
                                pool.wait_ge(s_y, CREDIT + 2 * i + 1 + b)
                                hold(pool, e.pool_passed)
                                pool.indirect_dma_start(out=e.d_ys, out_offset=bass.IndirectOffsetOnAxis(ap=dst[:, b, 1:2], axis=0),
                                                        in_=ys[:, b, :], in_offset=None, bounds_check=S * TOPK - 1, oob_is_err=False).then_inc(s_st, 16)
                        scatter(2)
                        pool.wait_ge(s_st, 32 * i + 32)
                        pool.sem_inc(s_sd)

            @block.scalar
            def _(act):
                def sources(i, slot):
                    act.dma_start(src[:, :, :], e.d_tok[bass.ds(slot, PASS), :].rearrange("(b p) o -> p b o", p=P)).then_inc(s_src, 16)

                def copy_rows(i):
                    for k in range(4):
                        act.wait_ge(s_xT, CREDIT + 4 * i + k + 1)
                        act.wait_ge(s_gu, CREDIT + JD * i)
                        act.activation(xT[:, 2 * k:2 * k + 2, :], ps[:, 6 + k % 2, :].rearrange("p (k n) -> p k n", k=2), ACT.Copy).then_inc(s_xTc, 1)

                with nc.allow_non_contiguous_dma("row numbers"):
                    sources(0, first_slot(act, 0))
                    copy_rows(0)
                    with act.Fori(0, NPASS) as i:
                        n = rows_left(act, i)
                        with act.If(n > 0):
                            act.wait_ge(s_x, 32 * i + 32)
                            hold(act, e.act_passed)
                            sources(i + 1, first_slot(act, i + 1))
                            act.wait_ge(s_sd, CREDIT + i)
                            hold(act, e.act_passed)
                            slot = first_slot(act, i)
                            act.dma_start(dst[:, :, :], e.d_tok[bass.ds(slot, PASS), :].rearrange("(b p) o -> p b o", p=P)).then_inc(s_dst, 16)

                            def sigmoids(w, nb):
                                for j in range(JD):
                                    act.wait_ge(s_g, CREDIT + JD * i + j + 1)
                                    act.activation(ss[:, j % 2, 0:w], gg[:, j % 2, 0:w], ACT.Sigmoid, scale=ALPHA).then_inc(s_sig, 1)
                            by_size(act, n, sigmoids)
                            copy_rows(i + 1)

            @block.vector
            def _(dve):
                dve.memset(aT[:, :, :], 0.0).then_inc(s_xset, 1)
                dve.wait_ge(s_xset, CREDIT + 2)
                with dve.Fori(0, NPASS) as i:
                    n = rows_left(dve, i)
                    ex = expert(dve, i)
                    with dve.If(n > 0):
                        dve.wait_ge(s_a, CREDIT + JD * i)
                        hold(dve, e.dve_passed)
                        Chain(dve, s_dch, i, 1 + 3 * JD)(dve.tensor_copy(bias[:, :], e.bgT[:, :, bass.ds(ex, 1)].rearrange("p j o -> p (j o)")))
                        hold(dve, e.dve_passed)

                        def body(w, nb):
                            ch = Chain(dve, s_dch, i, 1 + 3 * JD)
                            ch.n = 1
                            for j in range(JD):
                                g, u, s = gg[:, j % 2, 0:w], uu[:, j % 2, 0:w], ss[:, j % 2, 0:w]
                                dve.wait_ge(s_gu, CREDIT + JD * i + j + 1)
                                dve.tensor_scalar(g, ps[:, j % 2, 0:w], bias[:, j:j + 1], LIMIT, ALU.add, ALU.min).then_inc(s_g, 1)
                                ch(dve.tensor_scalar(u, ps[:, j % 2, PASS:PASS + w], bias[:, 8 + j:9 + j], LIMIT, ALU.add, ALU.min))
                                ch(dve.tensor_scalar(u, u, -LIMIT, 1.0, ALU.max, ALU.add))
                                ch(dve.tensor_tensor(u, u, g, ALU.mult))
                                dve.wait_ge(s_sig, CREDIT + JD * i + j + 1)
                                if j == 0:
                                    dve.wait_ge(s_down, CREDIT + NCH * i)
                                dve.tensor_tensor(aT[:, j, 0:w], u, s, ALU.mult).then_inc(s_a, 1)
                            ch.end()
                            dve.wait_ge(s_sd, CREDIT + i)
                            for b in range(2):
                                if b < nb:
                                    dve.wait_ge(s_down, CREDIT + NCH * i + NCH)
                                    dve.tensor_copy(ys[:, b, :].rearrange("p (c n) -> p c n", c=2), ps[:, 2 + 2 * b:4 + 2 * b, :]).then_inc(s_y, 1)
                                else:
                                    dve.memset(ys[:, b, :], 0.0).then_inc(s_y, 1)
                        by_size(dve, n, body)

            @block.tensor
            def _(pe):
                def turn_rows(i):
                    pe.wait_ge(s_x, 32 * i + 32)
                    for k in range(4):
                        pe.wait_ge(s_xTc, CREDIT + 4 * i + max(k - 1, 0))
                        for kk in range(2):
                            for b in range(2):
                                c = 2 * k + kk
                                mm = pe.transpose(ps[:, 6 + k % 2, kk * PASS + b * P:kk * PASS + (b + 1) * P], xg[:, b, c * P:(c + 1) * P], ident[:, :])
                        mm.then_inc(s_xT, 1)

                pe.wait_ge(s_id, CREDIT + 16)
                turn_rows(0)
                with pe.Fori(0, NPASS) as i:
                    n = rows_left(pe, i)
                    with pe.If(n > 0):
                        def body(w, nb):
                            pe.wait_ge(s_xTc, CREDIT + 4 * i + 4)
                            for j in range(JD):
                                if j % 2 == 0:
                                    pe.wait_ge(s_wg[j // 2], CREDIT + 16 * i + 16)
                                pe.wait_ge(s_a, CREDIT + JD * i + j - 1)
                                for half in range(2):
                                    c0 = 256 * (j % 2) + half
                                    for k in range(KD):
                                        mm = pe.matmul(ps[:, j % 2, half * PASS:half * PASS + w], wg[:, j // 2, k, c0:c0 + 255:2], xT[:, k, 0:w],
                                                       start=(k == 0), stop=(k == KD - 1))
                                mm.then_inc(s_gu, 1)
                            turn_rows(i + 1)
                            pe.wait_ge(s_a, CREDIT + JD * i + JD)
                            pe.wait_ge(s_y, CREDIT + 2 * i)
                            for c in range(NCH):
                                pe.wait_ge(s_wd[c], CREDIT + 16 * i + 16)
                                for b in range(nb):
                                    for h in range(2):
                                        for j in (2 * c, 2 * c + 1):
                                            mm = pe.matmul(ps[:, 2 + 2 * b + h, :], aT[:, j, b * P:(b + 1) * P], wd[:, c, j % 2, h * 512:(h + 1) * 512],
                                                           start=(j == 0), stop=(j == JD - 1))
                                mm.then_inc(s_down, 1)
                        by_size(pe, n, body)


def stage_combine(nc, e):
    with ExitStack() as ctx:
        sb, sem, ps = add_tools(nc, e, ctx)
        x3 = sb("x3_f", [P, 2, D])
        gate = sb("gate_f", [P, 2, TOPK])
        yr = sb("yr", [P, 2, TOPK, D])
        s_in, s_dv, s_out = ([sem(f"f_{n}{b}") for b in range(2)] for n in ("in", "sum", "stored"))
        with nc.Block() as block:
            @block.gpsimd
            def _(pool):
                give_credit(pool, e.sems)

            @block.sync
            def _(sp):
                with sp.Fori(0, NT // 2) as t:
                    for b in range(2):
                        rows = bass.ds((2 * t + b) * P, P)
                        sp.wait_ge(s_out[b], CREDIT + 16 * t)
                        sp.dma_start(yr[:, b, :, :], e.d_ys[bass.ds((2 * t + b) * P * TOPK, P * TOPK), :].rearrange("(p k) n -> p k n", k=TOPK)).then_inc(s_in[b], 16)
                        sp.dma_start(gate[:, b, :], e.d_gate[rows, :]).then_inc(s_in[b], 16)
                        sp.dma_start(x3[:, b, :], e.d_x3[rows, :]).then_inc(s_in[b], 16)

            @block.scalar
            def _(act):
                with act.Fori(0, NT // 2) as t:
                    for b in range(2):
                        act.wait_ge(s_dv[b], CREDIT + TOPK * t + TOPK)
                        act.dma_start(e.out[0, bass.ds((2 * t + b) * P, P), :], x3[:, b, :]).then_inc(s_out[b], 16)
                for b in range(2):
                    act.wait_ge(s_out[b], CREDIT + 16 * (NT // 2))

            @block.vector
            def _(dve):
                with dve.Fori(0, NT // 2) as t:
                    for b in range(2):
                        dve.wait_ge(s_in[b], CREDIT + 48 * t + 48)
                        for k in range(TOPK):
                            if k:
                                dve.wait_ge(s_dv[b], CREDIT + TOPK * t + k)
                            dve.scalar_tensor_tensor(x3[:, b, :], yr[:, b, k, :], gate[:, b, k:k + 1], x3[:, b, :], ALU.mult, ALU.add).then_inc(s_dv[b], 1)


def program(nc, e):
    with ExitStack() as ctx:
        keep = lambda n, s, d=F32: ctx.enter_context(nc.sbuf_tensor(n, s, d))
        e.bgT = keep("bgT", [P, 16, NE])
        e.kTm = keep("kTm", [P, 2, N_MEM])
        e.vmem = keep("vmem", [P, N_MEM // P, MH, MHD])
        e.cnt = keep("cnt", [P, NE])
        e.plan = keep("plan", [1, 4 * P], I32)
        e.pe_passed, e.act_passed, e.dve_passed, e.pool_passed, e.sp_passed = (
            ctx.enter_context(nc.semaphore(eng + "_passed")) for eng in ("pe", "act", "dve", "pool", "sp"))
        d = lambda n, s, t=F32: nc.dram_tensor(n, s, t, kind="Internal").ap()
        e.d_rev = d("d_rev", [2, HN + 1, REV])
        e.d_strip, e.d_wstrip = d("d_strip", [HN + 1, P, S]), d("d_wstrip", [HN + 1, P, WIN + P])
        e.d_qm, e.d_km, e.d_vm = d("d_qm", [HM, QK, S]), d("d_km", [HM, QK, S]), d("d_vm", [HM, S, VD])
        e.d_qn_flat = d("d_qn", [HN, HD, S])
        e.d_qn = [e.d_qn_flat[p::2] for p in range(2)]
        e.d_kn, e.d_cn = d("d_kn", [2, G * HD, S]), d("d_cn", [2, G * HD, S])
        e.d_vn = [d("d_vs", [G, S, HD]), d("d_vw", [G, S, HD])]
        e.d_gt = d("d_gt", [HN, S, 3])
        e.d_ck, e.d_cv = d("d_ck", [G, HD, NCMP]), d("d_cv", [G, NCMP, HD])
        e.d_y, e.d_h3, e.d_x3 = d("d_y", [S, D]), d("d_h3", [S, D]), d("d_x3", [S, D])
        e.d_gate = d("d_gate", [S, TOPK])
        e.d_tok, e.d_ys, e.d_plan = d("d_tok", [NE * CAP, 2], U32), d("d_ys", [S * TOPK, D]), d("d_plan", [4 * P], I32)
        e.skew_view = lambda k, h: bass.AP(e.d_rev.tensor, h * REV + k * (HN + 1) * REV, [[1, P], [1, S]])
        stage_setup(nc, e)
        stage_memory(nc, e)
        stage_project(nc, e)
        stage_compress(nc, e)
        stage_attend(nc, e)
        stage_mix(nc, e)
        stage_plan(nc, e)
        stage_experts(nc, e)
        stage_combine(nc, e)


def shape_constants():
    dist = (S - 1) - np.arange(REV)
    n = np.maximum(dist, 0)
    nf = np.maximum(n, 1).astype(np.float32)
    large = MAX_EXACT + (np.log(nf / MAX_EXACT) / np.log(MAX_DIST / MAX_EXACT) * (BUCKETS - MAX_EXACT)).astype(np.int32)
    bucket = np.where(n < MAX_EXACT, n, np.minimum(large, BUCKETS - 1))
    neg = np.where(dist < 0, NEG, 0.0).astype(np.float32)
    negw = np.where((dist < 0) | (dist >= WIN), NEG, 0.0).astype(np.float32)
    half = ROPE // 2
    inv = (np.float32(10000.0) ** (-np.arange(half, dtype=np.float32) / half)).astype(np.float32)
    ang = np.arange(S, dtype=np.float32)[:, None] * inv
    f = lambda a: np.ascontiguousarray(a, dtype=np.float32)
    return {
        "c_onehot": f(bucket[None, :] == np.arange(BUCKETS)[:, None]),
        "c_negrow": f(np.tile(neg, (HN + 1, 1))),
        "c_negwin": f(np.tile(negw, (HN + 1, 1))),
        "c_flip": f(np.eye(P)[::-1]),
        "c_ident": f(np.eye(P)),
        "c_before": f(np.triu(np.ones((P, P)), 1)),
        "c_ones": f(np.ones((P, P))),
        "c_trig": f(np.concatenate([np.cos(ang), np.sin(ang)], axis=1)),
        "c_inv_d": f([1 / QR, 1 / KVR] + [1 / HD] * 12),
        "c_post": f([1.0, 1.0] + [HD ** -0.5] * 8 + [1.0] * 4),
        "c_post2": f([QK ** -0.5] * HM + [1.0] * HM),
        "c_cvalid": f((np.arange(P) >= CMP_LEN - 1)[:, None]),
        "c_iota": f(np.arange(NE)),
        "c_ebase": f(np.arange(NE) * CAP),
        "c_pidx": f(np.arange(P)[:, None]),
        "c_tok": np.stack([np.repeat(np.arange(S), TOPK), np.arange(S * TOPK)], 1).reshape(S, TOPK, 2).astype(np.uint32),
    }


def kernel(**inputs):
    import concourse.bacc as bacc
    from concourse.bass_utils import run_bass_kernel_spmd as run

    nc = bacc.Bacc("TRN2", target_bir_lowering=False, num_devices=1)
    arrays = {name: np.ascontiguousarray(a) for name, a in inputs.items()}
    arrays.update(shape_constants())
    dram = {name: nc.dram_tensor("in_" + name, a.shape, mybir.dt.from_np(a.dtype), kind="ExternalInput").ap()
            for name, a in arrays.items()}
    e = Env()
    e.x, e.mem, e.g_attn_norm, e.w_in, e.g_cq, e.w_uq = (dram[n] for n in 'x mem g_attn_norm w_in g_cq w_uq'.split())
    e.g_ckv, e.w_ukv, e.g_q_mla, e.g_k_mla, e.cmp_k_pos, e.cmp_k_w1 = (dram[n] for n in 'g_ckv w_ukv g_q_mla g_k_mla cmp_k_pos cmp_k_w1'.split())
    e.cmp_k_w2, e.cmp_v_pos, e.cmp_v_w1, e.cmp_v_w2, e.g_q_nsa, e.g_k_nsa = (dram[n] for n in 'cmp_k_w2 cmp_v_pos cmp_v_w1 cmp_v_w2 g_q_nsa g_k_nsa'.split())
    e.rel_table, e.g_out_mla, e.g_out_nsa, e.w_out, e.g_mem_norm, e.g_mem_src = (dram[n] for n in 'rel_table g_out_mla g_out_nsa w_out g_mem_norm g_mem_src'.split())
    e.w_mq, e.w_mkv, e.g_mq, e.g_mk, e.w_mo, e.g_moe_norm = (dram[n] for n in 'w_mq w_mkv g_mq g_mk w_mo g_moe_norm'.split())
    e.router_w, e.router_b, e.w_gate_up, e.b_gate_up, e.w_down, e.b_down = (dram[n] for n in 'router_w router_b w_gate_up b_gate_up w_down b_down'.split())
    e.c_onehot, e.c_negrow, e.c_negwin, e.c_flip, e.c_ident, e.c_before = (dram[n] for n in 'c_onehot c_negrow c_negwin c_flip c_ident c_before'.split())
    e.c_ones, e.c_trig, e.c_inv_d, e.c_post, e.c_post2, e.c_cvalid = (dram[n] for n in 'c_ones c_trig c_inv_d c_post c_post2 c_cvalid'.split())
    e.c_iota, e.c_ebase, e.c_pidx, e.c_tok = (dram[n] for n in 'c_iota c_ebase c_pidx c_tok'.split())
    e.out = nc.dram_tensor("out_0", (1, S, D), F32, kind="ExternalOutput").ap()
    program(nc, e)
    r = run(nc, [{"in_" + name: a for name, a in arrays.items()}], core_ids=[0])
    return r.results[0]["out_0"]
```

```python
from contextlib import ExitStack

import numpy as np
import concourse.bass as bass
from concourse import mybir

F32 = mybir.dt.float32
U32 = mybir.dt.uint32
I32 = mybir.dt.int32
ALU = mybir.AluOpType
ACT = mybir.ActivationFunctionType
AX = mybir.AxisListType

P = 128
D = 1024
S = 1024
NT = S // P
KD = D // P
EPS = 1e-6
NEG = -1e30

HM, NOPE, ROPE, VD = 8, 64, 32, 64
QK = NOPE + ROPE
QR, KVR = 256, 128
HN, G, HD = 8, 2, 64
HPG = HN // G
CMP_LEN, CMP_STRIDE, CMP_HID = 32, 16, 128
NCMP = (S - CMP_LEN) // CMP_STRIDE + 1
WIN = 512
BUCKETS, MAX_EXACT, MAX_DIST = 32, 16, 512
N_MEM, MH, MHD = 256, 4, 64
NE, TOPK, FF = 32, 4, 1024
LIMIT, ALPHA = 7.0, 1.702
IN_COLS = 1720
PCH = 430
C_CQ, C_CKV, C_KR, C_Q = 0, 256, 384, 416
C_KC, C_VC, C_KS, C_VS, C_KW, C_VW, C_GT = 928, 1056, 1184, 1312, 1440, 1568, 1696
REV = S + P
PASS = 256
NPASS = NE + (S * TOPK - NE) // PASS
NOBODY = 1 << 20
CAP = S


CREDIT = 8


def give_credit(eng, sems):
    for s in sems:
        eng.sem_inc(s, CREDIT)


class Chain:

    def __init__(self, eng, sem, turn=0, per=0):
        self.eng, self.sem, self.base, self.per, self.n = eng, sem, turn * per, per, 0

    def __call__(self, ins):
        ins.then_inc(self.sem, 1)
        self.n += 1
        self.eng.wait_ge(self.sem, CREDIT + self.base + self.n)

    def end(self):
        assert self.n == self.per, (self.n, self.per)


def bcast(ap, shape):
    return ap.to_broadcast(shape)


def hold(eng, sem):
    eng.sem_inc(sem)


class Env:
    pass


def add_tools(nc, e, ctx):
    e.sb = lambda n, s, d=F32: ctx.enter_context(nc.sbuf_tensor(n, s, d))
    e.sems = []

    def sem(name):
        e.sems.append(ctx.enter_context(nc.semaphore(name)))
        return e.sems[-1]

    e.dma_sem = lambda name: ctx.enter_context(nc.semaphore(name))

    e.sem = sem
    e.ps = ctx.enter_context(nc.psum_tensor("ps" + str(nc.next_id()), [P, 8, 512], F32))
    return e.sb, e.sem, e.ps


def stage_setup(nc, e):
    with ExitStack() as ctx:
        sb, sem, ps = add_tools(nc, e, ctx)
        onehot = sb("onehot", [BUCKETS, REV])
        negrow = sb("negrow", [HN + 1, REV])
        negwin = sb("negwin", [HN + 1, REV])
        table = sb("table", [BUCKETS, HN + 1])
        rev = sb("rev", [HN + 1, 2, REV])
        flip = sb("flip", [P, P])
        skew = sb("skew", [P, 2, S])
        strip = sb("strip", [P, 2, S])
        bgu = sb("bgu", [NE, 2 * FF])
        ident = sb("ident_s", [P, P])
        s_in, s_tab, s_rows, s_rowsum = sem("u_in"), sem("u_table"), sem("u_rows"), sem("u_row_done")
        s_out, s_skew, s_flip, s_strip, s_stored = sem("u_rev_stored"), sem("u_skew"), sem("u_flip"), sem("u_strip"), sem("u_stored")
        with nc.Block() as block:
            @block.gpsimd
            def _(pool):
                give_credit(pool, e.sems)

            @block.sync
            def _(sp):
                sp.dma_start(onehot[:, :], e.c_onehot).then_inc(s_in, 16)
                sp.dma_start(negrow[:, :], e.c_negrow).then_inc(s_in, 16)
                sp.dma_start(negwin[:, :], e.c_negwin).then_inc(s_in, 16)
                sp.dma_start(flip[:, :], e.c_flip).then_inc(s_in, 16)
                sp.dma_start(ident[:, :], e.c_ident).then_inc(s_in, 16)
                sp.dma_start(bgu[:, :], e.b_gate_up[0]).then_inc(s_in, 16)
                sp.wait_ge(s_tab, CREDIT + 1)
                sp.dma_start(table[:, 0:HN], e.rel_table).then_inc(s_in, 16)
                sp.wait_ge(s_rowsum, CREDIT + 2)
                sp.dma_start(e.d_rev.rearrange("k h n -> h k n"), rev[:, :, :]).then_inc(s_out, 16)
                sp.wait_ge(s_out, CREDIT + 16)
                with sp.Fori(0, HN + 1) as h:
                    sp.wait_ge(s_flip, CREDIT + h)
                    for k in range(2):
                        sp.dma_start(skew[:, k, :], e.skew_view(k, h)).then_inc(s_skew, 16)
                    sp.wait_ge(s_strip, CREDIT + h + 1)
                    sp.dma_start(e.d_strip[bass.ds(h, 1)].rearrange("o p n -> (o p) n"), strip[:, 0, :]).then_inc(s_stored, 16)
                    sp.dma_start(e.d_wstrip[bass.ds(h, 1)].rearrange("o p n -> (o p) n"), strip[:, 1, 384:S]).then_inc(s_stored, 16)
                sp.wait_ge(s_stored, CREDIT + 32 * (HN + 1))

            @block.vector
            def _(dve):
                dve.memset(table[:, :], 0.0).then_inc(s_tab, 1)
                dve.wait_ge(s_in, CREDIT + 16 * 7)
                for k, neg in enumerate((negrow, negwin)):
                    dve.wait_ge(s_rows, CREDIT + k + 1)
                    dve.tensor_tensor(rev[:, k, :].rearrange("h (c n) -> h c n", c=3), ps[0:HN + 1, 0:3, 0:REV // 3],
                                      neg[:, :].rearrange("h (c n) -> h c n", c=3), ALU.add).then_inc(s_rowsum, 1)
                dve.wait_ge(s_rows, CREDIT + 3)
                dve.tensor_copy(e.bgT[:, :, :].rearrange("p (b j) n -> p b j n", b=4),
                                ps[:, 4:8, 0:4 * NE].rearrange("p b (j n) -> p b j n", n=NE)).then_inc(s_rowsum, 1)
                with dve.Fori(0, HN + 1) as h:
                    dve.wait_ge(s_flip, CREDIT + h + 1)
                    dve.wait_ge(s_stored, CREDIT + 32 * h)
                    dve.tensor_copy(strip[:, :, :].rearrange("p k (c n) -> p (k c) n", c=2), ps[:, 0:4, :]).then_inc(s_strip, 1)

            @block.tensor
            def _(pe):
                pe.wait_ge(s_in, CREDIT + 16 * 7)
                for k in range(2):
                    if k:
                        pe.wait_ge(s_rowsum, CREDIT + 1)
                    for c in range(3):
                        mm = pe.matmul(ps[0:HN + 1, c, 0:REV // 3], table[:, :], onehot[:, c * (REV // 3):(c + 1) * (REV // 3)],
                                       start=True, stop=True)
                    mm.then_inc(s_rows, 1)
                for half in range(2):
                    for j in range(8):
                        n = half * 8 + j
                        mm = pe.transpose(ps[:, 4 + n // 4, (n % 4) * NE:(n % 4 + 1) * NE],
                                          bgu[:, 2 * P * j + half:2 * P * (j + 1):2], ident[0:NE, 0:NE])
                mm.then_inc(s_rows, 1)
                pe.wait_ge(s_rowsum, CREDIT + 3)
                with pe.Fori(0, HN + 1) as h:
                    pe.wait_ge(s_strip, CREDIT + h)
                    pe.wait_ge(s_skew, CREDIT + 32 * (h + 1))
                    for k in range(2):
                        for c in range(2):
                            mm = pe.matmul(ps[:, 2 * k + c, :], flip[:, :], skew[:, k, c * 512:(c + 1) * 512], start=True, stop=True)
                    mm.then_inc(s_flip, 1)


def stage_project(nc, e):
    with ExitStack() as ctx:
        sb, sem, ps = add_tools(nc, e, ctx)

        def pair(name, shape):
            return [sb(name + str(b), shape) for b in range(2)]

        w_in = sb("w_in", [P, KD, IN_COLS])
        w_uq = sb("w_uq", [P, 2, HM * QK])
        w_ukv = sb("w_ukv", [P, HM * (NOPE + VD)])
        ident = sb("ident_a", [P, P])
        g_x = sb("g_x", [P, KD])
        g_c = sb("g_c", [P, 3])
        g_qk = sb("g_qk", [P, 2 * HM, QK])
        g_qn = sb("g_qn", [P, HD])
        g_kn = sb("g_kn", [P, HD])
        inv_d = sb("inv_d", [P, 14])
        post = sb("post", [P, 14])
        post2 = sb("post2", [P, 16])
        eps = sb("eps_a", [P, 1])
        x = pair("x_a", [P, D])
        trig = pair("trig", [P, ROPE])
        sq = sb("sq_a", [P, IN_COLS])
        st = pair("st_a", [P, 4])
        xn = pair("xn_a", [P, D])
        hT = pair("hT_a", [P, KD, P])
        pr = pair("pr", [P, IN_COLS])
        st1 = pair("st1", [P, 14])
        cn = pair("cn", [P, 384])
        cT = pair("cT", [P, 3, P])
        qk = pair("qk", [P, 2 * HM, QK])
        sqk = sq[:, 0:2 * HM * QK].rearrange("p (h d) -> p h d", d=QK)
        st2 = pair("st2", [P, 16])
        ra = pair("ra", [P, 4, 2 * HM, 16])
        v_m = pair("v_m", [P, HM, VD])
        nq = pair("nq", [P, 768])
        gt = pair("gt", [P, 24])
        qkT = pair("qkT", [QK, 2 * HM, P])
        nT = pair("nT", [P, 8, P])
        s_w, s_ssq, s_std, s_xn, s_xT, s_hT = (sem("a_" + n) for n in ("weights", "ssq", "std", "xn", "xT", "hT"))
        s_pr, s_prA, s_prD, s_st1, s_std1, s_cn, s_cT, s_cTd = (sem("a_" + n) for n in ("proj", "projA", "projD", "st1", "std1", "cn", "cT", "cTd"))
        s_up, s_upA, s_upD, s_st2, s_std2, s_nq, s_qk, s_gt = (sem("a_" + n) for n in ("up", "upA", "upD", "st2", "std2", "nq", "qk", "gates"))
        s_oT, s_oTA, s_oTD, s_st, s_dch, s_ach = (sem("a_" + n) for n in ("outT", "outTA", "outTD", "stored", "dve_chain", "act_chain"))
        s_qkg, s_ra, s_ro, s_eps = sem("a_qkg"), sem("a_ra"), sem("a_ro"), sem("a_eps")
        s_x, s_trig = e.dma_sem("a_x"), e.dma_sem("a_trig")
        DVE_A = 17
        with nc.Block() as block:
            @block.gpsimd
            def _(pool):
                give_credit(pool, e.sems)
                with pool.Fori(0, NT // 2) as u:
                    pool.wait_ge(s_xn, CREDIT + 2 * u)
                    hold(pool, e.pool_passed)
                    for b in range(2):
                        pool.dma_start(x[b][:, :], e.x[0, bass.ds((2 * u + b) * P, P), :]).then_inc(s_x, 16)
                    pool.wait_ge(s_qk, CREDIT + 2 * u)
                    hold(pool, e.pool_passed)
                    for b in range(2):
                        pool.dma_start(trig[b][:, :], e.c_trig[bass.ds((2 * u + b) * P, P), :]).then_inc(s_trig, 16)

            @block.sync
            def _(sp):
                n = 0
                for dst, src in ((ident[:, :], e.c_ident), (w_in[:, :, :], e.w_in[0].rearrange("(k p) n -> p k n", p=P)),
                                 (w_uq[:, :, :], e.w_uq[0].rearrange("(k p) n -> p k n", p=P)), (w_ukv[:, :], e.w_ukv[0]),
                                 (inv_d[:, :], e.c_inv_d.partition_broadcast(P)), (post[:, :], e.c_post.partition_broadcast(P)),
                                 (post2[:, :], e.c_post2.partition_broadcast(P)),
                                 (g_qn[:, :], e.g_q_nsa[0].partition_broadcast(P)), (g_kn[:, :], e.g_k_nsa[0].partition_broadcast(P))):
                    sp.dma_start(dst, src).then_inc(s_w, 16)
                    n += 1
                for i in range(2 * HM):
                    sp.dma_start(g_qk[:, i, :], (e.g_q_mla if i < HM else e.g_k_mla)[0].partition_broadcast(P)).then_inc(s_w, 16)
                    n += 1
                with nc.allow_non_contiguous_dma("gain columns, once"):
                    for dst, src in ((g_x[:, :], e.g_attn_norm[0].rearrange("(k p) -> p k", p=P)),
                                     (g_c[:, 0:2], e.g_cq[0].rearrange("(k p) -> p k", p=P)),
                                     (g_c[:, 2:3], e.g_ckv[0].rearrange("(k p) -> p k", p=P))):
                        sp.dma_start(dst, src).then_inc(s_w, 16)
                        n += 1
                assert n == 28
                with sp.Fori(0, NT // 2) as u:
                    for b in range(2):
                        t = 2 * u + b
                        rows = bass.ds(t * P, P)
                        sp.wait_ge(s_upD, CREDIT + t + 1)
                        sp.dma_start(e.d_vm[:, rows, :].rearrange("h p d -> p h d"), v_m[b][:, :, :]).then_inc(s_st, 16)
                        sp.wait_ge(s_gt, CREDIT + t + 1)
                        with nc.allow_non_contiguous_dma("12-byte gates"):
                            sp.dma_start(e.d_gt[:, rows, :].rearrange("h p d -> p h d"), gt[b][:, :].rearrange("p (h d) -> p h d", d=3)).then_inc(s_st, 16)
                        for i, c in enumerate((C_VS, C_VW)):
                            sp.dma_start(e.d_vn[i][:, rows, :].rearrange("g p d -> p g d"),
                                         pr[b][:, c:c + 128].rearrange("p (g d) -> p g d", d=HD)).then_inc(s_st, 16)
                    for b in range(2):
                        t = 2 * u + b
                        rows = bass.ds(t * P, P)
                        sp.wait_ge(s_oTA, CREDIT + t + 1)
                        sp.wait_ge(s_oTD, CREDIT + t + 1)
                        hold(sp, e.sp_passed)
                        sp.dma_start(e.d_qm[:, :, rows].rearrange("h d p -> d h p"), qkT[b][:, 0:HM, :]).then_inc(s_st, 16)
                        sp.dma_start(e.d_km[:, :, rows].rearrange("h d p -> d h p"), qkT[b][:, HM:, :]).then_inc(s_st, 16)
                        for par in range(2):
                            sp.dma_start(e.d_qn[par][:, :, rows].rearrange("j d p -> d j p"), nT[b][HD * par:HD * (par + 1), 0:4, :]).then_inc(s_st, 16)
                        sp.dma_start(e.d_kn[:, :, rows].rearrange("w d p -> d w p"), nT[b][:, 4:6, :]).then_inc(s_st, 16)
                        sp.dma_start(e.d_cn[:, :, rows].rearrange("w d p -> d w p"), nT[b][:, 6:8, :]).then_inc(s_st, 16)
                sp.wait_ge(s_st, CREDIT + 160 * NT)

            @block.scalar
            def _(act):
                act.wait_ge(s_w, CREDIT + 16 * 28)
                act.wait_ge(s_eps, CREDIT + 1)
                with act.Fori(0, NT // 2) as u:
                    ch = Chain(act, s_ach, u, 2)
                    act.wait_ge(s_x, 32 * u + 32)
                    hold(act, e.act_passed)
                    for b in range(2):
                        t = 2 * u + b
                        act.wait_ge(s_std1, CREDIT + t - 1)
                        act.activation(xn[b][:, :], x[b][:, :], ACT.Square, accum_out=st[b][:, 0:1]).then_inc(s_ssq, 1)
                        act.wait_ge(s_ssq, CREDIT + t + 1)
                        act.activation(st[b][:, 1:2], st[b][:, 0:1], ACT.Sqrt, bias=eps[:, 0:1], scale=1.0 / D).then_inc(s_std, 1)
                    for b in range(2):
                        t = 2 * u + b
                        act.wait_ge(s_pr, CREDIT + t + 1)
                        act.wait_ge(s_st, CREDIT + 320 * u)
                        act.activation(pr[b][:, 0:2 * PCH].rearrange("p (c n) -> p c n", c=2), ps[:, 4 * b:4 * b + 2, 0:PCH], ACT.Copy).then_inc(s_prA, 1)
                    for b in range(2):
                        t = 2 * u + b
                        act.wait_ge(s_st1, CREDIT + t + 1)
                        act.activation(st1[b][:, :], st1[b][:, :], ACT.Sqrt, bias=eps[:, 0:1]).then_inc(s_std1, 1)
                    for b in range(2):
                        t = 2 * u + b
                        act.wait_ge(s_up, CREDIT + t + 1)
                        act.activation(qk[b][:, 0:HM, :].rearrange("p (c n) d -> p c (n d)", c=2), ps[:, 4 * b:4 * b + 2, 0:4 * QK], ACT.Copy).then_inc(s_upA, 1)
                        act.wait_ge(s_prD, CREDIT + t + 1)
                        ch(act.activation(gt[b][:, :], pr[b][:, C_GT:C_GT + 24], ACT.Sigmoid))
                    for b in range(2):
                        t = 2 * u + b
                        act.wait_ge(s_st2, CREDIT + t + 1)
                        act.activation(st2[b][:, :], st2[b][:, :], ACT.Sqrt, bias=eps[:, 0:1], scale=1.0 / QK).then_inc(s_std2, 1)
                    for b in range(2):
                        t = 2 * u + b
                        act.wait_ge(s_oT, CREDIT + 4 * u + 1 + b)
                        act.activation(nT[b][:, :, :].rearrange("p (c n) d -> p c (n d)", c=2), ps[:, 4 * b:4 * b + 2, :], ACT.Copy).then_inc(s_gt, 1)
                    for b in range(2):
                        t = 2 * u + b
                        act.wait_ge(s_oT, CREDIT + 4 * u + 3 + b)
                        act.activation(qkT[b][:, 0:HM, :].rearrange("p (c n) d -> p c (n d)", c=2), ps[0:QK, 4 * b:4 * b + 2, :], ACT.Copy).then_inc(s_oTA, 1)
                    ch.end()

            @block.vector
            def _(dve):
                dve.memset(eps[:, :], EPS).then_inc(s_eps, 1)
                dve.wait_ge(s_w, CREDIT + 16 * 28)
                with dve.Fori(0, NT // 2) as u:
                    ch = Chain(dve, s_dch, u, 2 * DVE_A)
                    for b in range(2):
                        t = 2 * u + b
                        dve.wait_ge(s_std, CREDIT + t + 1)
                        ch(dve.reciprocal(st[b][:, 2:3], st[b][:, 1:2]))
                        dve.tensor_scalar(xn[b][:, :], x[b][:, :], st[b][:, 2:3], None, ALU.mult).then_inc(s_xn, 1)
                    for b in range(2):
                        t = 2 * u + b
                        dve.wait_ge(s_xT, CREDIT + t + 1)
                        dve.wait_ge(s_pr, CREDIT + t - 1)
                        dve.tensor_tensor(hT[b][:, :, :].rearrange("p (c n) d -> p c n d", c=2), ps[:, 4 * b:4 * b + 2, :].rearrange("p c (n d) -> p c n d", d=P),
                                          bcast(g_x[:, :].rearrange("p (c n) -> p c n", c=2).unsqueeze(3), [P, 2, 4, P]), ALU.mult).then_inc(s_hT, 1)
                    for b in range(2):
                        t = 2 * u + b
                        dve.wait_ge(s_pr, CREDIT + t + 1)
                        dve.wait_ge(s_st, CREDIT + 320 * u)
                        dve.tensor_copy(pr[b][:, 2 * PCH:].rearrange("p (c n) -> p c n", c=2), ps[:, 4 * b + 2:4 * b + 4, 0:PCH]).then_inc(s_prD, 1)
                        dve.wait_ge(s_prD, CREDIT + t + 1)
                        dve.wait_ge(s_prA, CREDIT + t + 1)
                        ch(dve.tensor_tensor(sq[:, :], pr[b][:, :], pr[b][:, :], ALU.mult))
                        ch(dve.tensor_reduce(st1[b][:, 0:1], sq[:, C_CQ:C_CQ + QR], AX.X, ALU.add))
                        ch(dve.tensor_reduce(st1[b][:, 1:2], sq[:, C_CKV:C_CKV + KVR], AX.X, ALU.add))
                        ch(dve.tensor_reduce(st1[b][:, 2:10], sq[:, C_Q:C_Q + 512].rearrange("p (h d) -> p h d", d=HD), AX.X, ALU.add))
                        ch(dve.tensor_reduce(st1[b][:, 10:12], sq[:, C_KS:C_KS + 128].rearrange("p (h d) -> p h d", d=HD), AX.X, ALU.add))
                        ch(dve.tensor_reduce(st1[b][:, 12:14], sq[:, C_KW:C_KW + 128].rearrange("p (h d) -> p h d", d=HD), AX.X, ALU.add))
                        dve.tensor_tensor(st1[b][:, :], st1[b][:, :], inv_d[:, :], ALU.mult).then_inc(s_st1, 1)
                    for b in range(2):
                        t = 2 * u + b
                        dve.wait_ge(s_std1, CREDIT + t + 1)
                        ch(dve.reciprocal(st1[b][:, :], st1[b][:, :]))
                        ch(dve.tensor_tensor(st1[b][:, :], st1[b][:, :], post[:, :], ALU.mult))
                        ch(dve.tensor_scalar(cn[b][:, 0:QR], pr[b][:, C_CQ:C_CQ + QR], st1[b][:, 0:1], None, ALU.mult))
                        dve.tensor_scalar(cn[b][:, QR:], pr[b][:, C_CKV:C_CKV + KVR], st1[b][:, 1:2], None, ALU.mult).then_inc(s_cn, 1)
                    for b in range(2):
                        t = 2 * u + b
                        dve.wait_ge(s_cT, CREDIT + t + 1)
                        dve.tensor_tensor(cT[b][:, :, :], ps[:, 4 * b + 3, 0:384].rearrange("p (n d) -> p n d", d=P),
                                          bcast(g_c[:, :].unsqueeze(2), [P, 3, P]), ALU.mult).then_inc(s_cTd, 1)
                        for dst, src, r, n in ((0, C_Q, 2, 8), (512, C_KS, 10, 2), (640, C_KW, 12, 2)):
                            d3 = nq[b][:, dst:dst + n * HD].rearrange("p (h d) -> p h d", d=HD)
                            dve.tensor_tensor(d3, pr[b][:, src:src + n * HD].rearrange("p (h d) -> p h d", d=HD),
                                              bcast(st1[b][:, r:r + n].unsqueeze(2), [P, n, HD]), ALU.mult).then_inc(s_nq, 1)
                        dve.wait_ge(s_nq, CREDIT + 4 * t + 3)
                        ch(dve.tensor_tensor(nq[b][:, 0:512].rearrange("p (h d) -> p h d", d=HD), nq[b][:, 0:512].rearrange("p (h d) -> p h d", d=HD),
                                             bcast(g_qn[:, :].unsqueeze(1), [P, 8, HD]), ALU.mult))
                        dve.tensor_tensor(nq[b][:, 512:].rearrange("p (h d) -> p h d", d=HD), nq[b][:, 512:].rearrange("p (h d) -> p h d", d=HD),
                                          bcast(g_kn[:, :].unsqueeze(1), [P, 4, HD]), ALU.mult).then_inc(s_nq, 1)
                    for b in range(2):
                        t = 2 * u + b
                        dve.wait_ge(s_up, CREDIT + t + 1)
                        kv = ps[:, 4 * b + 2:4 * b + 4, :].rearrange("p c (n d) -> p c n d", d=NOPE + VD)
                        ch(dve.tensor_copy(qk[b][:, HM:, 0:NOPE].rearrange("p (c n) d -> p c n d", c=2), kv[:, :, :, 0:NOPE]))
                        dve.tensor_copy(v_m[b][:, :, :].rearrange("p (c n) d -> p c n d", c=2), kv[:, :, :, NOPE:]).then_inc(s_upD, 1)
                        ch(dve.tensor_copy(qk[b][:, HM:, NOPE:], bcast(pr[b][:, C_KR:C_KR + ROPE].unsqueeze(1), [P, HM, ROPE])))
                        dve.wait_ge(s_upA, CREDIT + t + 1)
                        ch(dve.tensor_tensor(sqk, qk[b][:, :, :], qk[b][:, :, :], ALU.mult))
                        dve.tensor_reduce(st2[b][:, :], sqk, AX.X, ALU.add).then_inc(s_st2, 1)
                    for b in range(2):
                        t = 2 * u + b
                        dve.wait_ge(s_std2, CREDIT + t + 1)
                        ch(dve.reciprocal(st2[b][:, :], st2[b][:, :]))
                        ch(dve.tensor_tensor(st2[b][:, :], st2[b][:, :], post2[:, :], ALU.mult))
                        ch(dve.tensor_tensor(qk[b][:, :, :], qk[b][:, :, :], bcast(st2[b][:, :].unsqueeze(2), [P, 16, QK]), ALU.mult))
                        dve.tensor_tensor(qk[b][:, :, :], qk[b][:, :, :], g_qk[:, :, :], ALU.mult).then_inc(s_qkg, 1)
                        dve.wait_ge(s_qkg, CREDIT + t + 1)
                        dve.wait_ge(s_trig, 32 * u + 32)
                        hold(dve, e.dve_passed)
                        x1, x2 = qk[b][:, :, NOPE:NOPE + 16], qk[b][:, :, NOPE + 16:]
                        cos, sin = (bcast(trig[b][:, a:a + 16].unsqueeze(1), [P, 16, 16]) for a in (0, 16))
                        for n, (half, factor) in enumerate(((x1, cos), (x2, sin), (x2, cos), (x1, sin))):
                            dve.tensor_tensor(ra[b][:, n, :, :], half, factor, ALU.mult).then_inc(s_ra, 1)
                        dve.wait_ge(s_ra, CREDIT + 4 * t + 4)
                        dve.tensor_tensor(x1, ra[b][:, 0, :, :], ra[b][:, 1, :, :], ALU.subtract).then_inc(s_ro, 1)
                        dve.tensor_tensor(x2, ra[b][:, 2, :, :], ra[b][:, 3, :, :], ALU.add).then_inc(s_qk, 1)
                    for b in range(2):
                        t = 2 * u + b
                        dve.wait_ge(s_oT, CREDIT + 4 * u + 3 + b)
                        dve.tensor_copy(qkT[b][:, HM:, :].rearrange("p (c n) d -> p c (n d)", c=2), ps[0:QK, 4 * b + 2:4 * b + 4, :]).then_inc(s_oTD, 1)
                        dve.wait_ge(s_oTD, CREDIT + t + 1)
                    ch.end()

            @block.tensor
            def _(pe):
                pe.wait_ge(s_w, CREDIT + 16 * 28)
                with pe.Fori(0, NT // 2) as u:
                    for b in range(2):
                        t = 2 * u + b
                        pe.wait_ge(s_xn, CREDIT + t + 1)
                        pe.wait_ge(s_oTA, CREDIT + t - 1)
                        pe.wait_ge(s_oTD, CREDIT + t - 1)
                        for k in range(KD):
                            mm = pe.transpose(ps[:, 4 * b + k // 4, (k % 4) * P:(k % 4 + 1) * P], xn[b][:, k * P:(k + 1) * P], ident[:, :])
                        mm.then_inc(s_xT, 1)
                    for b in range(2):
                        t = 2 * u + b
                        pe.wait_ge(s_hT, CREDIT + t + 1)
                        for c in range(4):
                            for k in range(KD):
                                mm = pe.matmul(ps[:, 4 * b + c, 0:PCH], hT[b][:, k, :], w_in[:, k, c * PCH:(c + 1) * PCH], start=(k == 0), stop=(k == KD - 1))
                        mm.then_inc(s_pr, 1)
                    for b in range(2):
                        t = 2 * u + b
                        pe.wait_ge(s_cn, CREDIT + t + 1)
                        pe.wait_ge(s_prD, CREDIT + t + 1)
                        for k in range(3):
                            mm = pe.transpose(ps[:, 4 * b + 3, k * P:(k + 1) * P], cn[b][:, k * P:(k + 1) * P], ident[:, :])
                        mm.then_inc(s_cT, 1)
                    for b in range(2):
                        t = 2 * u + b
                        pe.wait_ge(s_cTd, CREDIT + t + 1)
                        pe.wait_ge(s_prA, CREDIT + t + 1)
                        for c in range(2):
                            for k in range(2):
                                pe.matmul(ps[:, 4 * b + c, 0:4 * QK], cT[b][:, k, :], w_uq[:, k, c * 4 * QK:(c + 1) * 4 * QK], start=(k == 0), stop=(k == 1))
                        for c in range(2):
                            mm = pe.matmul(ps[:, 4 * b + 2 + c, :], cT[b][:, 2, :], w_ukv[:, c * 512:(c + 1) * 512], start=True, stop=True)
                        mm.then_inc(s_up, 1)
                    for b in range(2):
                        t = 2 * u + b
                        pe.wait_ge(s_nq, CREDIT + 4 * t + 4)
                        pe.wait_ge(s_upA, CREDIT + t + 1)
                        for j in range(8):
                            src = nq[b][:, j * P:(j + 1) * P] if j < 6 else pr[b][:, C_KC + (j - 6) * P:C_KC + (j - 5) * P]
                            mm = pe.transpose(ps[:, 4 * b + j // 4, (j % 4) * P:(j % 4 + 1) * P], src, ident[:, :])
                        mm.then_inc(s_oT, 1)
                    for b in range(2):
                        t = 2 * u + b
                        pe.wait_ge(s_qk, CREDIT + t + 1)
                        pe.wait_ge(s_gt, CREDIT + t + 1)
                        for j in range(2 * HM):
                            mm = pe.transpose(ps[0:QK, 4 * b + j // 4, (j % 4) * P:(j % 4 + 1) * P], qk[b][:, j, :], ident[:, :])
                        mm.then_inc(s_oT, 1)


def stage_compress(nc, e):
    with ExitStack() as ctx:
        sb, sem, ps = add_tools(nc, e, ctx)
        ident = sb("ident_c", [P, P])
        kcT = sb("kcT_all", [HD, 2, G, S])
        w1 = sb("w1", [HD, 2, CMP_LEN, CMP_HID])
        w2 = sb("w2", [CMP_HID, 2, HD])
        pos = sb("pos", [CMP_LEN, 2, HD])
        posT = sb("posT", [HD, 2, CMP_LEN])
        pb = sb("pb", [CMP_HID, 2])
        gk = sb("gk", [P, HD])
        eps = sb("eps_c", [P, 1])
        u = sb("u", [CMP_HID, 2, G * NCMP])
        hid = sb("hid", [CMP_HID, 2, G * NCMP])
        cc = sb("cc", [NCMP, 2 * G, HD])
        sq = sb("sq_c", [NCMP, G, HD])
        st = sb("st_c", [NCMP, G])
        kT = sb("kT_c", [HD, G, NCMP])
        s_in, s_ps, s_dv, s_act, s_out = (sem("c_" + n) for n in ("in", "pe", "dve", "act", "stored"))
        with nc.Block() as block:
            @block.gpsimd
            def _(pool):
                give_credit(pool, e.sems)

            @block.sync
            def _(sp):
                sp.dma_start(ident[:, :], e.c_ident).then_inc(s_in, 16)
                sp.dma_start(gk[:, :], e.g_k_nsa[0].partition_broadcast(P)).then_inc(s_in, 16)
                for i in range(2):
                    for g in range(G):
                        sp.dma_start(kcT[:, i, g, :], e.d_cn[i, g * HD:(g + 1) * HD, :]).then_inc(s_in, 16)
                for i, (a, b, c) in enumerate(((e.cmp_k_w1, e.cmp_k_w2, e.cmp_k_pos), (e.cmp_v_w1, e.cmp_v_w2, e.cmp_v_pos))):
                    sp.dma_start(w1[:, i, :, :], a[0].rearrange("l d f -> d l f")).then_inc(s_in, 16)
                    sp.dma_start(w2[:, i, :], b[0]).then_inc(s_in, 16)
                    sp.dma_start(pos[:, i, :], c[0]).then_inc(s_in, 16)
                sp.wait_ge(s_dv, CREDIT + 11)
                sp.dma_start(e.d_ck.rearrange("g d n -> d g n"), kT[:, :, :]).then_inc(s_out, 16)
                sp.dma_start(e.d_cv.rearrange("g n d -> n g d"), cc[:, G:, :]).then_inc(s_out, 16)
                sp.wait_ge(s_out, CREDIT + 32)

            @block.tensor
            def _(pe):
                pe.wait_ge(s_in, CREDIT + 16 * 12)
                for i in range(2):
                    mm = pe.transpose(ps[0:HD, 0, i * CMP_LEN:(i + 1) * CMP_LEN], pos[:, i, :], ident[0:CMP_LEN, 0:CMP_LEN])
                mm.then_inc(s_ps, 1)
                pe.wait_ge(s_dv, CREDIT + 2)
                for i in range(2):
                    for l in range(CMP_LEN):
                        mv = kcT[:, i, :, l:l + CMP_STRIDE * (NCMP - 1) + 1:CMP_STRIDE]
                        pe.matmul(ps[:, 1 + i, 0:G * NCMP].rearrange("p (g n) -> p g n", g=G), w1[:, i, l, :], mv, start=(l == 0), stop=(l == CMP_LEN - 1))
                    for l in range(CMP_LEN):
                        mm = pe.matmul(ps[:, 3 + i, 0:1], w1[:, i, l, :], posT[:, i, l:l + 1], start=(l == 0), stop=(l == CMP_LEN - 1))
                mm.then_inc(s_ps, 1)
                pe.wait_ge(s_act, CREDIT + 2)
                for i in range(2):
                    for g in range(G):
                        mm = pe.matmul(ps[0:NCMP, 5, (i * G + g) * HD:(i * G + g + 1) * HD], hid[:, i, g * NCMP:(g + 1) * NCMP], w2[:, i, :], start=True, stop=True)
                mm.then_inc(s_ps, 1)
                pe.wait_ge(s_dv, CREDIT + 10)
                for g in range(G):
                    mm = pe.transpose(ps[0:HD, 6, g * P:g * P + NCMP], cc[:, g, :], ident[0:NCMP, 0:NCMP])
                mm.then_inc(s_ps, 1)

            @block.scalar
            def _(act):
                for i in range(2):
                    act.wait_ge(s_dv, CREDIT + 4 + 2 * i)
                    act.activation(hid[:, i, :], u[:, i, :], ACT.Gelu_apprx_tanh).then_inc(s_act, 1)
                act.wait_ge(s_dv, CREDIT + 9)
                act.activation(st[:, :], st[:, :], ACT.Sqrt, bias=eps[0:NCMP, 0:1], scale=1.0 / HD).then_inc(s_act, 1)

            @block.vector
            def _(dve):
                n = [0]

                def step(ins):
                    ins.then_inc(s_dv, 1)
                    n[0] += 1
                    dve.wait_ge(s_dv, CREDIT + n[0])
                step(dve.memset(eps[:, :], EPS))
                dve.wait_ge(s_ps, CREDIT + 1)
                step(dve.tensor_copy(posT[:, :, :], ps[0:HD, 0, 0:2 * CMP_LEN].rearrange("p (i l) -> p i l", i=2)))
                dve.wait_ge(s_ps, CREDIT + 2)
                for i in range(2):
                    step(dve.tensor_copy(pb[:, i:i + 1], ps[:, 3 + i, 0:1]))
                    step(dve.tensor_scalar(u[:, i, :], ps[:, 1 + i, 0:G * NCMP], pb[:, i:i + 1], None, ALU.add))
                dve.wait_ge(s_ps, CREDIT + 3)
                dve.wait_ge(s_in, CREDIT + 16 * 12)
                step(dve.tensor_copy(cc[:, :, :], ps[0:NCMP, 5, 0:2 * G * HD].rearrange("p (i d) -> p i d", d=HD)))
                step(dve.tensor_tensor(sq[:, :, :], cc[:, 0:G, :], cc[:, 0:G, :], ALU.mult))
                step(dve.tensor_reduce(st[:, :], sq[:, :, :], AX.X, ALU.add))
                dve.wait_ge(s_act, CREDIT + 3)
                dve.reciprocal(st[:, :], st[:, :]).then_inc(s_act, 1)
                dve.wait_ge(s_act, CREDIT + 4)
                dve.tensor_tensor(cc[:, 0:G, :], cc[:, 0:G, :], bcast(st[:, :].unsqueeze(2), [NCMP, G, HD]), ALU.mult).then_inc(s_act, 1)
                dve.wait_ge(s_act, CREDIT + 5)
                step(dve.tensor_tensor(cc[:, 0:G, :], cc[:, 0:G, :], bcast(gk[0:NCMP, :].unsqueeze(1), [NCMP, G, HD]), ALU.mult))
                dve.wait_ge(s_ps, CREDIT + 4)
                step(dve.tensor_copy(kT[:, :, :], ps[0:HD, 6, 0:G * P].rearrange("p (g n) -> p g n", g=G)[:, :, 0:NCMP]))


def stage_attend(nc, e):
    STEPS = [(b, q) for b in "mcws" for q in range(NT)]
    NS = len(STEPS)

    def tiles(b, q):
        return [0] if b == "c" else list(range(max(0, q - WIN // P), q + 1)) if b == "w" else list(range(q + 1))

    def width(b, q):
        return min(NCMP, (P * (q + 1) - CMP_LEN) // CMP_STRIDE + 1) if b == "c" else P * len(tiles(b, q))

    groups = [(len(tiles(*s)) + 3) // 4 for s in STEPS]
    NG = sum(groups)
    N2 = sum(g == 2 for g in groups)
    gdone = [sum(groups[:i + 1]) for i in range(NS)]
    g2done = [sum(g == 2 for g in groups[:i + 1]) for i in range(NS)]
    with ExitStack() as ctx:
        sb, sem, ps = add_tools(nc, e, ctx)
        ident = sb("ident_t", [P, P])
        qm, km = sb("qm", [QK, S]), sb("km", [QK, S])
        vm = sb("vm", [P, NT, VD])
        qn = sb("qn", [HD, S])
        kn = sb("kn", [HD, 2, S])
        vn = sb("vn", [P, 2, NT, HD])
        ck, cv = sb("ck", [HD, NCMP]), sb("cv", [NCMP, HD])
        mstrip, strip, wstrip = sb("mstrip", [P, S]), sb("strip_t", [P, S]), sb("wstrip", [P, WIN + P])
        gates = sb("gates", [P, NT, 3])
        cvalid = sb("cvalid", [P, 1])
        sc = sb("sc", [P, 4, S])
        pT = sb("pT", [P, 2, S])
        mx, nm, rs, co = (sb(n, [P, 4]) for n in ("mx", "nm", "rs", "co"))
        ym, yn = sb("ym", [P, NT, VD]), sb("yn", [P, NT, HD])
        s_c, s_lm, s_ln, s_fm, s_g = (sem("t_" + n) for n in ("const", "load_mla", "load_nsa", "mla_used", "gate"))
        s_s, s_m, s_p, s_pT, s_cA, s_cD, s_o, s_y = (sem("t_" + n) for n in
            ("scores", "max", "probs", "probsT", "copiedA", "copiedD", "out", "y"))
        s_ym, s_yn, s_dch, s_hd = (sem("t_" + n) for n in ("ym_stored", "yn_stored", "dve_chain", "sc_set"))
        NLN = 9
        DCH = 3 * NS - NT + 1
        dy = e.d_y.rearrange("(t p) n -> p t n", p=P)
        with nc.Block() as block:
            @block.gpsimd
            def _(pool):
                give_credit(pool, e.sems)

            @block.sync
            def _(sp):
                sp.dma_start(ident[:, :], e.c_ident).then_inc(s_c, 16)
                sp.dma_start(mstrip[:, :], e.d_strip[HN]).then_inc(s_c, 16)
                sp.dma_start(cvalid[:, :], e.c_cvalid).then_inc(s_c, 16)
                def load_mla(h):
                    one = bass.ds(h, 1)
                    sp.dma_start(qm[:, :], e.d_qm[one].rearrange("o d n -> (o d) n")).then_inc(s_lm, 16)
                    sp.dma_start(km[:, :], e.d_km[one].rearrange("o d n -> (o d) n")).then_inc(s_lm, 16)
                    sp.dma_start(vm[:, :, :], e.d_vm[one].rearrange("o (t p) d -> p (o t) d", p=P)).then_inc(s_lm, 16)

                def head(h, last):
                    one = bass.ds(h, 1)
                    g = bass.ds(h // HPG, 1)
                    gd = bass.ds((h // HPG) * HD, HD)
                    sp.wait_ge(s_y, CREDIT + NS * h)
                    sp.dma_start(ck[:, :], e.d_ck[g].rearrange("o d n -> (o d) n")).then_inc(s_ln, 16)
                    sp.dma_start(cv[:, :], e.d_cv[g].rearrange("o n d -> (o n) d")).then_inc(s_ln, 16)
                    sp.dma_start(qn[:, :], e.d_qn_flat[one].rearrange("o d n -> (o d) n")).then_inc(s_ln, 16)
                    sp.dma_start(kn[:, :, :], e.d_kn[:, gd, :].rearrange("w d n -> d w n")).then_inc(s_ln, 16)
                    for i in range(2):
                        sp.dma_start(vn[:, i, :, :], e.d_vn[i][g].rearrange("o (t p) d -> p (o t) d", p=P)).then_inc(s_ln, 16)
                    sp.dma_start(strip[:, :], e.d_strip[one].rearrange("o p n -> (o p) n")).then_inc(s_ln, 16)
                    sp.dma_start(wstrip[:, :], e.d_wstrip[one].rearrange("o p n -> (o p) n")).then_inc(s_ln, 16)
                    with nc.allow_non_contiguous_dma("12-byte gates"):
                        sp.dma_start(gates[:, :, :], e.d_gt[one].rearrange("o (t p) b -> p (o t) b", p=P)).then_inc(s_ln, 16)
                    sp.wait_ge(s_y, CREDIT + NS * h + NT)
                    sp.dma_start(dy[:, :, bass.ds(h * VD, VD)], ym[:, :, :]).then_inc(s_ym, 16)
                    if not last:
                        load_mla(h + 1)
                    sp.wait_ge(s_y, CREDIT + NS * h + NS)
                    sp.dma_start(dy[:, :, bass.ds(h * HD + HM * VD, HD)], yn[:, :, :]).then_inc(s_yn, 16)

                load_mla(0)
                with sp.Fori(0, HM - 1) as h:
                    head(h, False)
                head(HM - 1, True)
                sp.wait_ge(s_ym, CREDIT + 16 * HM)
                sp.wait_ge(s_yn, CREDIT + 16 * HM)

            @block.tensor
            def _(pe):
                pe.wait_ge(s_c, CREDIT + 48)
                with pe.Fori(0, HM) as h:
                    def scores(i):
                        b, q = STEPS[i]
                        if i == 0:
                            pe.wait_ge(s_lm, CREDIT + 48 * h + 48)
                        if i == NT:
                            pe.wait_ge(s_ln, CREDIT + 16 * NLN * h + 16 * NLN)
                        pe.wait_ge(s_m, CREDIT + NS * h + max(i - 1, 0))
                        hold(pe, e.pe_passed)
                        w, lo = width(b, q), tiles(b, q)[0] * P
                        Q = qm if b == "m" else qn
                        K = {"m": km, "c": ck, "w": kn[:, 1, :], "s": kn[:, 0, :]}[b][:, lo:lo + w]
                        for c in range(0, w, 512):
                            mm = pe.matmul(ps[:, 2 * (i % 2) + c // 512, 0:min(512, w - c)], Q[:, q * P:(q + 1) * P], K[:, c:min(c + 512, w)],
                                           start=True, stop=True)
                        mm.then_inc(s_s, 1)

                    def turn(i):
                        pe.wait_ge(s_p, CREDIT + NS * h + i + 1)
                        hold(pe, e.pe_passed)
                        n = len(tiles(*STEPS[i]))
                        for j in range(groups[i]):
                            if j == 0:
                                pe.wait_ge(s_cA, CREDIT + NS * h + i)
                            else:
                                pe.wait_ge(s_cD, CREDIT + N2 * h + g2done[i] - 1)
                            hold(pe, e.pe_passed)
                            for k in range(4 * j, min(n, 4 * j + 4)):
                                mm = pe.transpose(ps[:, 4 + j, (k % 4) * P:(k % 4 + 1) * P], sc[:, i % 4, k * P:(k + 1) * P], ident[:, :])
                            mm.then_inc(s_pT, 1)

                    def values(i):
                        b, q = STEPS[i]
                        pe.wait_ge(s_cA, CREDIT + NS * h + i + 1)
                        if groups[i] == 2:
                            pe.wait_ge(s_cD, CREDIT + N2 * h + g2done[i])
                        pe.wait_ge(s_y, CREDIT + NS * h + max(i - 1, 0))
                        hold(pe, e.pe_passed)
                        ts = tiles(b, q)
                        for n, k in enumerate(ts):
                            if b == "c":
                                w = width(b, q)
                                mm = pe.matmul(ps[:, 6 + i % 2, 0:HD], pT[0:w, i % 2, 0:P], cv[0:w, :], start=True, stop=True)
                            else:
                                V = vm[:, k, :] if b == "m" else vn[:, "sw".index(b), k, :]
                                mm = pe.matmul(ps[:, 6 + i % 2, 0:HD], pT[:, i % 2, n * P:(n + 1) * P], V, start=(n == 0), stop=(n == len(ts) - 1))
                        mm.then_inc(s_o, 1)

                    scores(0)
                    scores(1)
                    for i in range(NS):
                        turn(i)
                        if i:
                            values(i - 1)
                        if i + 2 < NS:
                            scores(i + 2)
                    values(NS - 1)

            @block.scalar
            def _(act):
                act.wait_ge(s_c, CREDIT + 48)
                with act.Fori(0, HM) as h:
                    def copy(i):
                        act.wait_ge(s_pT, CREDIT + NG * h + gdone[i] - groups[i] + 1)
                        act.wait_ge(s_o, CREDIT + NS * h + max(i - 1, 0))
                        w = P * min(4, len(tiles(*STEPS[i])))
                        act.activation(pT[:, i % 2, 0:w], ps[:, 4, 0:w], ACT.Copy).then_inc(s_cA, 1)

                    def exps(i):
                        act.wait_ge(s_m, CREDIT + NS * h + i + 1)
                        w = width(*STEPS[i])
                        act.activation(sc[:, i % 4, 0:w], sc[:, i % 4, 0:w], ACT.Exp, bias=nm[:, i % 4:i % 4 + 1],
                                       accum_out=rs[:, i % 4:i % 4 + 1]).then_inc(s_p, 1)

                    exps(0)
                    for i in range(NS):
                        if i + 1 < NS:
                            exps(i + 1)
                        copy(i)

            @block.vector
            def _(dve):
                dve.memset(sc[:, :, :], 0.0).then_inc(s_hd, 1)
                dve.wait_ge(s_hd, CREDIT + 1)
                dve.wait_ge(s_c, CREDIT + 48)
                with dve.Fori(0, HM) as h:
                    ch = Chain(dve, s_dch, h, DCH)

                    def peak(i):
                        b, q = STEPS[i]
                        w = width(b, q)
                        if b == "c":
                            bias = strip[:, S + CMP_LEN - 1 - P * (q + 1):S + CMP_LEN - 1 - P * (q + 1) + CMP_STRIDE * (w - 1) + 1:CMP_STRIDE]
                        elif b == "w":
                            bias = wstrip[:, WIN + P - w:]
                        else:
                            bias = (mstrip if b == "m" else strip)[:, S - w:]
                        if i == NT:
                            dve.wait_ge(s_ln, CREDIT + 16 * NLN * h + 16 * NLN)
                            ch(dve.tensor_tensor(gates[:, 0, 0:1], gates[:, 0, 0:1], cvalid[:, :], ALU.mult))
                        dve.wait_ge(s_s, CREDIT + NS * h + i + 1)
                        dve.wait_ge(s_pT, CREDIT + NG * h + (gdone[i - 4] if i >= 4 else 0))
                        hold(dve, e.dve_passed)
                        src = ps[:, 2 * (i % 2):2 * (i % 2) + 2, :].rearrange("p c n -> p (c n)")[:, 0:w]
                        ch(dve.tensor_tensor_reduce(sc[:, i % 4, 0:w], src, bias, 1.0, -3.0e38, ALU.add, ALU.max, mx[:, i % 4:i % 4 + 1]))
                        dve.tensor_scalar(nm[:, i % 4:i % 4 + 1], mx[:, i % 4:i % 4 + 1], -1.0, None, ALU.mult).then_inc(s_m, 1)

                    def copy(i):
                        if groups[i] == 2:
                            n = len(tiles(*STEPS[i])) - 4
                            dve.wait_ge(s_pT, CREDIT + NG * h + gdone[i])
                            dve.wait_ge(s_o, CREDIT + NS * h + max(i - 1, 0))
                            dve.tensor_copy(pT[:, i % 2, 512:512 + n * P], ps[:, 5, 0:n * P]).then_inc(s_cD, 1)

                    def finish(i):
                        b, q = STEPS[i]
                        k = i % 4
                        if i == 0:
                            dve.wait_ge(s_ym, CREDIT + 16 * h)
                        if i == NT:
                            dve.wait_ge(s_yn, CREDIT + 16 * h)
                        dve.wait_ge(s_o, CREDIT + NS * h + i + 1)
                        ch(dve.reciprocal(co[:, k:k + 1], rs[:, k:k + 1]))
                        O = ps[:, 6 + i % 2, 0:HD]
                        if b == "m":
                            dve.tensor_scalar(ym[:, q, :], O, co[:, k:k + 1], None, ALU.mult).then_inc(s_y, 1)
                        else:
                            ch(dve.tensor_tensor(co[:, k:k + 1], co[:, k:k + 1], gates[:, q, "csw".index(b):"csw".index(b) + 1], ALU.mult))
                            if b == "c":
                                dve.tensor_scalar(yn[:, q, :], O, co[:, k:k + 1], None, ALU.mult).then_inc(s_y, 1)
                            else:
                                dve.scalar_tensor_tensor(yn[:, q, :], O, co[:, k:k + 1], yn[:, q, :], ALU.mult, ALU.add).then_inc(s_y, 1)

                    peak(0)
                    for i in range(NS):
                        if i + 1 < NS:
                            peak(i + 1)
                        copy(i)
                        if i:
                            finish(i - 1)
                    finish(NS - 1)
                    ch.end()


def stage_memory(nc, e):
    with ExitStack() as ctx:
        sb, sem, ps = add_tools(nc, e, ctx)
        MT = N_MEM // P
        ident = sb("ident_m", [P, P])
        w = sb("w_mkv", [P, KD, 2 * MH * MHD])
        gx, gk = sb("gx_m", [P, KD]), sb("gk_m", [P, MHD])
        eps = sb("eps_m", [P, 1])
        m, mn, sq = sb("m", [P, MT, D]), sb("mn", [P, D]), sb("sq_m", [P, D])
        st, sk = sb("st_m", [P, 2]), sb("sk_m", [P, MH])
        mT = sb("mT", [P, KD, P])
        kk = sb("kk", [P, MH, MHD])
        none = sb("none", [P, 2 * NE * CAP // P], U32)
        s_in, s_pe, s_act, s_dv, s_z, s_k = (sem("m_" + n) for n in ("in", "pe", "act", "dve", "rows_unused", "key"))
        with nc.Block() as block:
            @block.sync
            def _(sp):
                for dst, src in ((ident[:, :], e.c_ident), (w[:, :, :], e.w_mkv[0].rearrange("(k p) n -> p k n", p=P)),
                                 (m[:, :, :], e.mem[0].rearrange("(t p) d -> p t d", p=P)), (gk[:, :], e.g_mk[0].partition_broadcast(P))):
                    sp.dma_start(dst, src).then_inc(s_in, 16)
                with nc.allow_non_contiguous_dma("gain columns, once"):
                    sp.dma_start(gx[:, :], e.g_mem_src[0].rearrange("(k p) -> p k", p=P)).then_inc(s_in, 16)
                sp.wait_ge(s_z, CREDIT + 1)
                sp.dma_start(e.d_tok.rearrange("(p n) o -> p (n o)", p=P), none[:, :]).then_inc(s_z, 16)
                sp.wait_ge(s_z, CREDIT + 17)

            @block.gpsimd
            def _(pool):
                give_credit(pool, e.sems)
                pool.memset(none[:, :], NOBODY).then_inc(s_z, 1)

            @block.scalar
            def _(act):
                act.wait_ge(s_in, CREDIT + 80)
                for i in range(MT):
                    act.wait_ge(s_dv, CREDIT + 7 * i + 1)
                    act.activation(sq[:, :], m[:, i, :], ACT.Square, accum_out=st[:, 0:1]).then_inc(s_act, 1)
                    act.wait_ge(s_act, CREDIT + 3 * i + 1)
                    act.activation(st[:, 1:2], st[:, 0:1], ACT.Sqrt, bias=eps[:, 0:1], scale=1.0 / D).then_inc(s_act, 1)
                    act.wait_ge(s_dv, CREDIT + 7 * i + 5)
                    act.activation(sk[:, :], sk[:, :], ACT.Sqrt, bias=eps[:, 0:1], scale=1.0 / MHD).then_inc(s_act, 1)

            @block.vector
            def _(dve):
                n = [0]

                def step(ins):
                    ins.then_inc(s_dv, 1)
                    n[0] += 1
                    dve.wait_ge(s_dv, CREDIT + n[0])

                step(dve.memset(eps[:, :], EPS))
                dve.wait_ge(s_in, CREDIT + 80)
                for i in range(MT):
                    dve.wait_ge(s_act, CREDIT + 3 * i + 2)
                    dve.reciprocal(st[:, 1:2], st[:, 1:2]).then_inc(s_k, 1)
                    dve.wait_ge(s_k, CREDIT + 4 * i + 1)
                    step(dve.tensor_scalar(mn[:, :], m[:, i, :], st[:, 1:2], None, ALU.mult))
                    dve.wait_ge(s_pe, CREDIT + 3 * i + 1)
                    step(dve.tensor_tensor(mT[:, :, :].rearrange("p (c n) d -> p c n d", c=2), ps[:, 0:2, :].rearrange("p c (n d) -> p c n d", d=P),
                                           bcast(gx[:, :].rearrange("p (c n) -> p c n", c=2).unsqueeze(3), [P, 2, 4, P]), ALU.mult))
                    dve.wait_ge(s_pe, CREDIT + 3 * i + 2)
                    dve.tensor_copy(kk[:, :, :], ps[:, 2, 0:256].rearrange("p (h d) -> p h d", d=MHD)).then_inc(s_k, 1)
                    dve.wait_ge(s_k, CREDIT + 4 * i + 2)
                    step(dve.tensor_tensor(sq[:, 0:256].rearrange("p (h d) -> p h d", d=MHD), kk[:, :, :], kk[:, :, :], ALU.mult))
                    step(dve.tensor_reduce(sk[:, :], sq[:, 0:256].rearrange("p (h d) -> p h d", d=MHD), AX.X, ALU.add))
                    dve.wait_ge(s_act, CREDIT + 3 * i + 3)
                    dve.reciprocal(sk[:, :], sk[:, :]).then_inc(s_k, 1)
                    dve.wait_ge(s_k, CREDIT + 4 * i + 3)
                    dve.tensor_tensor(kk[:, :, :], kk[:, :, :], bcast(sk[:, :].unsqueeze(2), [P, MH, MHD]), ALU.mult).then_inc(s_k, 1)
                    dve.wait_ge(s_k, CREDIT + 4 * i + 4)
                    step(dve.tensor_tensor(kk[:, :, :], kk[:, :, :], bcast(gk[:, :].unsqueeze(1), [P, MH, MHD]), ALU.mult))
                    step(dve.tensor_copy(e.vmem[:, i, :, :], ps[:, 2, 256:512].rearrange("p (h d) -> p h d", d=MHD)))
                    dve.wait_ge(s_pe, CREDIT + 3 * i + 3)
                    step(dve.tensor_copy(e.kTm[:, :, i * P:(i + 1) * P], ps[:, 3, 0:256].rearrange("p (j n) -> p j n", n=P)))

            @block.tensor
            def _(pe):
                pe.wait_ge(s_in, CREDIT + 80)
                for i in range(MT):
                    pe.wait_ge(s_dv, CREDIT + 7 * i + 2)
                    for k in range(KD):
                        mm = pe.transpose(ps[:, k // 4, (k % 4) * P:(k % 4 + 1) * P], mn[:, k * P:(k + 1) * P], ident[:, :])
                    mm.then_inc(s_pe, 1)
                    pe.wait_ge(s_dv, CREDIT + 7 * i + 3)
                    for k in range(KD):
                        mm = pe.matmul(ps[:, 2, :], mT[:, k, :], w[:, k, :], start=(k == 0), stop=(k == KD - 1))
                    mm.then_inc(s_pe, 1)
                    pe.wait_ge(s_dv, CREDIT + 7 * i + 6)
                    for j in range(2):
                        mm = pe.transpose(ps[:, 3, j * P:(j + 1) * P], kk[:, 2 * j:2 * j + 2, :].rearrange("p h d -> p (h d)"), ident[:, :])
                    mm.then_inc(s_pe, 1)


def stage_mix(nc, e):
    with ExitStack() as ctx:
        sb, sem, ps = add_tools(nc, e, ctx)
        ident, before, ones = sb("ident_x", [P, P]), sb("before", [P, P]), sb("ones", [P, P])
        w_out, w_mq = sb("w_out", [P, KD, D]), sb("w_mq", [P, KD, MH * MHD])
        w_mo, rw = sb("w_mo", [P, 2, D]), sb("rw", [P, KD, NE])
        bdown = sb("bdown", [NE, D])
        g_o, g_m, g_e = sb("g_o", [P, KD]), sb("g_m", [P, KD]), sb("g_e", [P, D])
        g_q, rb, iota, ebase = sb("g_q", [P, MHD]), sb("rb", [P, NE]), sb("iota", [P, NE]), sb("ebase", [P, NE])
        eps = sb("eps_x", [P, 1])
        tok = sb("tok", [P, TOPK, 2], U32)
        x, y = sb("x_x", [P, D]), sb("y_x", [P, D])
        sq, h, hT = sb("sq_x", [P, D]), sb("h_x", [P, D]), sb("hT_x", [P, KD, P])
        x1, x2, x3 = sb("x1", [P, D]), sb("x2", [P, D]), sb("x3", [P, D])
        st = sb("st_x", [P, 4])
        q, sq4 = sb("q_x", [P, MH, MHD]), sb("sq4", [P, MH])
        qT = sb("qT_x", [P, 2, P])
        pr, pT = sb("pr_x", [P, MH, N_MEM]), sb("pT_x", [P, 2 * MH, P])
        mx, rs = sb("mx_x", [P, MH]), sb("rs_x", [P, MH])
        o, oT = sb("o_x", [P, MH, MHD]), sb("oT_x", [P, 2, P])
        lg, m8, i8, i8f = sb("lg", [P, NE]), sb("m8", [P, 8]), sb("i8", [P, 8], U32), sb("i8f", [P, 8])
        g4, gs, hot, tmp = sb("g4", [P, TOPK]), sb("gs", [P, 2]), sb("hot", [P, TOPK, NE]), sb("tmp", [P, TOPK, NE])
        mask, gm, gmT, where = sb("mask", [P, NE]), sb("gm", [P, NE]), sb("gmT", [NE, P]), sb("where", [P, NE])
        slf, slot = sb("slf", [P, TOPK]), sb("slot", [P, TOPK], U32)
        s_w, s_in, s_tok, s_dv, s_ak, s_sd, s_st = (sem("x_" + n) for n in ("weights", "in", "tok", "dve", "act", "scatter_done", "stored"))
        s_sc = e.dma_sem("x_scattered")
        names = ("ssy yn yT yTd o1 x1 ss1 h2 h2T h2Td q qn qT qTd s mx p pT pTc O on oT oTd mo x2 ss2 h3 h3T h3Td lg gx g4 "
                 "msk rk gmT slot bd x3").split()
        m = {n: sem("x_m_" + n) for n in names + ["s0", "qd"]}

        N_W = 18
        DV, AK = 24, 4
        with nc.Block() as block:
            @block.sync
            def _(sp):
                n = 0
                for dst, src in ((ident[:, :], e.c_ident), (before[:, :], e.c_before), (ones[:, :], e.c_ones),
                                 (w_out[:, :, :], e.w_out[0].rearrange("(k p) n -> p k n", p=P)),
                                 (w_mq[:, :, :], e.w_mq[0].rearrange("(k p) n -> p k n", p=P)),
                                 (w_mo[:, :, :], e.w_mo[0].rearrange("(k p) n -> p k n", p=P)),
                                 (rw[:, :, :], e.router_w[0].rearrange("(k p) n -> p k n", p=P)), (bdown[:, :], e.b_down[0]),
                                 (g_e[:, :], e.g_moe_norm[0].partition_broadcast(P)), (g_q[:, :], e.g_mq[0].partition_broadcast(P)),
                                 (rb[:, :], e.router_b[0].partition_broadcast(P)), (iota[:, :], e.c_iota.partition_broadcast(P)),
                                 (ebase[:, :], e.c_ebase.partition_broadcast(P))):
                    sp.dma_start(dst, src).then_inc(s_w, 16)
                    n += 1
                with nc.allow_non_contiguous_dma("gain columns, once"):
                    for dst, src in ((g_o[:, 0:4], e.g_out_mla[0].rearrange("(k p) -> p k", p=P)),
                                     (g_o[:, 4:8], e.g_out_nsa[0].rearrange("(k p) -> p k", p=P)),
                                     (g_m[:, :], e.g_mem_norm[0].rearrange("(k p) -> p k", p=P))):
                        sp.dma_start(dst, src).then_inc(s_w, 16)
                        n += 1
                assert n == N_W - 2
                with sp.Fori(0, NT) as t:
                    rows = bass.ds(t * P, P)
                    sp.wait_ge(m["x1"], CREDIT + t)
                    sp.dma_start(y[:, :], e.d_y[rows, :]).then_inc(s_in, 16)
                    sp.dma_start(x[:, :], e.x[0, rows, :]).then_inc(s_in, 16)
                    sp.wait_ge(s_sd, CREDIT + t)
                    hold(sp, e.sp_passed)
                    sp.dma_start(tok[:, :, :], e.c_tok[rows, :, :]).then_inc(s_tok, 16)
                    sp.wait_ge(m["h3"], CREDIT + t + 1)
                    sp.dma_start(e.d_h3[rows, :], h[:, :]).then_inc(s_st, 16)
                    sp.wait_ge(m["slot"], CREDIT + t + 1)
                    hold(sp, e.sp_passed)
                    sp.dma_start(e.d_gate[rows, :], g4[:, :]).then_inc(s_st, 16)
                    sp.wait_ge(m["x3"], CREDIT + t + 1)
                    sp.dma_start(e.d_x3[rows, :], x3[:, :]).then_inc(s_st, 16)
                sp.wait_ge(s_st, CREDIT + 48 * NT)

            @block.gpsimd
            def _(pool):
                give_credit(pool, e.sems)
                pool.memset(e.cnt[:, :], 0.0).then_inc(s_w, 16)
                pool.memset(eps[:, :], EPS).then_inc(s_w, 16)
                with pool.Fori(0, NT) as t:
                    pool.wait_ge(m["slot"], CREDIT + t + 1)
                    hold(pool, e.pool_passed)
                    pool.wait_ge(s_tok, CREDIT + 16 * t + 16)
                    hold(pool, e.pool_passed)
                    for k in range(TOPK):
                        pool.indirect_dma_start(out=e.d_tok, out_offset=bass.IndirectOffsetOnAxis(ap=slot[:, k:k + 1], axis=0),
                                                in_=tok[:, k, :], in_offset=None).then_inc(s_sc, 16)
                    pool.wait_ge(s_sc, 64 * t + 64)
                    pool.sem_inc(s_sd)

            @block.scalar
            def _(act):
                act.wait_ge(s_w, CREDIT + 16 * N_W)
                with act.Fori(0, NT) as t:
                    ch = Chain(act, s_ak, t, AK)
                    act.wait_ge(s_in, CREDIT + 32 * t + 32)
                    ch(act.activation(sq[:, 0:512], y[:, 0:512], ACT.Square, accum_out=st[:, 0:1]))
                    ch(act.activation(sq[:, 512:], y[:, 512:], ACT.Square, accum_out=st[:, 1:2]))
                    act.activation(st[:, 0:2], st[:, 0:2], ACT.Sqrt, bias=eps[:, 0:1], scale=1.0 / 512).then_inc(m["ssy"], 1)
                    act.wait_ge(m["x1"], CREDIT + t + 1)
                    ch(act.activation(sq[:, :], x1[:, :], ACT.Square, accum_out=st[:, 2:3]))
                    act.activation(st[:, 2:3], st[:, 2:3], ACT.Sqrt, bias=eps[:, 0:1], scale=1.0 / D).then_inc(m["ss1"], 1)
                    act.wait_ge(m["q"], CREDIT + t + 1)
                    act.activation(sq4[:, :], sq4[:, :], ACT.Sqrt, bias=eps[:, 0:1], scale=1.0 / MHD).then_inc(m["qn"], 1)
                    act.wait_ge(m["mx"], CREDIT + t + 1)
                    for j in range(MH):
                        act.activation(pr[:, j, :], ps[:, 4 + j % 2, (j // 2) * N_MEM:(j // 2 + 1) * N_MEM], ACT.Exp, bias=mx[:, j:j + 1],
                                       accum_out=rs[:, j:j + 1]).then_inc(m["p"], 1)
                    act.wait_ge(m["x2"], CREDIT + t + 1)
                    ch(act.activation(sq[:, :], x2[:, :], ACT.Square, accum_out=st[:, 3:4]))
                    act.activation(st[:, 3:4], st[:, 3:4], ACT.Sqrt, bias=eps[:, 0:1], scale=1.0 / D).then_inc(m["ss2"], 1)
                    act.wait_ge(m["gx"], CREDIT + t + 1)
                    act.activation(g4[:, :], m8[:, 0:TOPK], ACT.Exp, bias=gs[:, 0:1], accum_out=gs[:, 1:2]).then_inc(m["g4"], 1)
                    ch.end()

            @block.vector
            def _(dve):
                dve.wait_ge(s_w, CREDIT + 16 * N_W)
                with dve.Fori(0, NT) as t:
                    ch = Chain(dve, s_dv, t, DV)

                    def wait(name, k=1):
                        dve.wait_ge(m[name], CREDIT + k * t + k)

                    def turned(dst, src, gain):
                        d4 = dst.rearrange("p (c n) d -> p c n d", c=2)
                        s4 = src.rearrange("p c (n d) -> p c n d", d=P)
                        if gain is None:
                            return dve.tensor_copy(d4, s4)
                        return dve.tensor_tensor(d4, s4, bcast(gain.rearrange("p (c n) -> p c n", c=2).unsqueeze(3), [P, 2, 4, P]), ALU.mult)

                    wait("ssy")
                    ch(dve.reciprocal(st[:, 0:2], st[:, 0:2]))
                    dve.wait_ge(s_st, CREDIT + 48 * t)
                    dve.tensor_tensor(h[:, :].rearrange("p (c n) -> p c n", c=2), y[:, :].rearrange("p (c n) -> p c n", c=2),
                                      bcast(st[:, 0:2].unsqueeze(2), [P, 2, 512]), ALU.mult).then_inc(m["yn"], 1)
                    wait("yT")
                    turned(hT[:, :, :], ps[:, 0:2, :], g_o[:, :]).then_inc(m["yTd"], 1)
                    wait("o1")
                    dve.tensor_tensor(x1[:, :].rearrange("p (c n) -> p c n", c=2), ps[:, 2:4, :], x[:, :].rearrange("p (c n) -> p c n", c=2), ALU.add).then_inc(m["x1"], 1)
                    wait("ss1")
                    ch(dve.reciprocal(st[:, 2:3], st[:, 2:3]))
                    dve.tensor_scalar(h[:, :], x1[:, :], st[:, 2:3], None, ALU.mult).then_inc(m["h2"], 1)
                    wait("h2T")
                    turned(hT[:, :, :], ps[:, 0:2, :], g_m[:, :]).then_inc(m["h2Td"], 1)
                    wait("s0")
                    q2 = q[:, :, :]
                    ch(dve.tensor_copy(q2, ps[:, 2, 0:256].rearrange("p (h d) -> p h d", d=MHD)))
                    s2 = h[:, 0:256].rearrange("p (h d) -> p h d", d=MHD)
                    ch(dve.tensor_tensor(s2, q2, q2, ALU.mult))
                    dve.tensor_reduce(sq4[:, :], s2, AX.X, ALU.add).then_inc(m["q"], 1)
                    wait("qn")
                    ch(dve.reciprocal(sq4[:, :], sq4[:, :]))
                    ch(dve.tensor_scalar(sq4[:, :], sq4[:, :], MHD ** -0.5, None, ALU.mult))
                    ch(dve.tensor_tensor(q2, q2, bcast(sq4[:, :].unsqueeze(2), [P, MH, MHD]), ALU.mult))
                    dve.tensor_tensor(q2, q2, bcast(g_q[:, :].unsqueeze(1), [P, MH, MHD]), ALU.mult).then_inc(m["qd"], 1)
                    wait("qT")
                    dve.tensor_copy(qT[:, :, :], ps[:, 3, 0:256].rearrange("p (j n) -> p j n", n=P)).then_inc(m["qTd"], 1)
                    wait("s")
                    ch(dve.tensor_reduce(mx[:, :].rearrange("p (j c) -> p c j", c=2), ps[:, 4:6, :].rearrange("p c (j n) -> p c j n", n=N_MEM), AX.X, ALU.max))
                    dve.tensor_scalar(mx[:, :], mx[:, :], -1.0, None, ALU.mult).then_inc(m["mx"], 1)
                    wait("pT")
                    turned(pT[:, :, :], ps[:, 6:8, :], None).then_inc(m["pTc"], 1)
                    ch(dve.reciprocal(rs[:, :], rs[:, :]))
                    wait("O")
                    dve.tensor_tensor(o[:, :, :], ps[:, 0, 0:256].rearrange("p (h d) -> p h d", d=MHD), bcast(rs[:, :].unsqueeze(2), [P, MH, MHD]), ALU.mult).then_inc(m["on"], 1)
                    wait("oT")
                    dve.tensor_copy(oT[:, :, :], ps[:, 1, 0:256].rearrange("p (j n) -> p j n", n=P)).then_inc(m["oTd"], 1)
                    wait("mo")
                    dve.tensor_tensor(x2[:, :].rearrange("p (c n) -> p c n", c=2), ps[:, 2:4, :], x1[:, :].rearrange("p (c n) -> p c n", c=2), ALU.add).then_inc(m["x2"], 1)
                    wait("ss2")
                    ch(dve.reciprocal(st[:, 3:4], st[:, 3:4]))
                    dve.scalar_tensor_tensor(h[:, :], x2[:, :], st[:, 3:4], g_e[:, :], ALU.mult, ALU.mult).then_inc(m["h3"], 1)
                    wait("h3T")
                    turned(hT[:, :, :], ps[:, 0:2, :], None).then_inc(m["h3Td"], 1)
                    wait("lg")
                    ch(dve.tensor_tensor(lg[:, :], ps[:, 2, 0:NE], rb[:, :], ALU.add))
                    hold(dve, e.dve_passed)
                    ch(dve.max(m8[:, :], lg[:, :]))
                    hold(dve, e.dve_passed)
                    ch(dve.max_index(i8[:, :], m8[:, :], lg[:, :]))
                    dve.tensor_scalar(gs[:, 0:1], m8[:, 0:1], -1.0, None, ALU.mult).then_inc(m["gx"], 1)
                    ch(dve.tensor_copy(i8f[:, :], i8[:, :]))
                    ch(dve.tensor_tensor(hot[:, :, :], bcast(iota[:, :].unsqueeze(1), [P, TOPK, NE]), bcast(i8f[:, 0:TOPK].unsqueeze(2), [P, TOPK, NE]), ALU.is_equal))
                    ch(dve.tensor_reduce(mask[:, :], hot[:, :, :].rearrange("p k e -> p e k"), AX.X, ALU.add))
                    wait("g4")
                    ch(dve.reciprocal(gs[:, 1:2], gs[:, 1:2]))
                    ch(dve.tensor_scalar(g4[:, :], g4[:, :], gs[:, 1:2], None, ALU.mult))
                    ch(dve.tensor_tensor(tmp[:, :, :], hot[:, :, :], bcast(g4[:, :].unsqueeze(2), [P, TOPK, NE]), ALU.mult))
                    dve.tensor_reduce(gm[:, :], tmp[:, :, :].rearrange("p k e -> p e k"), AX.X, ALU.add).then_inc(m["msk"], 1)
                    wait("rk")
                    ch(dve.tensor_tensor(where[:, :], ps[:, 3, 0:NE], e.cnt[:, :], ALU.add))
                    ch(dve.tensor_tensor(where[:, :], where[:, :], ebase[:, :], ALU.add))
                    dve.tensor_copy(gmT[:, :], ps[0:NE, 4, 0:P]).then_inc(m["gmT"], 1)
                    ch(dve.tensor_tensor(tmp[:, :, :], hot[:, :, :], bcast(where[:, :].unsqueeze(1), [P, TOPK, NE]), ALU.mult))
                    ch(dve.tensor_reduce(slf[:, :], tmp[:, :, :], AX.X, ALU.add))
                    dve.wait_ge(s_sd, CREDIT + t)
                    dve.tensor_copy(slot[:, :], slf[:, :]).then_inc(m["slot"], 1)
                    ch(dve.tensor_tensor(e.cnt[:, :], e.cnt[:, :], ps[:, 3, NE:2 * NE], ALU.add))
                    wait("bd")
                    dve.tensor_tensor(x3[:, :].rearrange("p (c n) -> p c n", c=2), ps[:, 0:2, :], x2[:, :].rearrange("p (c n) -> p c n", c=2), ALU.add).then_inc(m["x3"], 1)
                    ch.end()

            @block.tensor
            def _(pe):
                pe.wait_ge(s_w, CREDIT + 16 * N_W)
                with pe.Fori(0, NT) as t:
                    def wait(name, k=1):
                        pe.wait_ge(m[name], CREDIT + k * t + k)

                    def turn(src, bank):
                        for k in range(KD):
                            mm = pe.transpose(ps[:, bank + k // 4, (k % 4) * P:(k % 4 + 1) * P], src[:, k * P:(k + 1) * P], ident[:, :])
                        return mm

                    def project(w, cols, bank, n=KD, src=hT):
                        for c in range(0, cols, 512):
                            for k in range(n):
                                mm = pe.matmul(ps[:, bank + c // 512, 0:min(512, cols - c)], src[:, k, :], w[:, k, c:min(cols, c + 512)], start=(k == 0), stop=(k == n - 1))
                        return mm

                    wait("yn")
                    pe.wait_ge(m["x3"], CREDIT + t)
                    turn(h, 0).then_inc(m["yT"], 1)
                    wait("yTd")
                    project(w_out, D, 2).then_inc(m["o1"], 1)
                    wait("h2")
                    turn(h, 0).then_inc(m["h2T"], 1)
                    wait("h2Td")
                    wait("x1")
                    project(w_mq, MH * MHD, 2).then_inc(m["s0"], 1)
                    wait("qd")
                    for j in range(2):
                        mm = pe.transpose(ps[:, 3, j * P:(j + 1) * P], q[:, 2 * j:2 * j + 2, :].rearrange("p h d -> p (h d)"), ident[:, :])
                    mm.then_inc(m["qT"], 1)
                    wait("qTd")
                    hold(pe, e.pe_passed)
                    for j in range(MH):
                        r = slice(MHD * (j % 2), MHD * (j % 2 + 1))
                        mm = pe.matmul(ps[:, 4 + j % 2, (j // 2) * N_MEM:(j // 2 + 1) * N_MEM], qT[r, j // 2, :], e.kTm[r, j // 2, :], start=True, stop=True)
                    mm.then_inc(m["s"], 1)
                    wait("p", MH)
                    for j in range(2 * MH):
                        mm = pe.transpose(ps[:, 6 + j // 4, (j % 4) * P:(j % 4 + 1) * P], pr[:, j // 2, (j % 2) * P:(j % 2 + 1) * P], ident[:, :])
                    mm.then_inc(m["pT"], 1)
                    wait("pTc")
                    for j in range(2 * MH):
                        mm = pe.matmul(ps[:, 0, (j // 2) * MHD:(j // 2 + 1) * MHD], pT[:, j, :], e.vmem[:, j % 2, j // 2, :], start=(j % 2 == 0), stop=(j % 2 == 1))
                    mm.then_inc(m["O"], 1)
                    wait("on")
                    for j in range(2):
                        mm = pe.transpose(ps[:, 1, j * P:(j + 1) * P], o[:, 2 * j:2 * j + 2, :].rearrange("p h d -> p (h d)"), ident[:, :])
                    mm.then_inc(m["oT"], 1)
                    wait("oTd")
                    project(w_mo, D, 2, n=2, src=oT).then_inc(m["mo"], 1)
                    wait("h3")
                    turn(h, 0).then_inc(m["h3T"], 1)
                    wait("h3Td")
                    project(rw, NE, 2).then_inc(m["lg"], 1)
                    wait("msk")
                    pe.matmul(ps[:, 3, 0:NE], before[:, :], mask[:, :], start=True, stop=True)
                    pe.matmul(ps[:, 3, NE:2 * NE], ones[:, :], mask[:, :], start=True, stop=True)
                    pe.transpose(ps[0:NE, 4, 0:P], gm[:, :], ident[:, :]).then_inc(m["rk"], 1)
                    wait("gmT")
                    for c in range(2):
                        mm = pe.matmul(ps[:, c, :], gmT[:, :], bdown[:, c * 512:(c + 1) * 512], start=True, stop=True)
                    mm.then_inc(m["bd"], 1)


def stage_plan(nc, e):
    with ExitStack() as ctx:
        sb, sem, ps = add_tools(nc, e, ctx)
        iota, pidx, ones = sb("iota_p", [P, NE]), sb("pidx", [P, 1]), sb("ones_p", [P, NE])
        a, npas, ends, done, eq = (sb(n, [P, NE]) for n in ("a", "npas", "ends", "donep", "eq"))
        r = sb("r", [P, 8])
        plan = sb("plan_f", [P, 4], I32)
        s_in, s_dv, s_out = sem("p_in"), sem("p_dve"), sem("p_out")
        with nc.Block() as block:
            @block.gpsimd
            def _(pool):
                give_credit(pool, e.sems)

            @block.sync
            def _(sp):
                sp.dma_start(iota[:, :], e.c_iota.partition_broadcast(P)).then_inc(s_in, 16)
                sp.dma_start(pidx[:, :], e.c_pidx).then_inc(s_in, 16)
                sp.wait_ge(s_dv, CREDIT + 25)
                sp.dma_start(e.d_plan.rearrange("(p n) -> p n", n=4), plan[:, :]).then_inc(s_out, 16)
                sp.wait_ge(s_out, CREDIT + 16)
                sp.dma_start(e.plan[:, :], e.d_plan.rearrange("(o n) -> o n", o=1)).then_inc(s_out, 16)
                sp.wait_ge(s_out, CREDIT + 32)

            @block.vector
            def _(dve):
                n = [0]

                def step(ins):
                    ins.then_inc(s_dv, 1)
                    n[0] += 1
                    dve.wait_ge(s_dv, CREDIT + n[0])

                cnt = e.cnt
                dve.wait_ge(s_in, CREDIT + 32)
                step(dve.memset(ones[:, :], 1.0))
                step(dve.memset(r[:, :], 0.0))
                step(dve.tensor_scalar(npas[:, :], cnt[:, :], 0.0, None, ALU.is_gt))
                for k in range(1, CAP // PASS):
                    step(dve.tensor_scalar(a[:, :], cnt[:, :], float(k * PASS), None, ALU.is_gt))
                    step(dve.tensor_tensor(npas[:, :], npas[:, :], a[:, :], ALU.add))
                step(dve.tensor_tensor_scan(ends[:, :], ones[:, :], npas[:, :], 0.0, ALU.mult, ALU.add))
                step(dve.tensor_scalar(done[:, :], ends[:, :], pidx[:, 0:1], None, ALU.is_le))
                step(dve.tensor_reduce(r[:, 0:1], done[:, :], AX.X, ALU.add))
                step(dve.tensor_tensor(a[:, :], done[:, :], npas[:, :], ALU.mult))
                step(dve.tensor_reduce(r[:, 1:2], a[:, :], AX.X, ALU.add))
                step(dve.tensor_tensor(r[:, 2:3], pidx[:, :], r[:, 1:2], ALU.subtract))
                step(dve.tensor_scalar(r[:, 2:3], r[:, 2:3], float(PASS), None, ALU.mult))
                step(dve.tensor_scalar(eq[:, :], iota[:, :], r[:, 0:1], None, ALU.is_equal))
                step(dve.tensor_tensor(a[:, :], eq[:, :], cnt[:, :], ALU.mult))
                step(dve.tensor_reduce(r[:, 3:4], a[:, :], AX.X, ALU.add))
                step(dve.tensor_tensor(r[:, 6:7], r[:, 3:4], r[:, 2:3], ALU.subtract))
                step(dve.tensor_scalar(r[:, 6:7], r[:, 6:7], 0.0, None, ALU.max))
                step(dve.tensor_scalar(r[:, 4:5], r[:, 0:1], float(NE - 1), None, ALU.min))
                step(dve.scalar_tensor_tensor(r[:, 5:6], r[:, 4:5], float(CAP), r[:, 2:3], ALU.mult, ALU.add))
                step(dve.tensor_scalar(r[:, 5:6], r[:, 5:6], float(NE * CAP - PASS), None, ALU.min))
                step(dve.tensor_copy(plan[:, :], r[:, 4:8]))


def stage_experts(nc, e):
    with ExitStack() as ctx:
        sb, sem, ps = add_tools(nc, e, ctx)
        NCH = 4
        JD = FF // P
        ident = sb("ident_e", [P, P])
        wg = sb("wg", [P, NCH, KD, 512])
        wd = sb("wd", [P, NCH, 2, D])
        src, dst = sb("src", [P, 2, 2], U32), sb("dst", [P, 2, 2], U32)
        xg, xT = sb("xg", [P, 2, D]), sb("xT_e", [P, KD, PASS])
        bias = sb("bias", [P, 16])
        gg, ss, uu = (sb(n, [P, 2, PASS]) for n in ("gg", "ss", "uu"))
        aT = sb("aT", [P, JD, PASS])
        ys = sb("ys_e", [P, 2, D])
        s_id, s_src, s_dst, s_xT, s_xTc, s_xset = (sem("e_" + n) for n in
            ("ident", "source_rows", "target_rows", "rowsT", "rowsT_copied", "rows_set"))
        s_x, s_st = e.dma_sem("e_rows"), e.dma_sem("e_stored")
        s_wg = [sem(f"e_wg{c}") for c in range(NCH)]
        s_wd = [sem(f"e_wd{c}") for c in range(NCH)]
        s_gu, s_g, s_sig, s_a, s_down, s_y, s_sd, s_dch = (sem("e_" + n) for n in
            ("gate_up", "gate", "sigmoid", "act", "down", "y", "scatter_done", "dve_chain"))

        def rows_left(eng, i):
            return eng.value_load(e.plan[0:1, bass.ds(4 * i + 2, 1)], min_val=0, max_val=CAP)

        def expert(eng, i):
            return eng.value_load(e.plan[0:1, bass.ds(4 * i, 1)], min_val=0, max_val=NE - 1)

        def first_slot(eng, i):
            return eng.value_load(e.plan[0:1, bass.ds(4 * i + 1, 1)], min_val=0, max_val=NE * CAP - PASS)

        def by_size(eng, n, body):
            with eng.If(n > P):
                with eng.If(n > P + P // 2):
                    body(2 * P, 2)
                with eng.Else():
                    body(P + P // 2, 2)
            with eng.Else():
                body(P, 1)

        with nc.Block() as block:
            @block.sync
            def _(sp):
                sp.dma_start(ident[:, :], e.c_ident).then_inc(s_id, 16)
                with sp.Fori(0, NPASS) as i:
                    n = rows_left(sp, i)
                    ex = expert(sp, i)
                    with sp.If(n > 0):
                        one = bass.ds(ex, 1)
                        for c in range(NCH):
                            sp.wait_ge(s_gu, CREDIT + JD * i + 2 * (c + 1) - JD)
                            hold(sp, e.sp_passed)
                            sp.dma_start(wg[:, c, :, :], e.w_gate_up[0][one, :, c * 512:(c + 1) * 512].rearrange("o (k p) n -> p (o k) n", p=P)).then_inc(s_wg[c], 16)
                        for c in range(NCH):
                            sp.wait_ge(s_down, CREDIT + NCH * i + c + 1 - NCH)
                            hold(sp, e.sp_passed)
                            sp.dma_start(wd[:, c, :, :], e.w_down[0][one, c * 256:(c + 1) * 256, :].rearrange("o (k p) n -> p (o k) n", p=P)).then_inc(s_wd[c], 16)

            @block.gpsimd
            def _(pool):
                give_credit(pool, e.sems)

                def gather(i):
                    pool.wait_ge(s_src, CREDIT + 16 * i + 16)
                    hold(pool, e.pool_passed)
                    pool.wait_ge(s_xT, CREDIT + 4 * i)
                    hold(pool, e.pool_passed)
                    for b in range(2):
                        pool.indirect_dma_start(out=xg[:, b, :], out_offset=None, in_=e.d_h3, bounds_check=S - 1, oob_is_err=False,
                                                in_offset=bass.IndirectOffsetOnAxis(ap=src[:, b, 0:1], axis=0)).then_inc(s_x, 16)

                pool.memset(xg[:, :, :], 0.0).then_inc(s_xset, 1)
                pool.wait_ge(s_xset, CREDIT + 2)
                gather(0)
                with pool.Fori(0, NPASS) as i:
                    n = rows_left(pool, i)
                    with pool.If(n > 0):
                        gather(i + 1)
                        pool.wait_ge(s_dst, CREDIT + 16 * i + 16)
                        hold(pool, e.pool_passed)

                        def scatter(nb):
                            for b in range(nb):
                                pool.wait_ge(s_y, CREDIT + 2 * i + 1 + b)
                                hold(pool, e.pool_passed)
                                pool.indirect_dma_start(out=e.d_ys, out_offset=bass.IndirectOffsetOnAxis(ap=dst[:, b, 1:2], axis=0),
                                                        in_=ys[:, b, :], in_offset=None, bounds_check=S * TOPK - 1, oob_is_err=False).then_inc(s_st, 16)
                        scatter(2)
                        pool.wait_ge(s_st, 32 * i + 32)
                        pool.sem_inc(s_sd)

            @block.scalar
            def _(act):
                def sources(i, slot):
                    act.dma_start(src[:, :, :], e.d_tok[bass.ds(slot, PASS), :].rearrange("(b p) o -> p b o", p=P)).then_inc(s_src, 16)

                def copy_rows(i):
                    for k in range(4):
                        act.wait_ge(s_xT, CREDIT + 4 * i + k + 1)
                        act.wait_ge(s_gu, CREDIT + JD * i)
                        act.activation(xT[:, 2 * k:2 * k + 2, :], ps[:, 6 + k % 2, :].rearrange("p (k n) -> p k n", k=2), ACT.Copy).then_inc(s_xTc, 1)

                with nc.allow_non_contiguous_dma("row numbers"):
                    sources(0, first_slot(act, 0))
                    copy_rows(0)
                    with act.Fori(0, NPASS) as i:
                        n = rows_left(act, i)
                        with act.If(n > 0):
                            act.wait_ge(s_x, 32 * i + 32)
                            hold(act, e.act_passed)
                            sources(i + 1, first_slot(act, i + 1))
                            act.wait_ge(s_sd, CREDIT + i)
                            hold(act, e.act_passed)
                            slot = first_slot(act, i)
                            act.dma_start(dst[:, :, :], e.d_tok[bass.ds(slot, PASS), :].rearrange("(b p) o -> p b o", p=P)).then_inc(s_dst, 16)

                            def sigmoids(w, nb):
                                for j in range(JD):
                                    act.wait_ge(s_g, CREDIT + JD * i + j + 1)
                                    act.activation(ss[:, j % 2, 0:w], gg[:, j % 2, 0:w], ACT.Sigmoid, scale=ALPHA).then_inc(s_sig, 1)
                            by_size(act, n, sigmoids)
                            copy_rows(i + 1)

            @block.vector
            def _(dve):
                dve.memset(aT[:, :, :], 0.0).then_inc(s_xset, 1)
                dve.wait_ge(s_xset, CREDIT + 2)
                with dve.Fori(0, NPASS) as i:
                    n = rows_left(dve, i)
                    ex = expert(dve, i)
                    with dve.If(n > 0):
                        dve.wait_ge(s_a, CREDIT + JD * i)
                        hold(dve, e.dve_passed)
                        Chain(dve, s_dch, i, 1 + 3 * JD)(dve.tensor_copy(bias[:, :], e.bgT[:, :, bass.ds(ex, 1)].rearrange("p j o -> p (j o)")))
                        hold(dve, e.dve_passed)

                        def body(w, nb):
                            ch = Chain(dve, s_dch, i, 1 + 3 * JD)
                            ch.n = 1
                            for j in range(JD):
                                g, u, s = gg[:, j % 2, 0:w], uu[:, j % 2, 0:w], ss[:, j % 2, 0:w]
                                dve.wait_ge(s_gu, CREDIT + JD * i + j + 1)
                                dve.tensor_scalar(g, ps[:, j % 2, 0:w], bias[:, j:j + 1], LIMIT, ALU.add, ALU.min).then_inc(s_g, 1)
                                ch(dve.tensor_scalar(u, ps[:, j % 2, PASS:PASS + w], bias[:, 8 + j:9 + j], LIMIT, ALU.add, ALU.min))
                                ch(dve.tensor_scalar(u, u, -LIMIT, 1.0, ALU.max, ALU.add))
                                ch(dve.tensor_tensor(u, u, g, ALU.mult))
                                dve.wait_ge(s_sig, CREDIT + JD * i + j + 1)
                                if j == 0:
                                    dve.wait_ge(s_down, CREDIT + NCH * i)
                                dve.tensor_tensor(aT[:, j, 0:w], u, s, ALU.mult).then_inc(s_a, 1)
                            ch.end()
                            dve.wait_ge(s_sd, CREDIT + i)
                            for b in range(2):
                                if b < nb:
                                    dve.wait_ge(s_down, CREDIT + NCH * i + NCH)
                                    dve.tensor_copy(ys[:, b, :].rearrange("p (c n) -> p c n", c=2), ps[:, 2 + 2 * b:4 + 2 * b, :]).then_inc(s_y, 1)
                                else:
                                    dve.memset(ys[:, b, :], 0.0).then_inc(s_y, 1)
                        by_size(dve, n, body)

            @block.tensor
            def _(pe):
                def turn_rows(i):
                    pe.wait_ge(s_x, 32 * i + 32)
                    for k in range(4):
                        pe.wait_ge(s_xTc, CREDIT + 4 * i + max(k - 1, 0))
                        for kk in range(2):
                            for b in range(2):
                                c = 2 * k + kk
                                mm = pe.transpose(ps[:, 6 + k % 2, kk * PASS + b * P:kk * PASS + (b + 1) * P], xg[:, b, c * P:(c + 1) * P], ident[:, :])
                        mm.then_inc(s_xT, 1)

                pe.wait_ge(s_id, CREDIT + 16)
                turn_rows(0)
                with pe.Fori(0, NPASS) as i:
                    n = rows_left(pe, i)
                    with pe.If(n > 0):
                        def body(w, nb):
                            pe.wait_ge(s_xTc, CREDIT + 4 * i + 4)
                            for j in range(JD):
                                if j % 2 == 0:
                                    pe.wait_ge(s_wg[j // 2], CREDIT + 16 * i + 16)
                                pe.wait_ge(s_a, CREDIT + JD * i + j - 1)
                                for half in range(2):
                                    c0 = 256 * (j % 2) + half
                                    for k in range(KD):
                                        mm = pe.matmul(ps[:, j % 2, half * PASS:half * PASS + w], wg[:, j // 2, k, c0:c0 + 255:2], xT[:, k, 0:w],
                                                       start=(k == 0), stop=(k == KD - 1))
                                mm.then_inc(s_gu, 1)
                            turn_rows(i + 1)
                            pe.wait_ge(s_a, CREDIT + JD * i + JD)
                            pe.wait_ge(s_y, CREDIT + 2 * i)
                            for c in range(NCH):
                                pe.wait_ge(s_wd[c], CREDIT + 16 * i + 16)
                                for b in range(nb):
                                    for h in range(2):
                                        for j in (2 * c, 2 * c + 1):
                                            mm = pe.matmul(ps[:, 2 + 2 * b + h, :], aT[:, j, b * P:(b + 1) * P], wd[:, c, j % 2, h * 512:(h + 1) * 512],
                                                           start=(j == 0), stop=(j == JD - 1))
                                mm.then_inc(s_down, 1)
                        by_size(pe, n, body)


def stage_combine(nc, e):
    with ExitStack() as ctx:
        sb, sem, ps = add_tools(nc, e, ctx)
        x3 = sb("x3_f", [P, 2, D])
        gate = sb("gate_f", [P, 2, TOPK])
        yr = sb("yr", [P, 2, TOPK, D])
        s_in, s_dv, s_out = ([sem(f"f_{n}{b}") for b in range(2)] for n in ("in", "sum", "stored"))
        with nc.Block() as block:
            @block.gpsimd
            def _(pool):
                give_credit(pool, e.sems)

            @block.sync
            def _(sp):
                with sp.Fori(0, NT // 2) as t:
                    for b in range(2):
                        rows = bass.ds((2 * t + b) * P, P)
                        sp.wait_ge(s_out[b], CREDIT + 16 * t)
                        sp.dma_start(yr[:, b, :, :], e.d_ys[bass.ds((2 * t + b) * P * TOPK, P * TOPK), :].rearrange("(p k) n -> p k n", k=TOPK)).then_inc(s_in[b], 16)
                        sp.dma_start(gate[:, b, :], e.d_gate[rows, :]).then_inc(s_in[b], 16)
                        sp.dma_start(x3[:, b, :], e.d_x3[rows, :]).then_inc(s_in[b], 16)

            @block.scalar
            def _(act):
                with act.Fori(0, NT // 2) as t:
                    for b in range(2):
                        act.wait_ge(s_dv[b], CREDIT + TOPK * t + TOPK)
                        act.dma_start(e.out[0, bass.ds((2 * t + b) * P, P), :], x3[:, b, :]).then_inc(s_out[b], 16)
                for b in range(2):
                    act.wait_ge(s_out[b], CREDIT + 16 * (NT // 2))

            @block.vector
            def _(dve):
                with dve.Fori(0, NT // 2) as t:
                    for b in range(2):
                        dve.wait_ge(s_in[b], CREDIT + 48 * t + 48)
                        for k in range(TOPK):
                            if k:
                                dve.wait_ge(s_dv[b], CREDIT + TOPK * t + k)
                            dve.scalar_tensor_tensor(x3[:, b, :], yr[:, b, k, :], gate[:, b, k:k + 1], x3[:, b, :], ALU.mult, ALU.add).then_inc(s_dv[b], 1)


def program(nc, e):
    with ExitStack() as ctx:
        keep = lambda n, s, d=F32: ctx.enter_context(nc.sbuf_tensor(n, s, d))
        e.bgT = keep("bgT", [P, 16, NE])
        e.kTm = keep("kTm", [P, 2, N_MEM])
        e.vmem = keep("vmem", [P, N_MEM // P, MH, MHD])
        e.cnt = keep("cnt", [P, NE])
        e.plan = keep("plan", [1, 4 * P], I32)
        e.pe_passed = e.act_passed = e.dve_passed = e.pool_passed = e.sp_passed = ctx.enter_context(nc.semaphore("passed"))
        d = lambda n, s, t=F32: nc.dram_tensor(n, s, t, kind="Internal").ap()
        e.d_rev = d("d_rev", [2, HN + 1, REV])
        e.d_strip, e.d_wstrip = d("d_strip", [HN + 1, P, S]), d("d_wstrip", [HN + 1, P, WIN + P])
        e.d_qm, e.d_km, e.d_vm = d("d_qm", [HM, QK, S]), d("d_km", [HM, QK, S]), d("d_vm", [HM, S, VD])
        e.d_qn_flat = d("d_qn", [HN, HD, S])
        e.d_qn = [e.d_qn_flat[p::2] for p in range(2)]
        e.d_kn, e.d_cn = d("d_kn", [2, G * HD, S]), d("d_cn", [2, G * HD, S])
        e.d_vn = [d("d_vs", [G, S, HD]), d("d_vw", [G, S, HD])]
        e.d_gt = d("d_gt", [HN, S, 3])
        e.d_ck, e.d_cv = d("d_ck", [G, HD, NCMP]), d("d_cv", [G, NCMP, HD])
        e.d_y, e.d_h3, e.d_x3 = d("d_y", [S, D]), d("d_h3", [S, D]), d("d_x3", [S, D])
        e.d_gate = d("d_gate", [S, TOPK])
        e.d_tok, e.d_ys, e.d_plan = d("d_tok", [NE * CAP, 2], U32), d("d_ys", [S * TOPK, D]), d("d_plan", [4 * P], I32)
        e.skew_view = lambda k, h: bass.AP(e.d_rev.tensor, h * REV + k * (HN + 1) * REV, [[1, P], [1, S]])
        stage_setup(nc, e)
        stage_memory(nc, e)
        stage_project(nc, e)
        stage_compress(nc, e)
        stage_attend(nc, e)
        stage_mix(nc, e)
        stage_plan(nc, e)
        stage_experts(nc, e)
        stage_combine(nc, e)


def shape_constants():
    dist = (S - 1) - np.arange(REV)
    n = np.maximum(dist, 0)
    nf = np.maximum(n, 1).astype(np.float32)
    large = MAX_EXACT + (np.log(nf / MAX_EXACT) / np.log(MAX_DIST / MAX_EXACT) * (BUCKETS - MAX_EXACT)).astype(np.int32)
    bucket = np.where(n < MAX_EXACT, n, np.minimum(large, BUCKETS - 1))
    neg = np.where(dist < 0, NEG, 0.0).astype(np.float32)
    negw = np.where((dist < 0) | (dist >= WIN), NEG, 0.0).astype(np.float32)
    half = ROPE // 2
    inv = (np.float32(10000.0) ** (-np.arange(half, dtype=np.float32) / half)).astype(np.float32)
    ang = np.arange(S, dtype=np.float32)[:, None] * inv
    f = lambda a: np.ascontiguousarray(a, dtype=np.float32)
    return {
        "c_onehot": f(bucket[None, :] == np.arange(BUCKETS)[:, None]),
        "c_negrow": f(np.tile(neg, (HN + 1, 1))),
        "c_negwin": f(np.tile(negw, (HN + 1, 1))),
        "c_flip": f(np.eye(P)[::-1]),
        "c_ident": f(np.eye(P)),
        "c_before": f(np.triu(np.ones((P, P)), 1)),
        "c_ones": f(np.ones((P, P))),
        "c_trig": f(np.concatenate([np.cos(ang), np.sin(ang)], axis=1)),
        "c_inv_d": f([1 / QR, 1 / KVR] + [1 / HD] * 12),
        "c_post": f([1.0, 1.0] + [HD ** -0.5] * 8 + [1.0] * 4),
        "c_post2": f([QK ** -0.5] * HM + [1.0] * HM),
        "c_cvalid": f((np.arange(P) >= CMP_LEN - 1)[:, None]),
        "c_iota": f(np.arange(NE)),
        "c_ebase": f(np.arange(NE) * CAP),
        "c_pidx": f(np.arange(P)[:, None]),
        "c_tok": np.stack([np.repeat(np.arange(S), TOPK), np.arange(S * TOPK)], 1).reshape(S, TOPK, 2).astype(np.uint32),
    }


def kernel(**inputs):
    import concourse.bacc as bacc
    from concourse.bass_utils import run_bass_kernel_spmd as run

    nc = bacc.Bacc("TRN2", target_bir_lowering=False, num_devices=1)
    arrays = {name: np.ascontiguousarray(a) for name, a in inputs.items()}
    arrays.update(shape_constants())
    dram = {name: nc.dram_tensor("in_" + name, a.shape, mybir.dt.from_np(a.dtype), kind="ExternalInput").ap()
            for name, a in arrays.items()}
    e = Env()
    e.x, e.mem, e.g_attn_norm, e.w_in, e.g_cq, e.w_uq = (dram[n] for n in 'x mem g_attn_norm w_in g_cq w_uq'.split())
    e.g_ckv, e.w_ukv, e.g_q_mla, e.g_k_mla, e.cmp_k_pos, e.cmp_k_w1 = (dram[n] for n in 'g_ckv w_ukv g_q_mla g_k_mla cmp_k_pos cmp_k_w1'.split())
    e.cmp_k_w2, e.cmp_v_pos, e.cmp_v_w1, e.cmp_v_w2, e.g_q_nsa, e.g_k_nsa = (dram[n] for n in 'cmp_k_w2 cmp_v_pos cmp_v_w1 cmp_v_w2 g_q_nsa g_k_nsa'.split())
    e.rel_table, e.g_out_mla, e.g_out_nsa, e.w_out, e.g_mem_norm, e.g_mem_src = (dram[n] for n in 'rel_table g_out_mla g_out_nsa w_out g_mem_norm g_mem_src'.split())
    e.w_mq, e.w_mkv, e.g_mq, e.g_mk, e.w_mo, e.g_moe_norm = (dram[n] for n in 'w_mq w_mkv g_mq g_mk w_mo g_moe_norm'.split())
    e.router_w, e.router_b, e.w_gate_up, e.b_gate_up, e.w_down, e.b_down = (dram[n] for n in 'router_w router_b w_gate_up b_gate_up w_down b_down'.split())
    e.c_onehot, e.c_negrow, e.c_negwin, e.c_flip, e.c_ident, e.c_before = (dram[n] for n in 'c_onehot c_negrow c_negwin c_flip c_ident c_before'.split())
    e.c_ones, e.c_trig, e.c_inv_d, e.c_post, e.c_post2, e.c_cvalid = (dram[n] for n in 'c_ones c_trig c_inv_d c_post c_post2 c_cvalid'.split())
    e.c_iota, e.c_ebase, e.c_pidx, e.c_tok = (dram[n] for n in 'c_iota c_ebase c_pidx c_tok'.split())
    e.out = nc.dram_tensor("out_0", (1, S, D), F32, kind="ExternalOutput").ap()
    program(nc, e)
    r = run(nc, [{"in_" + name: a for name, a in arrays.items()}], core_ids=[0])
    return r.results[0]["out_0"]
```
